# Optimizing a Trainium2 kernel written in Bass

```python
import math
import jax
import jax.numpy as jnp
from jax import lax
import numpy as np

D_MODEL = 1024
BATCH = 1
SEQ = 1024
DEPTH = 2

S5_WIDTH = D_MODEL // 2
S5_GROUP = 16
S5_GROUPS = S5_WIDTH // S5_GROUP
S5_STATE = 64
ATTN_HEADS = 8
HEAD_DIM = 64
ATTN_WIDTH = ATTN_HEADS * HEAD_DIM
IDX_HEADS = 8
IDX_DIM = 64
TOPK_MAX = 256
Q_BLOCK = 128
ROPE_THETA = 500000.0
ROPE_DIM = HEAD_DIM // 4
MIX_WIDTH = S5_WIDTH + ATTN_WIDTH
IN_SPLITS = (S5_WIDTH, ATTN_WIDTH, HEAD_DIM, HEAD_DIM, IDX_HEADS * IDX_DIM, IDX_DIM, IDX_HEADS)
IN_WIDTH = sum(IN_SPLITS)
POOL_WINDOWS = (2, 4, 8, 16)
POOL_GROUP = D_MODEL // len(POOL_WINDOWS)
N_EXPERTS = 64
TOP_K = 8
N_EXPERT_GROUPS = 8
TOPK_GROUPS = 4
EXPERT_DIM = 256
SHARED_DIM = 256
ROUTED_SCALE = 2.5
ROW_BLOCK = 128
N_EVEN = (DEPTH + 1) // 2
N_ODD = DEPTH // 2
EPS = 1e-6

kernel_name = 'hybrid_s5_dsa_pool_moe_trunk'

def rms_norm(x, g):
    xf = x.astype(jnp.float32)
    y = xf * lax.rsqrt(jnp.mean(xf * xf, axis=-1, keepdims=True) + EPS)
    return (y * g.astype(jnp.float32)).astype(x.dtype)

def ada_mod(cs, w, b):
    return jnp.split(cs @ w + b, 3, axis=-1)

def modulate(n, shift, scale):
    return n * (1.0 + scale[:, None, :]) + shift[:, None, :]

def rope_tables(positions, rot_dim):
    inv = jnp.power(jnp.float32(ROPE_THETA), -jnp.arange(0, rot_dim, 2, dtype=jnp.float32) / rot_dim)
    ang = positions.astype(jnp.float32)[..., None] * inv
    return jnp.cos(ang)[:, :, None, :], jnp.sin(ang)[:, :, None, :]

def partial_rope(x, cos, sin):
    half = cos.shape[-1]
    xr = x[..., :2 * half].astype(jnp.float32)
    x1, x2 = xr[..., :half], xr[..., half:]
    rot = jnp.concatenate([x1 * cos - x2 * sin, x1 * sin + x2 * cos], axis=-1)
    return jnp.concatenate([rot.astype(x.dtype), x[..., 2 * half:]], axis=-1)

def _ssm_combine(e1, e2):
    a1r, a1i, b1r, b1i = e1
    a2r, a2i, b2r, b2i = e2
    return (a2r * a1r - a2i * a1i, a2r * a1i + a2i * a1r,
            a2r * b1r - a2i * b1i + b2r, a2r * b1i + a2i * b1r + b2i)

def s5_mixer(u, lam_re, lam_im, log_dt, b_re, b_im, c_re, c_im, d_skip, glu_w, glu_b):
    bsz, seq, _ = u.shape
    uf = u.astype(jnp.float32).reshape(bsz, seq, S5_GROUPS, S5_GROUP)
    lr = lam_re.astype(jnp.float32)
    li = lam_im.astype(jnp.float32)
    dt = jnp.exp(log_dt.astype(jnp.float32))[:, None]
    mag = jnp.exp(lr * dt)
    ar, ai = mag * jnp.cos(li * dt), mag * jnp.sin(li * dt)
    nr, ni = ar - 1.0, ai
    den = lr * lr + li * li
    cr, ci = (nr * lr + ni * li) / den, (ni * lr - nr * li) / den
    bre, bim = b_re.astype(jnp.float32), b_im.astype(jnp.float32)
    bbar_r = cr[..., None] * bre - ci[..., None] * bim
    bbar_i = cr[..., None] * bim + ci[..., None] * bre
    bu_r = jnp.einsum('gph,bsgh->bsgp', bbar_r, uf)
    bu_i = jnp.einsum('gph,bsgh->bsgp', bbar_i, uf)
    a_r = jnp.broadcast_to(ar, bu_r.shape)
    a_i = jnp.broadcast_to(ai, bu_i.shape)
    _, _, st_r, st_i = lax.associative_scan(_ssm_combine, (a_r, a_i, bu_r, bu_i), axis=1)
    y = (jnp.einsum('ghp,bsgp->bsgh', c_re.astype(jnp.float32), st_r)
         - jnp.einsum('ghp,bsgp->bsgh', c_im.astype(jnp.float32), st_i)
         + d_skip.astype(jnp.float32) * uf)
    y = jax.nn.gelu(y)
    y = y * jax.nn.sigmoid(jnp.einsum('bsgh,ghk->bsgk', y, glu_w.astype(jnp.float32)) + glu_b.astype(jnp.float32))
    return y.reshape(bsz, seq, S5_WIDTH).astype(u.dtype)

def dsa_mixer(q, k, v, qi, ki, wi, q_norm_g, k_norm_g, positions):
    bsz, seq, _ = q.shape
    cos, sin = rope_tables(positions, ROPE_DIM)
    q = partial_rope(rms_norm(q.reshape(bsz, seq, ATTN_HEADS, HEAD_DIM), q_norm_g), cos, sin)
    k = partial_rope(rms_norm(k, k_norm_g)[:, :, None, :], cos, sin)[:, :, 0]
    qi = partial_rope(qi.reshape(bsz, seq, IDX_HEADS, IDX_DIM), cos, sin).astype(jnp.float32)
    ki = partial_rope(ki[:, :, None, :], cos, sin)[:, :, 0].astype(jnp.float32)
    wi = wi.astype(jnp.float32) * IDX_HEADS ** -0.5
    k_sel = min(TOPK_MAX, seq // 4)
    n_blk = seq // Q_BLOCK
    key_pos = jnp.arange(seq, dtype=jnp.int32)

    def to_blocks(a):
        return jnp.moveaxis(a.reshape(bsz, n_blk, Q_BLOCK, *a.shape[2:]), 1, 0)

    def block(args):
        qb, qib, wb, tb = args
        iscore = jnp.einsum('bqhd,bsd->bqhs', qib, ki) * IDX_DIM ** -0.5
        iscore = jnp.einsum('bqh,bqhs->bqs', wb, jax.nn.relu(iscore))
        iscore = jnp.where(key_pos[None, None, :] <= tb[None, :, None], iscore, -jnp.inf)
        _, sel = lax.top_k(iscore, k_sel)
        valid = sel <= tb[None, :, None]
        kg = jax.vmap(lambda kk, ii: kk[ii])(k, sel)
        vg = jax.vmap(lambda vv, ii: vv[ii])(v, sel)
        sc = jnp.einsum('bqhd,bqkd->bqhk', qb, kg).astype(jnp.float32) * HEAD_DIM ** -0.5
        sc = jnp.where(valid[:, :, None, :], sc, -jnp.inf)
        p = jax.nn.softmax(sc, axis=-1).astype(vg.dtype)
        return jnp.einsum('bqhk,bqkd->bqhd', p, vg)

    q_pos = jnp.arange(seq, dtype=jnp.int32).reshape(n_blk, Q_BLOCK)
    out = lax.map(block, (to_blocks(q), to_blocks(qi), to_blocks(wi), q_pos))
    return jnp.moveaxis(out, 0, 1).reshape(bsz, seq, ATTN_WIDTH)

def hybrid_mixer(h, positions, w_in, w_out, lam_re, lam_im, log_dt, b_re, b_im, c_re, c_im,
                 d_skip, glu_w, glu_b, q_norm_g, k_norm_g):
    proj = h @ w_in
    cuts = np.cumsum(IN_SPLITS)[:-1].tolist()
    u, q, k, v, qi, ki, wi = jnp.split(proj, cuts, axis=-1)
    y_ssm = s5_mixer(u, lam_re, lam_im, log_dt, b_re, b_im, c_re, c_im, d_skip, glu_w, glu_b)
    y_att = dsa_mixer(q, k, v, qi, ki, wi, q_norm_g, k_norm_g, positions)
    return jnp.concatenate([y_ssm, y_att], axis=-1) @ w_out

def pool_mixer(h, pool_w, pool_scale):
    bsz, seq, d = h.shape
    hf = h.astype(jnp.float32)
    cs = jnp.concatenate([jnp.zeros((bsz, 1, d), jnp.float32), jnp.cumsum(hf, axis=1)], axis=1)
    hi = np.arange(1, seq + 1)
    outs = []
    for g, win in enumerate(POOL_WINDOWS):
        lo = np.maximum(hi - win, 0)
        cnt = (hi - lo).astype(np.float32)
        sl = slice(g * POOL_GROUP, (g + 1) * POOL_GROUP)
        csg = cs[:, :, sl]
        pooled = (csg[:, hi] - csg[:, lo]) / cnt[None, :, None] - hf[:, :, sl]
        outs.append(jnp.einsum('bsc,cd->bsd', pooled.astype(h.dtype), pool_w[g]))
    return jnp.concatenate(outs, axis=-1) * pool_scale

def moe_ffn(h, router_w, router_bias, w_gate, w_up, w_down, sh_gate, sh_up, sh_down):
    bsz, seq, d = h.shape
    n_tok = bsz * seq
    xt = h.reshape(n_tok, d)
    scores = jax.nn.sigmoid((xt @ router_w).astype(jnp.float32))
    sel = (scores + router_bias.astype(jnp.float32)).reshape(n_tok, N_EXPERT_GROUPS, -1)
    group_score = lax.top_k(sel, 2)[0].sum(-1)
    _, top_groups = lax.top_k(group_score, TOPK_GROUPS)
    group_mask = jax.nn.one_hot(top_groups, N_EXPERT_GROUPS, dtype=jnp.float32).sum(1) > 0
    sel = jnp.where(group_mask[:, :, None], sel, -jnp.inf).reshape(n_tok, N_EXPERTS)
    _, expert_idx = lax.top_k(sel, TOP_K)
    gate_w = jnp.take_along_axis(scores, expert_idx, axis=-1)
    gate_w = gate_w / jnp.sum(gate_w, axis=-1, keepdims=True) * ROUTED_SCALE
    n_assign = n_tok * TOP_K
    flat_e = expert_idx.reshape(n_assign)
    flat_tok = jnp.repeat(jnp.arange(n_tok, dtype=jnp.int32), TOP_K)
    flat_w = gate_w.reshape(n_assign)
    order = jnp.argsort(flat_e)
    se, stok, sw = flat_e[order], flat_tok[order], flat_w[order]
    counts = jnp.bincount(flat_e, length=N_EXPERTS)
    padded = (counts + ROW_BLOCK - 1) // ROW_BLOCK * ROW_BLOCK
    pad_end = jnp.cumsum(padded)
    pad_start = pad_end - padded
    start = jnp.cumsum(counts) - counts
    dest = pad_start[se] + jnp.arange(n_assign, dtype=jnp.int32) - start[se]
    n_blocks = -(-n_assign // ROW_BLOCK) + N_EXPERTS
    n_rows = n_blocks * ROW_BLOCK
    row_tok = jnp.full((n_rows,), n_tok, jnp.int32).at[dest].set(stok)
    row_w = jnp.zeros((n_rows,), jnp.float32).at[dest].set(sw)
    block_e = jnp.minimum(jnp.searchsorted(pad_end, jnp.arange(n_blocks, dtype=jnp.int32) * ROW_BLOCK, side='right'), N_EXPERTS - 1)
    x_pad = jnp.concatenate([xt, jnp.zeros((1, d), xt.dtype)], axis=0)

    def expert_block(args):
        rows, wr, e = args
        xb = x_pad[rows]
        hb = jax.nn.silu(xb @ w_gate[e]) * (xb @ w_up[e])
        return (hb @ w_down[e]) * wr[:, None].astype(xb.dtype)

    y = lax.map(expert_block, (row_tok.reshape(n_blocks, ROW_BLOCK), row_w.reshape(n_blocks, ROW_BLOCK), block_e))
    routed = jax.ops.segment_sum(y.reshape(n_rows, d), row_tok, num_segments=n_tok + 1)[:n_tok]
    shared = (jax.nn.silu(xt @ sh_gate) * (xt @ sh_up)) @ sh_down
    return (routed + shared).reshape(bsz, seq, d)

def setup_inputs(seed: int = 0) -> dict:
    key = jax.random.key(seed)
    ks = iter(jax.random.split(key, 48))
    f32 = jnp.float32

    def nrm(shape, std):
        return jax.random.normal(next(ks), shape, f32) * std

    D, G, P, H, E = D_MODEL, S5_GROUPS, S5_STATE, S5_GROUP, N_EXPERTS
    x = nrm((BATCH, SEQ, D), 1.0)
    c = nrm((BATCH, D), 1.0)
    positions = jnp.broadcast_to(jnp.arange(SEQ, dtype=jnp.int32)[None, :], (BATCH, SEQ))
    mix_norm_g = 1.0 + nrm((DEPTH, D), 0.02)
    mix_mod_w = nrm((DEPTH, D, 3 * D), 0.5 * D ** -0.5)
    mix_mod_b = nrm((DEPTH, 3 * D), 0.02)
    ffn_norm_g = 1.0 + nrm((DEPTH, D), 0.02)
    ffn_mod_w = nrm((DEPTH, D, 3 * D), 0.5 * D ** -0.5)
    ffn_mod_b = nrm((DEPTH, 3 * D), 0.02)
    hyb_w_in = nrm((N_EVEN, D, IN_WIDTH), D ** -0.5)
    hyb_w_out = nrm((N_EVEN, MIX_WIDTH, D), MIX_WIDTH ** -0.5)
    s5_lambda_re = -0.5 + nrm((N_EVEN, G, P), 0.01)
    s5_lambda_im = math.pi * jnp.arange(P, dtype=f32) + nrm((N_EVEN, G, P), 0.01)
    s5_log_dt = jax.random.uniform(next(ks), (N_EVEN, G), f32, math.log(1e-3), math.log(1e-1))
    s5_b_re = nrm((N_EVEN, G, P, H), (2 * H) ** -0.5)
    s5_b_im = nrm((N_EVEN, G, P, H), (2 * H) ** -0.5)
    s5_c_re = nrm((N_EVEN, G, H, P), 4.0 * P ** -0.5)
    s5_c_im = nrm((N_EVEN, G, H, P), 4.0 * P ** -0.5)
    s5_d = nrm((N_EVEN, G, H), 1.0)
    s5_glu_w = nrm((N_EVEN, G, H, H), H ** -0.5)
    s5_glu_b = nrm((N_EVEN, G, H), 0.02)
    attn_q_norm_g = 1.0 + nrm((N_EVEN, HEAD_DIM), 0.02)
    attn_k_norm_g = 1.0 + nrm((N_EVEN, HEAD_DIM), 0.02)
    pool_w = nrm((N_ODD, len(POOL_WINDOWS), POOL_GROUP, POOL_GROUP), POOL_GROUP ** -0.5)
    pool_scale = 1.0 + nrm((N_ODD, D), 0.1)
    router_w = nrm((DEPTH, D, E), D ** -0.5)
    router_bias = nrm((DEPTH, E), 0.01)
    exp_w_gate = nrm((DEPTH, E, D, EXPERT_DIM), D ** -0.5)
    exp_w_up = nrm((DEPTH, E, D, EXPERT_DIM), D ** -0.5)
    exp_w_down = nrm((DEPTH, E, EXPERT_DIM, D), EXPERT_DIM ** -0.5)
    sh_w_gate = nrm((DEPTH, D, SHARED_DIM), D ** -0.5)
    sh_w_up = nrm((DEPTH, D, SHARED_DIM), D ** -0.5)
    sh_w_down = nrm((DEPTH, SHARED_DIM, D), SHARED_DIM ** -0.5)
    return {'x': x, 'c': c, 'positions': positions,
            'mix_norm_g': mix_norm_g, 'mix_mod_w': mix_mod_w, 'mix_mod_b': mix_mod_b,
            'ffn_norm_g': ffn_norm_g, 'ffn_mod_w': ffn_mod_w, 'ffn_mod_b': ffn_mod_b,
            'hyb_w_in': hyb_w_in, 'hyb_w_out': hyb_w_out,
            's5_lambda_re': s5_lambda_re, 's5_lambda_im': s5_lambda_im, 's5_log_dt': s5_log_dt,
            's5_b_re': s5_b_re, 's5_b_im': s5_b_im, 's5_c_re': s5_c_re, 's5_c_im': s5_c_im,
            's5_d': s5_d, 's5_glu_w': s5_glu_w, 's5_glu_b': s5_glu_b,
            'attn_q_norm_g': attn_q_norm_g, 'attn_k_norm_g': attn_k_norm_g,
            'pool_w': pool_w, 'pool_scale': pool_scale,
            'router_w': router_w, 'router_bias': router_bias,
            'exp_w_gate': exp_w_gate, 'exp_w_up': exp_w_up, 'exp_w_down': exp_w_down,
            'sh_w_gate': sh_w_gate, 'sh_w_up': sh_w_up, 'sh_w_down': sh_w_down}

def reference(x, c, positions, mix_norm_g, mix_mod_w, mix_mod_b, ffn_norm_g, ffn_mod_w, ffn_mod_b,
              hyb_w_in, hyb_w_out, s5_lambda_re, s5_lambda_im, s5_log_dt, s5_b_re, s5_b_im,
              s5_c_re, s5_c_im, s5_d, s5_glu_w, s5_glu_b, attn_q_norm_g, attn_k_norm_g,
              pool_w, pool_scale, router_w, router_bias, exp_w_gate, exp_w_up, exp_w_down,
              sh_w_gate, sh_w_up, sh_w_down):
    cs = jax.nn.silu(c)
    for i in range(DEPTH):
        j = i // 2
        shift, scale, gate = ada_mod(cs, mix_mod_w[i], mix_mod_b[i])
        h = modulate(rms_norm(x, mix_norm_g[i]), shift, scale)
        if i % 2 == 0:
            y = hybrid_mixer(h, positions, hyb_w_in[j], hyb_w_out[j], s5_lambda_re[j], s5_lambda_im[j],
                             s5_log_dt[j], s5_b_re[j], s5_b_im[j], s5_c_re[j], s5_c_im[j], s5_d[j],
                             s5_glu_w[j], s5_glu_b[j], attn_q_norm_g[j], attn_k_norm_g[j])
        else:
            y = pool_mixer(h, pool_w[j], pool_scale[j])
        x = x + gate[:, None, :] * y
        shift, scale, gate = ada_mod(cs, ffn_mod_w[i], ffn_mod_b[i])
        h = modulate(rms_norm(x, ffn_norm_g[i]), shift, scale)
        y = moe_ffn(h, router_w[i], router_bias[i], exp_w_gate[i], exp_w_up[i], exp_w_down[i],
                    sh_w_gate[i], sh_w_up[i], sh_w_down[i])
        x = x + gate[:, None, :] * y
    return x


_drawn_inputs = setup_inputs


def setup_inputs(seed=0):
    import zlib

    import numpy as np

    out = dict(_drawn_inputs(seed))
    spreads = {}
    factors = {'s5_lambda_re': 8.0, 's5_glu_b': 8.0, 'attn_q_norm_g': 7.75, 'attn_k_norm_g': 6.552}
    for name, (base, spread) in spreads.items():
        noise = np.random.default_rng([zlib.crc32(name.encode()), seed]).standard_normal(out[name].shape)
        drawn = base * np.exp(spread * noise) if base else spread * noise
        out[name] = jnp.asarray(drawn.astype(out[name].dtype))
    for name, factor in factors.items():
        out[name] = (out[name] * factor).astype(out[name].dtype)
    return out
```

```python
from contextlib import ExitStack, nullcontext

import numpy as np

import concourse.bass as bass
from concourse import mybir

F32 = mybir.dt.float32
BF16 = mybir.dt.bfloat16
I32 = mybir.dt.int32
U32 = mybir.dt.uint32
ALU = mybir.AluOpType
ACT = mybir.ActivationFunctionType
AX = mybir.AxisListType.X

P = 128
D = 1024
SEQ = 1024
TILES = SEQ // P
KS = D // P
EPS = 1e-6

GROUPS, GH, NS = 32, 16, 64
CH = P // GH
CHUNKS = SEQ // CH
HALF_G = GROUPS // 2

HEADS, HD = 8, 64
TOPK = 256
ROPE = 8
QKV = 1224
REST = 1280

WINDOWS = (2, 4, 8, 16)
PG = D // len(WINDOWS)

E, TK, F = 64, 8, 256
BLOCKS = 128
LOOKED = BLOCKS + 2
SURE = SEQ * TK // P
NEG = -1e30

TWO_PI = 2.0 * np.pi
PI_A = float(np.float32(6.28125))
PI_B = float(np.float32(TWO_PI - 6.28125))
PI_C = float(np.float32(TWO_PI - 6.28125 - float(np.float32(TWO_PI - 6.28125))))


def constants():
    i = np.arange(P)
    parts = {
        "ident": np.eye(P),
        "iota": np.tile(i, (P, 1)),
        "before": (i[:, None] < i[None, :]) * 1.0,
        "causal": np.where(i[None, :] <= i[:, None], 0.0, NEG),
        "swap": np.eye(P)[(i + NS) % P],
        "row": i[:, None] * 1.0,
        "token1": i[:, None] + P * np.arange(TILES)[None, :] + 1.0,
        "padrow": i[:, None] + SEQ + 1.0,
        "tie": np.tile((np.arange(8)[None, :] < np.arange(8)[:, None]).reshape(1, 64) * 1.0, (P, 1)),
        "freq": np.tile(np.power(np.float32(500000.0), -np.arange(0, 16, 2, dtype=np.float32) / 16), (P, 1)),
    }
    at, n, cols = {}, 0, []
    for name, a in parts.items():
        at[name] = (n, n + a.shape[1])
        n += a.shape[1]
        cols.append(a.astype(np.float32))
    return np.ascontiguousarray(np.concatenate(cols, 1)), at


def bands():
    out = np.zeros((P, len(WINDOWS), 3, P), np.float32)
    for w, win in enumerate(WINDOWS):
        for t in range(P):
            for back in range(win):
                s = t - back
                if s >= 0:
                    out[s, w, 0, t] = 1.0 / min(win, t + 1)
                    out[s, w, 1, t] = 1.0 / win
                else:
                    out[s + P, w, 2, t] = 1.0 / win
            out[t, w, 0, t] -= 1.0
            out[t, w, 1, t] -= 1.0
    return out.reshape(P, -1)


CONST, AT = constants()
BAND = bands()


class Chain:

    def __init__(self, eng, sem):
        self.eng, self.sem, self.n = eng, sem, 0

    def step(self, ins):
        self.n += 1
        ins.then_inc(self.sem, 1)
        self.eng.wait_ge(self.sem, self.n)


def bc(ap, shape):
    return ap.to_broadcast(shape)


def spread(row, n=P):
    return row.partition_broadcast(n)


class Core:

    def __init__(self, nc, ctx, ap):
        self.nc, self.ctx, self.ap = nc, ctx, ap
        self.sems = []
        self.x = self.sb("x", [P, TILES, D])
        self.cst = self.sb("cst", [P, CONST.shape[1]])
        self.cos_sin = self.sb("cos_sin", [P, 2, TILES, ROPE])
        self.mod = nc.dram_tensor("mod_rows", (4, 3, D), F32).ap()
        self.h_rows = nc.dram_tensor("h_rows", (SEQ + P, D), F32).ap()
        self.moe_acc = [nc.dram_tensor(f"moe_acc{i}", (SEQ + P, D), F32).ap() for i in range(2)]

    def sb(self, name, shape, dt=F32, ctx=None):
        return (ctx or self.ctx).enter_context(self.nc.sbuf_tensor(name, shape, dt))

    def ps(self, name, shape, dt=F32, ctx=None):
        return (ctx or self.ctx).enter_context(self.nc.psum_tensor(name, shape, dt))

    def sem(self, name):
        self.sems.append(self.nc.alloc_semaphore(name))
        return self.sems[-1]

    def recycle(self):
        self.nc.clear_and_free_semaphores(self.sems)
        self.nc.all_engine_barrier()
        self.sems = []

    def c(self, name):
        a, b = AT[name]
        return self.cst[:, a:b]


def load_and_modulate(k):
    nc, ap = k.nc, k.ap
    RING = 4
    sources = [(ap["mix_mod_w"][0], ap["mix_mod_b"][0], ap["mix_norm_g"][0]),
               (ap["ffn_mod_w"][0], ap["ffn_mod_b"][0], ap["ffn_norm_g"][0]),
               (ap["mix_mod_w"][1], ap["mix_mod_b"][1], ap["mix_norm_g"][1]),
               (ap["ffn_mod_w"][1], ap["ffn_mod_b"][1], ap["ffn_norm_g"][1])]
    with ExitStack() as ctx:
        c_col = k.sb("c_col", [P, KS], ctx=ctx)
        c_silu = k.sb("c_silu", [P, KS], ctx=ctx)
        ring = k.sb("mod_w_ring", [P, RING, 3 * D], ctx=ctx)
        acc = k.sb("mod_acc", [P, 2, 3 * D], ctx=ctx)
        bias = k.sb("mod_bias", [1, 4, 3 * D], ctx=ctx)
        gain = k.sb("mod_gain", [1, 4, D], ctx=ctx)
        row = k.sb("mod_row", [1, 3 * D], ctx=ctx)
        ones = k.sb("mod_ones", [P, 1], ctx=ctx)
        total = [k.ps(f"mod_total{i}", [P, 512], ctx=ctx) for i in range(6)]
        small_in, x_in = k.sem("mod_small_in"), k.sem("x_in")
        w_in = [k.sem(f"mod_w_in{i}") for i in range(RING)]
        silu_done, w_used = k.sem("c_silu_done"), k.sem("mod_w_used")
        summed, row_read, row_out = k.sem("mod_summed"), k.sem("mod_row_read"), k.sem("mod_row_out")
        row_done, chain = k.sem("mod_row_done"), k.sem("mod_chain")
        with nc.Block() as block:

            @block.sync
            def _(sp):
                sp.dma_start(c_col[:], ap["c"][0].rearrange("(p k) -> p k", k=KS)).then_inc(small_in, 16)
                sp.dma_start(k.cst[:], ap["const"]).then_inc(small_in, 16)
                for m, (_, b, g) in enumerate(sources):
                    sp.dma_start(bias[:, m, :], b.unsqueeze(0)).then_inc(small_in, 16)
                    sp.dma_start(gain[:, m, :], g.unsqueeze(0)).then_inc(small_in, 16)
                for m, (w, _, _) in enumerate(sources):
                    rows = w.rearrange("(p k) n -> k p n", k=KS)
                    for s in range(KS):
                        n = m * KS + s
                        if n >= RING:
                            sp.wait_ge(w_used, n - RING + 1)
                        sp.dma_start(ring[:, n % RING, :], rows[s]).then_inc(w_in[n % RING], 16)
                    if m == 0:
                        sp.dma_start(k.x[:], ap["x"][0].rearrange("(i p) d -> p i d", p=P)).then_inc(x_in, 16)
                sp.wait_ge(x_in, 16)
                sp.wait_ge(row_out, 4 * 16)

            @block.scalar
            def _(act):
                act.wait_ge(small_in, 10 * 16)
                nc.scalar.activation(c_silu[:], c_col[:], ACT.Silu).then_inc(silu_done, 1)
                for m in range(4):
                    act.wait_ge(row_done, m + 1)
                    act.dma_start(k.mod[m].unsqueeze(0), row[:].rearrange("a (j d) -> a j d", j=3)).then_inc(row_out, 16)

            @block.vector
            def _(dve):
                ch = Chain(dve, chain)
                ch.step(nc.vector.memset(ones[:], 1.0))
                dve.wait_ge(silu_done, 1)
                for m in range(4):
                    a = acc[:, m % 2, :]
                    for s in range(KS):
                        n = m * KS + s
                        dve.wait_ge(w_in[n % RING], 16 * (n // RING + 1))
                        if s == 0:
                            if m >= 2:
                                dve.wait_ge(summed, m - 1)
                            ins = nc.vector.tensor_scalar(a, ring[:, n % RING, :], c_silu[:, s:s + 1], None, ALU.mult)
                        else:
                            dve.wait_ge(w_used, n)
                            ins = nc.vector.scalar_tensor_tensor(a, ring[:, n % RING, :], c_silu[:, s:s + 1], a,
                                                                 ALU.mult, ALU.add)
                        ins.then_inc(w_used, 1)
                    dve.wait_ge(summed, m + 1)
                    if m:
                        dve.wait_ge(row_out, 16 * m)
                    for i, (src, dst) in enumerate([(0, 1), (1, 0), (2, 2)]):
                        for h in range(2):
                            lo = src * D + h * 512
                            ins = nc.vector.tensor_tensor(row[:, dst * D + h * 512:dst * D + h * 512 + 512],
                                                          total[2 * src + h][0:1, :], bias[:, m, lo:lo + 512], ALU.add)
                    ch.step(ins)
                    ch.step(nc.vector.tensor_scalar(row[:, 0:D], row[:, 0:D], 1.0, None, ALU.add))
                    nc.vector.tensor_tensor(row[:, 0:D], row[:, 0:D], gain[:, m, :], ALU.mult).then_inc(row_done, 1)

            @block.tensor
            def _(pe):
                for m in range(4):
                    pe.wait_ge(w_used, KS * (m + 1))
                    if m:
                        pe.wait_ge(row_done, m)
                    else:
                        pe.wait_ge(chain, 1)
                    for i in range(6):
                        mm = nc.tensor.matmul(total[i][0:1, :], ones[:], acc[:, m % 2, 512 * i:512 * i + 512],
                                              start=True, stop=True)
                    mm.then_inc(summed, 1)


def normalise(k, m, h_out, name, permuted, hT=None, rows_out=False, extra=None):
    nc = k.nc
    with ExitStack() as ctx:
        gain = k.sb(name + "_gain", [P, D], ctx=ctx)
        shift = k.sb(name + "_shift", [P, D], ctx=ctx)
        squares = k.sb(name + "_sq", [P, D], ctx=ctx)
        stat = k.sb(name + "_stat", [P, 3, TILES], ctx=ctx)
        own = None if h_out is not None else k.sb(name + "_h", [P, 2, D], ctx=ctx)
        bank = [k.ps(f"{name}_bank{i}", [P, 512], ctx=ctx) for i in range(4)]
        rows_in, squared = k.sem(name + "_rows_in"), k.sem(name + "_squared")
        mean_done, root_done, inv_done = k.sem(name + "_mean"), k.sem(name + "_root"), k.sem(name + "_inv")
        scaled, h_done = k.sem(name + "_scaled"), k.sem(name + "_h_done")
        turned, copied_a, copied_v = k.sem(name + "_turned"), k.sem(name + "_copied_a"), k.sem(name + "_copied_v")
        stored = [k.sem(f"{name}_stored{i}") for i in range(2)] if rows_out else None

        def h(i):
            return h_out[:, i, :] if h_out is not None else own[:, i % 2, :]

        with nc.Block() as block:

            @block.sync
            def _(sp):
                sp.dma_start(gain[:], spread(k.mod[m, 0])).then_inc(rows_in, 16)
                sp.dma_start(shift[:], spread(k.mod[m, 1])).then_inc(rows_in, 16)
                if extra is not None:
                    extra(sp)
                if rows_out:
                    for i in range(TILES):
                        sp.wait_ge(h_done, i + 1)
                        sp.dma_start(k.h_rows[i * P:(i + 1) * P, :], h(i)).then_inc(stored[i % 2], 16)
                    for sem in stored:
                        sp.wait_ge(sem, 16 * (TILES // 2))

            @block.scalar
            def _(act):
                for i in range(TILES):
                    if i:
                        act.wait_ge(squared, i)
                    nc.scalar.activation(squares[:], k.x[:, i, :], ACT.Square,
                                         accum_out=stat[:, 0, i:i + 1]).then_inc(squared, 1)
                act.wait_ge(mean_done, 1)
                nc.scalar.activation(stat[:, 2, :], stat[:, 1, :], ACT.Sqrt).then_inc(root_done, 1)
                if hT is not None:
                    for i in range(TILES):
                        act.wait_ge(turned, 2 * i + 1)
                        nc.scalar.copy(hT[:, 0:4, i * P:(i + 1) * P],
                                       bank[2 * (i % 2)][:].rearrange("p (s t) -> p s t", s=4)).then_inc(copied_a, 1)

            @block.vector
            def _(dve):
                dve.wait_ge(squared, TILES)
                nc.vector.tensor_scalar(stat[:, 1, :], stat[:, 0, :], 1.0 / D, EPS, ALU.mult,
                                        ALU.add).then_inc(mean_done, 1)
                dve.wait_ge(root_done, 1)
                nc.vector.reciprocal(stat[:, 0, :], stat[:, 2, :]).then_inc(inv_done, 1)
                dve.wait_ge(inv_done, 1)
                dve.wait_ge(rows_in, 32)

                def copy_back(i):
                    dve.wait_ge(turned, 2 * i + 2)
                    nc.vector.tensor_copy(hT[:, 4:8, i * P:(i + 1) * P],
                                          bank[2 * (i % 2) + 1][:].rearrange("p (s t) -> p s t", s=4)).then_inc(copied_v, 1)

                for i in range(TILES):
                    if h_out is None and i >= 2:
                        if hT is not None:
                            dve.wait_ge(turned, 2 * (i - 1))
                        if rows_out:
                            dve.wait_ge(stored[i % 2], 16 * (i // 2))
                    nc.vector.scalar_tensor_tensor(squares[:], k.x[:, i, :], stat[:, 0, i:i + 1], gain[:],
                                                   ALU.mult, ALU.mult).then_inc(scaled, 1)
                    dve.wait_ge(scaled, i + 1)
                    if permuted:
                        out = h(i).rearrange("t (s p) -> t p s", s=KS)
                        a = squares[:].rearrange("t (p s) -> t p s", s=KS)
                        b = shift[:].rearrange("t (p s) -> t p s", s=KS)
                    else:
                        out, a, b = h(i), squares[:], shift[:]
                    nc.vector.tensor_tensor(out, a, b, ALU.add).then_inc(h_done, 1)
                    dve.wait_ge(h_done, i + 1)
                    if hT is not None and i:
                        copy_back(i - 1)
                if hT is not None:
                    copy_back(TILES - 1)

            @block.tensor
            def _(pe):
                if hT is None:
                    return
                for i in range(TILES):
                    pe.wait_ge(h_done, i + 1)
                    if i >= 2:
                        pe.wait_ge(copied_a, i - 1)
                        pe.wait_ge(copied_v, i - 1)
                    for half in range(2):
                        for s in range(4):
                            mm = nc.tensor.transpose(bank[2 * (i % 2) + half][:, s * P:(s + 1) * P],
                                                     h(i)[:, (4 * half + s) * P:(4 * half + s + 1) * P], k.c("ident"))
                        mm.then_inc(turned, 1)


class Routes:

    def __init__(self, k, ctx, name):
        self.token = k.sb(name + "_slot_token", [P, LOOKED], U32, ctx=ctx)
        self.weight = k.sb(name + "_slot_weight", [P, LOOKED], ctx=ctx)
        self.block_slot = k.sb(name + "_block_slot", [1, LOOKED], I32, ctx=ctx)
        self.need_even = k.sb(name + "_need_even", [1, LOOKED], I32, ctx=ctx)
        self.need_odd = k.sb(name + "_need_odd", [1, LOOKED], I32, ctx=ctx)
        self.end = k.sb(name + "_expert_end", [1, E], I32, ctx=ctx)


def route(k, layer, hT, routes, name):
    nc, ap = k.nc, k.ap
    TE = TILES * E
    with ExitStack() as ctx:
        w = k.sb(name + "_w", [P, KS, E], ctx=ctx)
        bias = k.sb(name + "_bias", [P, E], ctx=ctx)
        score, sel, mask = (k.sb(f"{name}_{n}", [P, TE], ctx=ctx) for n in ("score", "sel", "mask"))
        tmp, tmp2 = (k.sb(f"{name}_{n}", [P, TE], ctx=ctx) for n in ("tmp", "tmp2"))
        best2 = k.sb(name + "_best2", [P, TE], ctx=ctx)
        group = k.sb(name + "_group", [P, 64], ctx=ctx)
        rank = k.sb(name + "_rank", [P, 64], ctx=ctx)
        top8 = k.sb(name + "_top8", [P, TILES, TK], ctx=ctx)
        total = k.sb(name + "_total", [P, TILES], ctx=ctx)
        mask16 = k.sb(name + "_mask16", [P, TILES, E], BF16, ctx=ctx)
        seen16 = k.sb(name + "_seen16", [P, TILES + 1, E], BF16, ctx=ctx)
        before16 = k.sb(name + "_before16", [P, P], BF16, ctx=ctx)
        ones16 = k.sb(name + "_ones16", [P, P], BF16, ctx=ctx)
        ones64 = k.sb(name + "_ones64", [P, E], ctx=ctx)
        whole = k.sb(name + "_whole", [P, TE], I32, ctx=ctx)
        nblk, end, start = (k.sb(f"{name}_{n}", [P, E], ctx=ctx) for n in ("nblk", "end", "start"))
        col = k.sb(name + "_col", [P, 1], ctx=ctx)
        line = k.sb(name + "_line", [1, 4, BLOCKS], ctx=ctx)
        line_i = k.sb(name + "_line_i", [1, BLOCKS], I32, ctx=ctx)
        slot_p, slot_b, weight8 = (k.sb(f"{name}_{n}", [P, 64], ctx=ctx) for n in ("slot_p", "slot_b", "weight8"))
        eq = k.sb(name + "_eq", [P, TK, E], ctx=ctx)
        hot_p = k.sb(name + "_hot_p", [P, 2, TK, P], ctx=ctx)
        hot_b = k.sb(name + "_hot_b", [P, 2, TK, 2, P], ctx=ctx)
        blocks = k.sb(name + "_blocks", [P, TK, P], ctx=ctx)
        pad = k.sb(name + "_pad", [P, BLOCKS], ctx=ctx)
        ps_logit = k.ps(name + "_ps_logit", [P, TE], ctx=ctx)
        ps_rank = k.ps(name + "_ps_rank", [P, TE], ctx=ctx)
        ps_count = k.ps(name + "_ps_count", [P, 512], ctx=ctx)
        ps_line = k.ps(name + "_ps_line", [P, 512], ctx=ctx)
        ps_table = k.ps(name + "_ps_table", [P, 512], ctx=ctx)
        w_in, logits, scored = k.sem(name + "_w_in"), k.sem(name + "_logits"), k.sem(name + "_scored")
        masked, ranked, col_done, lined = (k.sem(f"{name}_{n}") for n in ("masked", "ranked", "col", "lined"))
        hot, tabled, chain = k.sem(name + "_hot"), k.sem(name + "_tabled"), k.sem(name + "_chain")

        def grid(t, n=E):
            return t[:].rearrange("p (i e) -> p i e", i=TILES)

        with nc.Block() as block:

            @block.sync
            def _(sp):
                sp.dma_start(w[:], ap["router_w"][layer].rearrange("(p s) e -> p s e", s=KS)).then_inc(w_in, 16)
                sp.dma_start(bias[:], spread(ap["router_bias"][layer])).then_inc(w_in, 16)

            @block.scalar
            def _(act):
                act.wait_ge(logits, 1)
                nc.scalar.activation(score[:], ps_logit[:], ACT.Sigmoid).then_inc(scored, 1)

            @block.tensor
            def _(pe):
                pe.wait_ge(w_in, 32)
                for i in range(TILES):
                    for s in range(KS):
                        mm = nc.tensor.matmul(ps_logit[:, i * E:(i + 1) * E], hT[:, s, i * P:(i + 1) * P], w[:, s, :],
                                              start=(s == 0), stop=(s == KS - 1))
                mm.then_inc(logits, 1)
                pe.wait_ge(masked, 1)
                for i in range(TILES):
                    out = ps_rank[:, i * E:(i + 1) * E]
                    nc.tensor.matmul(out, before16[:], mask16[:, i, :], start=True, stop=False)
                    nc.tensor.matmul(out, ones16[:], seen16[:, i, :], start=False, stop=True)
                nc.tensor.matmul(ps_count[:, 0:E], ones16[:], seen16[:, TILES, :], start=True,
                                 stop=True).then_inc(ranked, 1)
                pe.wait_ge(col_done, 1)
                nc.tensor.matmul(ps_line[0:1, 0:BLOCKS], col[:], k.c("ident"), start=True, stop=True).then_inc(lined, 1)
                for i in range(TILES):
                    pe.wait_ge(hot, i + 1)
                    for j in range(TK):
                        mm = nc.tensor.matmul(ps_table[:, 0:2 * P], hot_p[:, i % 2, j, :],
                                              hot_b[:, i % 2, j, :, :].rearrange("p a b -> p (a b)"),
                                              start=(i == 0 and j == 0), stop=(i == TILES - 1 and j == TK - 1))
                    mm.then_inc(tabled, 1)

            @block.vector
            def _(dve):
                v = nc.vector
                ch = Chain(dve, chain)
                ch.step(v.memset(ones16[:], 1.0))
                ch.step(v.memset(ones64[:], 1.0))
                ch.step(v.memset(seen16[:, 0, :], 0.0))
                ch.step(v.tensor_copy(before16[:], k.c("before")))
                dve.wait_ge(w_in, 32)
                dve.wait_ge(scored, 1)
                ch.step(v.tensor_tensor(grid(sel), grid(score), bias[:].unsqueeze(1).broadcast_to([P, TILES, E]), ALU.add))
                for n in range(64):
                    ins = v.max(best2[:, n * 8:n * 8 + 8], sel[:, n * 8:n * 8 + 8])
                ch.step(ins)
                best = best2[:].rearrange("p (n j) -> p n j", j=8)
                ch.step(v.tensor_tensor(group[:].unsqueeze(2), best[:, :, 0:1], best[:, :, 1:2], ALU.add))
                other = group[:].rearrange("p (i g) -> p i g", g=8).unsqueeze(2).broadcast_to([P, 8, 8, 8])
                mine = group[:].rearrange("p (i g) -> p i g", g=8).unsqueeze(3).broadcast_to([P, 8, 8, 8])
                four = lambda t: t[:].rearrange("p (i g h) -> p i g h", g=8, h=8)
                ch.step(v.tensor_tensor(four(tmp), other, mine, ALU.is_gt))
                ch.step(v.tensor_tensor(four(tmp2), other, mine, ALU.is_equal))
                ch.step(v.tensor_tensor(grid(tmp2), grid(tmp2), k.c("tie").unsqueeze(1).broadcast_to([P, TILES, 64]), ALU.mult))
                ch.step(v.tensor_tensor(tmp[:], tmp[:], tmp2[:], ALU.add))
                ch.step(v.tensor_reduce(rank[:], tmp[:].rearrange("p (n j) -> p n j", j=8), AX, ALU.add))
                ch.step(v.tensor_scalar(rank[:], rank[:], 3.5, None, ALU.is_lt))
                wide = rank[:].unsqueeze(2).broadcast_to([P, 64, 8])
                eight = lambda t: t[:].rearrange("p (n j) -> p n j", j=8)
                ch.step(v.tensor_tensor(eight(sel), eight(sel), wide, ALU.mult))
                ch.step(v.tensor_scalar(rank[:], rank[:], -NEG, NEG, ALU.mult, ALU.add))
                ch.step(v.tensor_tensor(eight(sel), eight(sel), wide, ALU.add))
                for i in range(TILES):
                    ins = v.max(top8[:, i, :], sel[:, i * E:(i + 1) * E])
                ch.step(ins)
                for i in range(TILES):
                    ins = v.match_replace(tmp[:, i * E:(i + 1) * E], top8[:, i, :], sel[:, i * E:(i + 1) * E], -3e38)
                ch.step(ins)
                ch.step(v.tensor_scalar(mask[:], tmp[:], -2e38, None, ALU.is_lt))
                ch.step(v.tensor_copy(mask16[:], grid(mask)))
                for i in range(TILES):
                    ins = v.tensor_tensor(seen16[:, i + 1, :], seen16[:, i, :], mask16[:, i, :], ALU.add)
                    if i < TILES - 1:
                        ch.step(ins)
                ins.then_inc(masked, 1)
                ch.step(v.tensor_tensor(score[:], score[:], mask[:], ALU.mult))
                ch.step(v.tensor_reduce(total[:], grid(score), AX, ALU.add))
                ch.step(v.reciprocal(total[:], total[:]))
                ch.step(v.tensor_scalar(total[:], total[:], 2.5, None, ALU.mult))
                ch.step(v.tensor_tensor(grid(score), grid(score), total[:].unsqueeze(2).broadcast_to([P, TILES, E]), ALU.mult))
                dve.wait_ge(ranked, 1)
                ch.step(v.tensor_scalar(whole[:, 0:E], ps_count[:, 0:E], 1.0 / P, 127.0 / 256, ALU.mult, ALU.add))
                ch.step(v.tensor_copy(nblk[:], whole[:, 0:E]))
                ch.step(v.tensor_tensor_scan(end[:], ones64[:], nblk[:], 0.0, ALU.mult, ALU.add))
                ch.step(v.tensor_tensor(start[:], end[:], nblk[:], ALU.subtract))
                ch.step(v.tensor_scalar(ones64[:], end[:], k.c("row"), 0.0, ALU.is_le, ALU.add, accum_out=col[:]))
                v.tensor_scalar(col[:], col[:], E - 1.0, None, ALU.min).then_inc(col_done, 1)
                ch.step(v.tensor_copy(routes.end[:], end[0:1, :]))
                ch.step(v.tensor_scalar(whole[:], ps_rank[:], 1.0 / P, -127.0 / 256, ALU.mult, ALU.add))
                ch.step(v.tensor_copy(tmp[:], whole[:]))
                ch.step(v.tensor_scalar(tmp[:], tmp[:], -(127.0 * P + P - 1), 1.0, ALU.mult, ALU.add))
                ch.step(v.scalar_tensor_tensor(tmp2[:], ps_rank[:], float(P), tmp[:], ALU.mult, ALU.add))
                ch.step(v.tensor_tensor(grid(tmp2), grid(tmp2), start[:].unsqueeze(1).broadcast_to([P, TILES, E]), ALU.add))
                ch.step(v.tensor_tensor(tmp2[:], tmp2[:], mask[:], ALU.mult))
                for i in range(TILES):
                    ins = v.max(top8[:, i, :], tmp2[:, i * E:(i + 1) * E])
                ch.step(ins)
                for i in range(TILES):
                    keys = tmp2[:, i * E:(i + 1) * E].unsqueeze(1).broadcast_to([P, TK, E])
                    mine = top8[:, i, :].unsqueeze(2).broadcast_to([P, TK, E])
                    gates = score[:, i * E:(i + 1) * E].unsqueeze(1).broadcast_to([P, TK, E])
                    ch.step(v.tensor_tensor(eq[:], keys, mine, ALU.is_equal))
                    ch.step(v.tensor_tensor(eq[:], eq[:], gates, ALU.mult))
                    ch.step(v.tensor_reduce(weight8[:, i * TK:(i + 1) * TK], eq[:], AX, ALU.add))
                flat8 = top8[:].rearrange("p i j -> p (i j)")
                ch.step(v.tensor_scalar(rank[:], flat8, -1.0, None, ALU.add))
                ch.step(v.tensor_scalar(whole[:, 0:64], rank[:], 1.0 / P, -127.0 / 256, ALU.mult, ALU.add))
                ch.step(v.tensor_copy(slot_p[:], whole[:, 0:64]))
                ch.step(v.scalar_tensor_tensor(slot_b[:], slot_p[:], -float(P), rank[:], ALU.mult, ALU.add))
                dve.wait_ge(lined, 1)
                ch.step(v.tensor_copy(line[:, 0, :], ps_line[0:1, 0:BLOCKS]))
                ch.step(v.tensor_scalar(line_i[:], line[:, 0, :], 0.5, -0.25, ALU.mult, ALU.add))
                ch.step(v.tensor_copy(line[:, 1, :], line_i[:]))
                ch.step(v.scalar_tensor_tensor(line[:, 2, :], line[:, 1, :], -2.0, line[:, 0, :], ALU.mult, ALU.add))
                ch.step(v.tensor_copy(routes.block_slot[:, 0:BLOCKS], line[:, 2, :]))
                ch.step(v.tensor_scalar(routes.need_even[:, 0:BLOCKS], line[:, 1, :], 48.0, 48.0, ALU.mult, ALU.add))
                ch.step(v.tensor_tensor(line[:, 3, :], line[:, 1, :], line[:, 2, :], ALU.add))
                ch.step(v.tensor_scalar(routes.need_odd[:, 0:BLOCKS], line[:, 3, :], 48.0, 48.0, ALU.mult, ALU.max))
                across = k.c("iota").unsqueeze(1).broadcast_to([P, TK, P])
                for i in range(TILES):
                    u = i % 2
                    if i >= 2:
                        dve.wait_ge(tabled, i - 1)
                    lo, hi = i * TK, (i + 1) * TK
                    v.tensor_tensor(hot_p[:, u], across, slot_p[:, lo:hi].unsqueeze(2).broadcast_to([P, TK, P]), ALU.is_equal)
                    ch.step(v.tensor_tensor(blocks[:], across, slot_b[:, lo:hi].unsqueeze(2).broadcast_to([P, TK, P]),
                                            ALU.is_equal))
                    v.tensor_scalar(hot_b[:, u, :, 0, :], blocks[:], k.c("token1")[:, i:i + 1], None, ALU.mult)
                    ins = v.tensor_tensor(hot_b[:, u, :, 1, :], blocks[:],
                                          weight8[:, lo:hi].unsqueeze(2).broadcast_to([P, TK, P]), ALU.mult)
                    ins.then_inc(hot, 1)
                    dve.wait_ge(hot, i + 1)
                dve.wait_ge(tabled, TILES)
                ch.step(v.tensor_scalar(pad[:], ps_table[:, 0:P], 0.0, k.c("padrow"), ALU.is_equal, ALU.mult))
                ch.step(v.scalar_tensor_tensor(pad[:], ps_table[:, 0:P], -1.0, pad[:], ALU.add, ALU.add))
                ch.step(v.tensor_copy(routes.token[:, 0:BLOCKS], pad[:]))
                ch.step(v.tensor_copy(routes.weight[:, 0:BLOCKS], ps_table[:, P:2 * P]))


def gated(nc, gate_up, silu, out_hidden):
    return nc.vector.tensor_tensor(out_hidden.rearrange("t (c p) -> t p c", c=2),
                                   silu.rearrange("t (p c) -> t p c", c=2),
                                   gate_up[:, F:2 * F].rearrange("t (p c) -> t p c", c=2), ALU.mult)


def shared_expert(k, layer, hT, name):
    nc, ap = k.nc, k.ap
    acc = k.moe_acc[layer]
    with ExitStack() as ctx:
        wg, wu = (k.sb(f"{name}_{n}", [P, KS, F], ctx=ctx) for n in ("wg", "wu"))
        wd = k.sb(name + "_wd", [P, 2, D], ctx=ctx)
        silu = k.sb(name + "_silu", [P, F], ctx=ctx)
        hidden = k.sb(name + "_hidden", [P, F], ctx=ctx)
        hidT = k.sb(name + "_hidT", [P, 2, P], ctx=ctx)
        y = k.sb(name + "_y", [P, 2, D], ctx=ctx)
        zero = k.sb(name + "_zero", [P, D], ctx=ctx)
        ps_gu = [k.ps(f"{name}_ps_gu{i}", [P, 512], ctx=ctx) for i in range(2)]
        ps_t = k.ps(name + "_ps_t", [P, 512], ctx=ctx)
        ps_y = [k.ps(f"{name}_ps_y{i}", [P, 512], ctx=ctx) for i in range(2)]
        w_in, gu_done, silu_done, hid_done = (k.sem(f"{name}_{n}") for n in ("w_in", "gu", "silu", "hid"))
        turned, hidT_done, y_done = (k.sem(f"{name}_{n}") for n in ("turned", "hidT", "y_done"))
        y_act, y_dve, zeroed = (k.sem(f"{name}_{n}") for n in ("y_act", "y_dve", "zeroed"))
        y_out = [k.sem(f"{name}_y_out{i}") for i in range(2)]
        zero_out = k.sem(name + "_zero_out")
        with nc.Block() as block:

            @block.sync
            def _(sp):
                sp.dma_start(wg[:], ap["sh_w_gate"][layer].rearrange("(p s) f -> p s f", s=KS)).then_inc(w_in, 16)
                sp.dma_start(wu[:], ap["sh_w_up"][layer].rearrange("(p s) f -> p s f", s=KS)).then_inc(w_in, 16)
                sp.dma_start(wd[:], ap["sh_w_down"][layer].rearrange("(p c) n -> p c n", c=2)).then_inc(w_in, 16)
                sp.wait_ge(zeroed, 1)
                sp.dma_start(acc[SEQ:SEQ + P, :], zero[:]).then_inc(zero_out, 16)
                sp.dma_start(k.h_rows[SEQ:SEQ + P, :], zero[:]).then_inc(zero_out, 16)
                for i in range(TILES):
                    sp.wait_ge(y_act, i + 1)
                    sp.wait_ge(y_dve, i + 1)
                    sp.dma_start(acc[i * P:(i + 1) * P, :], y[:, i % 2, :]).then_inc(y_out[i % 2], 16)
                for sem in y_out:
                    sp.wait_ge(sem, 16 * (TILES // 2))
                sp.wait_ge(zero_out, 32)

            @block.tensor
            def _(pe):
                def gate_up(i):
                    for half, w in enumerate((wg, wu)):
                        for s in range(KS):
                            mm = nc.tensor.matmul(ps_gu[i % 2][:, half * F:(half + 1) * F], hT[:, s, i * P:(i + 1) * P],
                                                  w[:, s, :], start=(s == 0), stop=(s == KS - 1))
                    mm.then_inc(gu_done, 1)

                pe.wait_ge(w_in, 48)
                gate_up(0)
                for i in range(TILES):
                    if i + 1 < TILES:
                        gate_up(i + 1)
                    pe.wait_ge(hid_done, i + 1)
                    for c in range(2):
                        mm = nc.tensor.transpose(ps_t[:, c * P:(c + 1) * P], hidden[:, c * P:(c + 1) * P], k.c("ident"))
                    mm.then_inc(turned, 1)
                    pe.wait_ge(hidT_done, i + 1)
                    if i:
                        pe.wait_ge(y_act, i)
                        pe.wait_ge(y_dve, i)
                    for n in range(2):
                        for c in range(2):
                            mm = nc.tensor.matmul(ps_y[n][:], hidT[:, c, :], wd[:, c, n * 512:(n + 1) * 512],
                                                  start=(c == 0), stop=(c == 1))
                    mm.then_inc(y_done, 1)

            @block.scalar
            def _(act):
                for i in range(TILES):
                    act.wait_ge(gu_done, i + 1)
                    if i:
                        act.wait_ge(hid_done, i)
                    nc.scalar.activation(silu[:], ps_gu[i % 2][:, 0:F], ACT.Silu).then_inc(silu_done, 1)
                    act.wait_ge(y_done, i + 1)
                    if i >= 2:
                        act.wait_ge(y_out[i % 2], 16 * (i // 2))
                    nc.scalar.copy(y[:, i % 2, 0:512], ps_y[0][:]).then_inc(y_act, 1)

            @block.vector
            def _(dve):
                nc.vector.memset(zero[:], 0.0).then_inc(zeroed, 1)
                for i in range(TILES):
                    dve.wait_ge(silu_done, i + 1)
                    if i:
                        dve.wait_ge(turned, i)
                    gated(nc, ps_gu[i % 2], silu[:], hidden[:]).then_inc(hid_done, 1)
                    dve.wait_ge(turned, i + 1)
                    nc.vector.tensor_copy(hidT[:], ps_t[:, 0:2 * P].rearrange("p (c t) -> p c t", c=2)).then_inc(hidT_done, 1)
                    dve.wait_ge(y_done, i + 1)
                    if i >= 2:
                        dve.wait_ge(y_out[i % 2], 16 * (i // 2))
                    nc.vector.tensor_copy(y[:, i % 2, 512:1024], ps_y[1][:]).then_inc(y_dve, 1)


def experts(k, layer, routes, name):
    nc, ap = k.nc, k.ap
    acc = k.moe_acc[layer]
    with ExitStack() as ctx:
        wg, wu = (k.sb(f"{name}_{n}", [P, 2, KS, F], ctx=ctx) for n in ("wg", "wu"))
        wd = k.sb(name + "_wd", [P, 2, 2, D], ctx=ctx)
        rows = [k.sb(f"{name}_rows{i}", [P, D], ctx=ctx) for i in range(2)]
        rowsT = [k.sb(f"{name}_rowsT{i}", [P, KS, P], ctx=ctx) for i in range(2)]
        gather_at = [k.sb(f"{name}_gather_at{i}", [P, 1], U32, ctx=ctx) for i in range(2)]
        add_at = k.sb(name + "_add_at", [P, 1], U32, ctx=ctx)
        silu = k.sb(name + "_silu", [P, F], ctx=ctx)
        hidden = k.sb(name + "_hidden", [P, F], ctx=ctx)
        hidT = [k.sb(f"{name}_hidT{i}", [P, 2, P], ctx=ctx) for i in range(2)]
        y = [k.sb(f"{name}_y{i}", [P, D], ctx=ctx) for i in range(2)]
        ps_x = [k.ps(f"{name}_ps_x{i}", [P, 512], ctx=ctx) for i in range(2)]
        ps_gu = k.ps(name + "_ps_gu", [P, 512], ctx=ctx)
        ps_t = k.ps(name + "_ps_t", [P, 512], ctx=ctx)
        ps_y = [k.ps(f"{name}_ps_y{i}", [P, 512], ctx=ctx) for i in range(2)]
        w_in = [k.sem(f"{name}_w_in{i}") for i in range(2)]
        rows_in = [k.sem(f"{name}_rows_in{i}") for i in range(2)]
        rows_turned, rowsT_act, rowsT_dve = (k.sem(f"{name}_{n}") for n in ("rows_turned", "rowsT_act", "rowsT_dve"))
        gu_done, silu_done, hid_done = (k.sem(f"{name}_{n}") for n in ("gu_done", "silu_done", "hid_done"))
        hid_turned, hidT_done = (k.sem(f"{name}_{n}") for n in ("hid_turned", "hidT_done"))
        y_done, y_act, y_dve = (k.sem(f"{name}_{n}") for n in ("y_done", "y_act", "y_dve"))
        added, gather_set, add_set, pool_steps = (k.sem(f"{name}_{n}") for n in ("added", "gather_set", "add_set", "pool_steps"))

        def used(eng):
            return eng.value_load(routes.end[0:1, E - 1:E], min_val=SURE, max_val=BLOCKS - 1)

        def when(eng, b, n, sure):
            return nullcontext() if sure else eng.If(b < n)

        def schedule(eng, step):
            n = used(eng)
            step(0, 0, n, True)
            step(1, 1, n, True)
            with eng.Fori(1, SURE // 2 - 1) as i:
                for half in range(2):
                    step(2 * i + half, half, n, True)
            with eng.Fori(SURE // 2 - 1, BLOCKS // 2) as i:
                for half in range(2):
                    step(2 * i + half, half, n, False)
            return n

        with nc.Block() as block:

            @block.sync
            def _(sp):
                def load(e, half):
                    for w, src in ((wg, "exp_w_gate"), (wu, "exp_w_up")):
                        table = ap[src][layer].rearrange("e (p s) f -> e p (s f)", s=KS)
                        sp.dma_start(w[:, half].rearrange("p s f -> p (s f)"),
                                     table[bass.ds(e, 1)].squeeze(0)).then_inc(w_in[half], 16)
                    table = ap["exp_w_down"][layer].rearrange("e (p c) n -> e p (c n)", c=2)
                    sp.dma_start(wd[:, half].rearrange("p c n -> p (c n)"),
                                 table[bass.ds(e, 1)].squeeze(0)).then_inc(w_in[half], 16)

                load(0, 0)
                load(1, 1)
                with sp.Fori(1, E // 2) as i:
                    for half in range(2):
                        before = sp.value_load(routes.end[0:1, bass.ds(2 * i + half - 2, 1)], min_val=0,
                                               max_val=BLOCKS - 1)
                        sp.wait_ge(y_done, before + 1)
                        load(2 * i + half, half)

            @block.gpsimd
            def _(pool):
                def gather(b, half, first=False):
                    if not first:
                        pool.wait_ge(rows_turned, 2 * (b - 1))
                    pool.tensor_copy(gather_at[half][:], routes.token[:, bass.ds(b, 1)]).then_inc(gather_set, 1)
                    pool.wait_ge(gather_set, b + 1)
                    pool.sem_inc(pool_steps, 1)
                    pool.indirect_dma_start(out=rows[half][:], out_offset=None, in_=k.h_rows,
                                            in_offset=bass.IndirectOffsetOnAxis(ap=gather_at[half][:], axis=0)
                                            ).then_inc(rows_in[half], 16)

                def add(b, half):
                    if not (isinstance(b, int) and b == 0):
                        pool.wait_ge(added, 16 * b)
                    pool.tensor_copy(add_at[:], routes.token[:, bass.ds(b, 1)]).then_inc(add_set, 1)
                    pool.wait_ge(add_set, b + 1)
                    pool.wait_ge(y_act, b + 1)
                    pool.wait_ge(y_dve, b + 1)
                    pool.sem_inc(pool_steps, 1)
                    pool.indirect_dma_start(out=acc, out_offset=bass.IndirectOffsetOnAxis(ap=add_at[:], axis=0),
                                            in_=y[half][:], in_offset=None, compute_op=ALU.add).then_inc(added, 16)

                def step(b, half, n, sure):
                    with when(pool, b + 2, n, sure):
                        gather(b + 2, half)
                    if isinstance(b, int) and b == 0:
                        return
                    with when(pool, b - 1, n, sure):
                        add(b - 1, 1 - half)

                gather(0, 0, first=True)
                gather(1, 1, first=True)
                n = schedule(pool, step)
                pool.wait_ge(added, 16 * n)

            @block.tensor
            def _(pe):
                def turn_rows(b, half):
                    pe.wait_ge(rows_in[half], 16 * (b // 2 + 1) if isinstance(b, int) else 8 * (b - half) + 16)
                    if not (isinstance(b, int) and b == 0):
                        pe.wait_ge(rowsT_act, b)
                        pe.wait_ge(rowsT_dve, b)
                    for bank in range(2):
                        for s in range(4):
                            mm = pe.transpose(ps_x[bank][:, s * P:(s + 1) * P],
                                              rows[half][:, (4 * bank + s) * P:(4 * bank + s + 1) * P], k.c("ident"))
                        mm.then_inc(rows_turned, 1)

                def expert_half(b):
                    return pe.value_load(routes.block_slot[0:1, bass.ds(b, 1)], min_val=0, max_val=1)

                def gate_up(b, half):
                    even = pe.value_load(routes.need_even[0:1, bass.ds(b, 1)], min_val=48, max_val=48 * E)
                    odd = pe.value_load(routes.need_odd[0:1, bass.ds(b, 1)], min_val=48, max_val=48 * E)
                    at = expert_half(b)
                    pe.wait_ge(w_in[0], even)
                    pe.wait_ge(w_in[1], odd)
                    pe.wait_ge(rowsT_act, b + 1)
                    pe.wait_ge(rowsT_dve, b + 1)
                    for j, w in enumerate((wg, wu)):
                        for s in range(KS):
                            mm = pe.matmul(ps_gu[:, j * F:(j + 1) * F], rowsT[half][:, s, :],
                                           w[:, bass.ds(at, 1), s, :].squeeze(1), start=(s == 0), stop=(s == KS - 1))
                    mm.then_inc(gu_done, 1)

                def down(b, half):
                    at = expert_half(b)
                    pe.wait_ge(hidT_done, b + 1)
                    if not (isinstance(b, int) and b == 0):
                        pe.wait_ge(y_act, b)
                        pe.wait_ge(y_dve, b)
                    for j in range(2):
                        for c in range(2):
                            mm = pe.matmul(ps_y[j][:], hidT[half][:, c, :],
                                           wd[:, bass.ds(at, 1), c, j * 512:(j + 1) * 512].squeeze(1),
                                           start=(c == 0), stop=(c == 1))
                    mm.then_inc(y_done, 1)

                def turn_hidden(b):
                    pe.wait_ge(hid_done, b + 1)
                    for c in range(2):
                        mm = pe.transpose(ps_t[:, c * P:(c + 1) * P], hidden[:, c * P:(c + 1) * P], k.c("ident"))
                    mm.then_inc(hid_turned, 1)

                def step(b, half, n, sure):
                    with when(pe, b, n, sure):
                        gate_up(b, half)
                    with when(pe, b + 1, n, sure):
                        turn_rows(b + 1, 1 - half)
                    if not (isinstance(b, int) and b == 0):
                        with when(pe, b - 1, n, sure):
                            down(b - 1, 1 - half)
                    with when(pe, b, n, sure):
                        turn_hidden(b)

                pe.sem_inc(y_done, 1)
                turn_rows(0, 0)
                schedule(pe, step)

            @block.scalar
            def _(act):
                def rows_back(b, half):
                    act.wait_ge(rows_turned, 2 * b + 1)
                    act.copy(rowsT[half][:, 0:4, :], ps_x[0][:].rearrange("p (s t) -> p s t", s=4)).then_inc(rowsT_act, 1)

                def silu_of(b):
                    act.wait_ge(gu_done, b + 1)
                    if not (isinstance(b, int) and b == 0):
                        act.wait_ge(hid_done, b)
                    act.activation(silu[:], ps_gu[:, 0:F], ACT.Silu).then_inc(silu_done, 1)

                def y_back(b, half):
                    act.wait_ge(y_done, b + 2)
                    if not (isinstance(b, int) and b < 2):
                        act.wait_ge(added, 16 * (b - 1))
                    act.activation(y[half][:, 0:512], ps_y[0][:], ACT.Copy,
                                   scale=routes.weight[:, bass.ds(b, 1)]).then_inc(y_act, 1)

                def step(b, half, n, sure):
                    with when(act, b, n, sure):
                        silu_of(b)
                    with when(act, b + 1, n, sure):
                        rows_back(b + 1, 1 - half)
                    if not (isinstance(b, int) and b == 0):
                        with when(act, b - 1, n, sure):
                            y_back(b - 1, 1 - half)

                rows_back(0, 0)
                schedule(act, step)

            @block.vector
            def _(dve):
                def rows_back(b, half):
                    dve.wait_ge(rows_turned, 2 * b + 2)
                    dve.tensor_copy(rowsT[half][:, 4:8, :],
                                    ps_x[1][:].rearrange("p (s t) -> p s t", s=4)).then_inc(rowsT_dve, 1)

                def hidden_of(b):
                    dve.wait_ge(silu_done, b + 1)
                    if not (isinstance(b, int) and b == 0):
                        dve.wait_ge(hid_turned, b)
                    gated(nc, ps_gu, silu[:], hidden[:]).then_inc(hid_done, 1)

                def hidden_back(b, half):
                    dve.wait_ge(hid_turned, b + 1)
                    dve.tensor_copy(hidT[half][:], ps_t[:, 0:2 * P].rearrange("p (c t) -> p c t", c=2)
                                    ).then_inc(hidT_done, 1)

                def y_back(b, half):
                    dve.wait_ge(y_done, b + 2)
                    if not (isinstance(b, int) and b < 2):
                        dve.wait_ge(added, 16 * (b - 1))
                    dve.tensor_scalar(y[half][:, 512:1024], ps_y[1][:], routes.weight[:, bass.ds(b, 1)], None,
                                      ALU.mult).then_inc(y_dve, 1)

                def step(b, half, n, sure):
                    with when(dve, b, n, sure):
                        hidden_of(b)
                    with when(dve, b + 1, n, sure):
                        rows_back(b + 1, 1 - half)
                    if not (isinstance(b, int) and b == 0):
                        with when(dve, b - 1, n, sure):
                            y_back(b - 1, 1 - half)
                    with when(dve, b, n, sure):
                        hidden_back(b, half)

                rows_back(0, 0)
                schedule(dve, step)


def moe_residual(k, layer, m, name, out=None):
    nc = k.nc
    acc = k.moe_acc[layer]
    with ExitStack() as ctx:
        gate = k.sb(name + "_gate", [P, D], ctx=ctx)
        part = k.sb(name + "_part", [P, 4, D], ctx=ctx)
        gate_in, gated_done, x_done = (k.sem(f"{name}_{n}") for n in ("gate_in", "gated", "x_done"))
        part_in = [k.sem(f"{name}_part_in{i}") for i in range(4)]
        out_done = k.sem(name + "_out")
        with nc.Block() as block:

            @block.sync
            def _(sp):
                sp.dma_start(gate[:], spread(k.mod[m, 2])).then_inc(gate_in, 16)
                for i in range(TILES):
                    if i >= 4:
                        sp.wait_ge(x_done, i - 3)
                    sp.dma_start(part[:, i % 4, :], acc[i * P:(i + 1) * P, :]).then_inc(part_in[i % 4], 16)

            @block.vector
            def _(dve):
                dve.wait_ge(gate_in, 16)
                for i in range(TILES):
                    dve.wait_ge(part_in[i % 4], 16 * (i // 4 + 1))
                    nc.vector.tensor_tensor(part[:, i % 4, :], part[:, i % 4, :], gate[:], ALU.mult).then_inc(gated_done, 1)
                    dve.wait_ge(gated_done, i + 1)
                    nc.vector.tensor_tensor(k.x[:, i, :], k.x[:, i, :], part[:, i % 4, :], ALU.add).then_inc(x_done, 1)

            @block.scalar
            def _(act):
                if out is None:
                    return
                for i in range(TILES):
                    act.wait_ge(x_done, i + 1)
                    act.dma_start(out[i * P:(i + 1) * P, :], k.x[:, i, :]).then_inc(out_done, 16)
                act.wait_ge(out_done, 16 * TILES)


def moe(k, layer, m, name, out=None):
    with ExitStack() as ctx:
        routes = Routes(k, ctx, name)
        with ExitStack() as inner:
            hT = k.sb(name + "_hT", [P, KS, SEQ], ctx=inner)
            normalise(k, m, None, name + "_n", True, hT=hT, rows_out=True)
            route(k, layer, hT, routes, name + "_r")
            shared_expert(k, layer, hT, name + "_s")
        experts(k, layer, routes, name + "_e")
    moe_residual(k, layer, m, name + "_x", out)


def project_u(k, hT, u_rows, uT):
    nc, ap = k.nc, k.ap
    W5 = GROUPS * GH
    with ExitStack() as ctx:
        w = k.sb("u_w", [P, KS, W5], ctx=ctx)
        ps = [k.ps(f"u_ps{i}", [P, 512], ctx=ctx) for i in range(2)]
        ps_t = [k.ps(f"u_ps_t{i}", [P, 512], ctx=ctx) for i in range(2)]
        w_in, done, copied, turned, back = (k.sem(f"u_{n}") for n in ("w_in", "done", "copied", "turned", "back"))
        with nc.Block() as block:

            @block.sync
            def _(sp):
                sp.dma_start(w[:], ap["hyb_w_in"][0][:, 0:W5].rearrange("(p s) n -> p s n", s=KS)).then_inc(w_in, 16)

            @block.tensor
            def _(pe):
                pe.wait_ge(w_in, 16)
                for j in range(CH):
                    if j >= 2:
                        pe.wait_ge(copied, j - 1)
                    for s in range(KS):
                        mm = pe.matmul(ps[j % 2][:], hT[:, s, j:SEQ:CH], w[:, s, :], start=(s == 0), stop=(s == KS - 1))
                    mm.then_inc(done, 1)
                pe.wait_ge(copied, CH)
                for q in range(GROUPS // 4):
                    if q >= 2:
                        pe.wait_ge(back, q - 1)
                    for g in range(4):
                        mm = pe.transpose(ps_t[q % 2][:, g * P:(g + 1) * P],
                                          u_rows[:, 4 * q + g].rearrange("c j h -> c (j h)"), k.c("ident"))
                    mm.then_inc(turned, 1)

            @block.scalar
            def _(act):
                for j in range(CH):
                    act.wait_ge(done, j + 1)
                    act.copy(u_rows[:, :, j, :], ps[j % 2][:].rearrange("c (g h) -> c g h", h=GH)).then_inc(copied, 1)

            @block.vector
            def _(dve):
                for q in range(GROUPS // 4):
                    dve.wait_ge(turned, q + 1)
                    dve.tensor_copy(uT[:, 4 * q:4 * q + 4, :], ps_t[q % 2][:].rearrange("p (g c) -> p g c", g=4)
                                    ).then_inc(back, 1)


def sine_tables(k, cos_sin, rotor, lam, dt, mag):
    nc, ap = k.nc, k.ap
    N = TILES * ROPE + GROUPS
    with ExitStack() as ctx:
        pos = k.sb("st_pos", [P, TILES], I32, ctx=ctx)
        pos_f = k.sb("st_pos_f", [P, TILES], ctx=ctx)
        lam_in = k.sb("st_lam_in", [GROUPS, 2, 2, NS], ctx=ctx)
        ang = k.sb("st_ang", [P, N], ctx=ctx)
        turns = k.sb("st_turns", [P, N], I32, ctx=ctx)
        turns_f = k.sb("st_turns_f", [P, N], ctx=ctx)
        co = k.sb("st_co", [P, N], ctx=ctx)
        both = k.sb("st_both", [P, 2, N], ctx=ctx)
        decay = k.sb("st_decay", [P, GROUPS], ctx=ctx)
        ps = k.ps("st_ps", [P, 512], ctx=ctx)
        loaded, turned, dt_done, ready, waves, chain = (k.sem(f"st_{n}") for n in
                                                        ("loaded", "turned", "dt", "ready", "waves", "chain"))
        with nc.Block() as block:

            @block.sync
            def _(sp):
                sp.dma_start(dt[:], spread(ap["s5_log_dt"][0])).then_inc(loaded, 16)
                for half in range(2):
                    sp.dma_start(lam_in[:, 0, half, :], ap["s5_lambda_re"][0]).then_inc(loaded, 16)
                    sp.dma_start(lam_in[:, 1, half, :], ap["s5_lambda_im"][0]).then_inc(loaded, 16)
                with nc.allow_non_contiguous_dma(reason="1024 positions"):
                    sp.dma_start(pos[:], ap["positions"][0].rearrange("(i p) -> p i", p=P)).then_inc(loaded, 16)

            @block.tensor
            def _(pe):
                pe.wait_ge(loaded, 96)
                for i in range(2):
                    mm = pe.transpose(ps[:, i * GROUPS:(i + 1) * GROUPS], lam_in[:, i].rearrange("g a p -> g (a p)"),
                                      k.c("ident")[0:GROUPS, 0:GROUPS])
                mm.then_inc(turned, 1)

            @block.scalar
            def _(act):
                act.wait_ge(loaded, 96)
                act.activation(dt[:], dt[:], ACT.Exp).then_inc(dt_done, 1)
                act.wait_ge(ready, 1)
                act.activation(mag[:, 0, :], decay[:], ACT.Exp)
                act.activation(mag[:, 1, :], decay[:], ACT.Exp, scale=float(CH)).then_inc(waves, 1)
                act.wait_ge(ready, 2)
                act.activation(both[:, 0, :], co[:], ACT.Sin)
                act.activation(both[:, 1, :], ang[:], ACT.Sin).then_inc(waves, 1)

            @block.vector
            def _(dve):
                ch = Chain(dve, chain)
                dve.wait_ge(turned, 1)
                ch.step(dve.tensor_copy(lam[:], ps[:, 0:2 * GROUPS].rearrange("p (a g) -> p a g", a=2)))
                dve.wait_ge(dt_done, 1)
                ch.step(dve.tensor_copy(pos_f[:], pos[:]))
                ch.step(dve.tensor_tensor(ang[:, 0:64].rearrange("p (i r) -> p i r", r=ROPE),
                                          pos_f[:].unsqueeze(2).broadcast_to([P, TILES, ROPE]),
                                          k.c("freq").unsqueeze(1).broadcast_to([P, TILES, ROPE]), ALU.mult))
                ch.step(dve.tensor_tensor(ang[:, 64:N], lam[:, 1, :], dt[:], ALU.mult))
                dve.tensor_tensor(decay[:], lam[:, 0, :], dt[:], ALU.mult).then_inc(ready, 1)
                ch.step(dve.tensor_scalar(turns[:], ang[:], float(1.0 / TWO_PI), None, ALU.mult))
                ch.step(dve.tensor_copy(turns_f[:], turns[:]))
                for part in (PI_A, PI_B, PI_C):
                    ch.step(dve.scalar_tensor_tensor(ang[:], turns_f[:], -part, ang[:], ALU.mult, ALU.add))
                ch.step(dve.tensor_scalar(ang[:], ang[:], 3.1415925, -3.1415925, ALU.min, ALU.max))
                ch.step(dve.scalar_tensor_tensor(co[:], ang[:], -1.0, ang[:], ALU.mult, ALU.max))
                dve.tensor_scalar(co[:], co[:], -1.0, float(np.pi / 2), ALU.mult, ALU.add).then_inc(ready, 1)
                dve.wait_ge(waves, 2)
                ch.step(dve.tensor_copy(cos_sin[:], both[:, :, 0:64].rearrange("p a (i r) -> p a i r", r=ROPE)))
                ch.step(dve.tensor_copy(rotor[:], both[:, :, 64:N]))


def s5(k, uT, rows, mixT, rotor, lam, mag):
    nc, ap = k.nc, k.ap
    G = HALF_G
    NQ = GROUPS // 4
    with ExitStack() as ctx:
        sbt = lambda n, shape: k.sb("s5_" + n, shape, ctx=ctx)
        cc = sbt("c", [P, 2, GROUPS, GH])
        bb = sbt("b", [P, 2, GROUPS, GH])
        coef = sbt("coef", [P, 6, GROUPS])
        pw = sbt("pw", [P, 2, CH + 1, GROUPS])
        sg = sbt("sg", [P, 4, CH + 1, GROUPS])
        wbuf = sbt("wbuf", [P, G, 16, GH])
        vrev = sbt("vrev", [P, G, CH, GH])
        tmp_w = sbt("tmp_w", [P, (CH + 1) * G * GH])
        rot = sbt("rot", [P, 2, 7, GROUPS])
        tr = sbt("tr", [P, 2, G, CHUNKS])
        tmp_t = sbt("tmp_t", [P, G, CHUNKS // 2])
        bpad = sbt("bpad", [P, 4, 15, GH])
        m3 = sbt("m3", [P, 2, 4, P])
        m1 = sbt("m1", [P, 4, P])
        z = sbt("z", [P, 4, CHUNKS])
        zt = sbt("zt", [P, 4, CHUNKS])
        st = sbt("st", [P, 4, CHUNKS + 1])
        dcol = sbt("dcol", [P, GROUPS])
        bcol = sbt("bcol", [P, GROUPS])
        b_in = tmp_w[:, 0:1024].rearrange("p (a g h) -> p a g h", a=2, h=GH)
        tmp_b = tmp_w[:, 1024:1536].rearrange("p (g h) -> p g h", h=GH)
        c_in = tmp_t[:].rearrange("p g c -> p (g c)").rearrange("p (a t u n) -> p a t u n", a=2, t=4, u=2)
        glu = rows.rearrange("p g j h -> p g (j h)")
        out_rows = rows.rearrange("p g j h -> p (g j h)").rearrange("c (j n) -> c j n", j=CH)
        gate = sbt("gate", [P, 2, 4, CHUNKS])
        bank = [k.ps(f"s5_ps{i}", [P, 512], ctx=ctx) for i in range(8)]
        loaded, glu_clear, glu_in, c_turned, chain = (k.sem(f"s5_{n}") for n in
                                                      ("loaded", "glu_clear", "glu_in", "c_turned", "chain"))
        ready, m3_turned, m3_back, m1_done, m1_back = (k.sem(f"s5_{n}") for n in
                                                       ("ready", "m3_turned", "m3_back", "m1_done", "m1_back"))
        w_done, z_done, swapped, s_done, y_done, y_read = (k.sem(f"s5_{n}") for n in
                                                           ("w_done", "z_done", "swapped", "s_done", "y_done", "y_read"))
        gelu_done, glu_done, biased, sig_done, gated_done = (k.sem(f"s5_{n}") for n in
                                                             ("gelu", "glu_done", "biased", "sig", "gated"))
        y_turned, y_rows, mix_turned, mix_a, mix_v = (k.sem(f"s5_{n}") for n in
                                                      ("y_turned", "y_rows", "mix_turned", "mix_a", "mix_v"))

        with nc.Block() as block:

            @block.sync
            def _(sp):
                with nc.allow_non_contiguous_dma(reason="small tables of the S5 heads"):
                    for half in range(2):
                        for i, n in enumerate(("s5_b_re", "s5_b_im")):
                            sp.dma_start(b_in[half * NS:(half + 1) * NS, i], ap[n][0].rearrange("g p h -> p g h")
                                         ).then_inc(loaded, 16)
                        for i, n in enumerate(("s5_c_re", "s5_c_im")):
                            sp.dma_start(c_in[:, i, :, half, :], ap[n][0].rearrange("(t g) h p -> (g h) t p", t=4)
                                         ).then_inc(loaded, 16)
                    for j in range(CH):
                        sp.dma_start(dcol[j * GH:(j + 1) * GH, :], ap["s5_d"][0].rearrange("g h -> h g")).then_inc(loaded, 16)
                        sp.dma_start(bcol[j * GH:(j + 1) * GH, :], ap["s5_glu_b"][0].rearrange("g h -> h g")
                                     ).then_inc(loaded, 16)
                    sp.wait_ge(glu_clear, 1)
                    for j in range(CH):
                        sp.dma_start(glu[j * GH:(j + 1) * GH, :, j * GH:(j + 1) * GH],
                                     ap["s5_glu_w"][0].rearrange("g h e -> h g e")).then_inc(glu_in, 16)

            @block.gpsimd
            def _(pool):
                pool.memset(glu, 0.0).then_inc(glu_clear, 1)

            @block.tensor
            def _(pe):
                ident = k.c("ident")
                pe.wait_ge(loaded, 24 * 16)
                for i in range(2):
                    for t in range(4):
                        mm = pe.transpose(bank[i][:, t * P:(t + 1) * P], c_in[:, i, t].rearrange("q a p -> q (a p)"), ident)
                mm.then_inc(c_turned, 1)
                for q in range(NQ):
                    gs = [4 * (q % 4) + g for g in range(4)]
                    pe.wait_ge(ready, q + 1)
                    if q:
                        pe.wait_ge(m3_back, q)
                        pe.wait_ge(m1_back, q)
                    for g in range(4):
                        mm = pe.transpose(bank[0][:, g * P:(g + 1) * P], vrev[:, gs[g]].rearrange("p j h -> p (j h)"), ident)
                    mm.then_inc(m3_turned, 1)
                    for g in range(4):
                        bp = bpad[:, g].rearrange("p j h -> p (j h)")
                        wb = wbuf[:, gs[g]].rearrange("p j h -> p (j h)")
                        for j in range(CH):
                            mm = pe.matmul(bank[1][:, g * P:(g + 1) * P], bp[:, (7 - j) * GH:(7 - j) * GH + P],
                                           wb[:, (7 - j) * GH:(7 - j) * GH + P], start=(j == 0), stop=(j == CH - 1))
                    mm.then_inc(m1_done, 1)
                    pe.wait_ge(m3_back, q + 1)
                    if q:
                        pe.wait_ge(z_done, q)
                    for v in range(2):
                        for g in range(4):
                            mm = pe.matmul(bank[2 + v][:, g * P:(g + 1) * P], m3[:, v, g, :], uT[:, 4 * q + g, :],
                                           start=True, stop=True)
                    mm.then_inc(w_done, 1)
                    pe.wait_ge(z_done, q + 1)
                    if q:
                        pe.wait_ge(s_done, q)
                    pe.matmul(bank[4][:], k.c("swap"), z[:].rearrange("p g c -> p (g c)"), start=True,
                              stop=True).then_inc(swapped, 1)
                    pe.wait_ge(s_done, q + 1)
                    pe.wait_ge(m1_back, q + 1)
                    if q:
                        pe.wait_ge(y_read, q)
                    for g in range(4):
                        out = bank[5][:, g * P:(g + 1) * P]
                        pe.matmul(out, m1[:, g, :], uT[:, 4 * q + g, :], start=True, stop=False)
                        mm = pe.matmul(out, wbuf[:, gs[g], 8:16].rearrange("p j h -> p (j h)"), st[:, g, 0:CHUNKS],
                                       start=False, stop=True)
                    mm.then_inc(y_done, 1)
                pe.wait_ge(gelu_done, NQ)
                pe.wait_ge(glu_in, 16 * CH)
                for q in range(NQ):
                    if q >= 2:
                        pe.wait_ge(biased, q - 1)
                    for g in range(4):
                        mm = pe.matmul(bank[6 + q % 2][:, g * P:(g + 1) * P], glu[:, 4 * q + g, :], uT[:, 4 * q + g, :],
                                       start=True, stop=True)
                    mm.then_inc(glu_done, 1)
                for q in range(NQ):
                    pe.wait_ge(gated_done, q + 1)
                    if q >= 2:
                        pe.wait_ge(y_rows, q - 1)
                    for g in range(4):
                        mm = pe.transpose(bank[q % 2][:, g * P:(g + 1) * P], uT[:, 4 * q + g, :], ident)
                    mm.then_inc(y_turned, 1)
                pe.wait_ge(y_rows, NQ)
                for t in range(4):
                    if t:
                        pe.wait_ge(mix_a, t)
                        pe.wait_ge(mix_v, t)
                    for j in range(CH):
                        mm = pe.transpose(bank[2 + j // 4][:, (j % 4) * P:(j % 4 + 1) * P], out_rows[:, j, t * P:(t + 1) * P], ident)
                    mm.then_inc(mix_turned, 1)

            @block.scalar
            def _(act):
                for q in range(NQ):
                    act.wait_ge(m1_done, q + 1)
                    if q:
                        act.wait_ge(y_done, q)
                    act.copy(m1[:].rearrange("p g n -> p (g n)"), bank[1][:]).then_inc(m1_back, 1)
                    act.wait_ge(y_read, q + 1)
                    part = uT[:, 4 * q:4 * q + 4, :]
                    act.activation(part, part, ACT.Gelu_apprx_tanh).then_inc(gelu_done, 1)
                for q in range(NQ):
                    act.wait_ge(biased, q + 1)
                    act.activation(gate[:, q % 2], gate[:, q % 2], ACT.Sigmoid).then_inc(sig_done, 1)
                for q in range(NQ):
                    act.wait_ge(y_turned, q + 1)
                    act.copy(out_rows[:, :, 4 * q * GH:4 * (q + 1) * GH].rearrange("c j (g h) -> c g j h", g=4),
                             bank[q % 2][:].rearrange("c (g j h) -> c g j h", g=4, j=CH)).then_inc(y_rows, 1)
                for t in range(4):
                    act.wait_ge(mix_turned, t + 1)
                    act.copy(mixT[:, t, :].rearrange("p (c j) -> p j c", j=CH)[:, 0:4, :],
                             bank[2][:].rearrange("p (j c) -> p j c", j=4)).then_inc(mix_a, 1)

            @block.vector
            def _(dve):
                ch = Chain(dve, chain)
                tt, ts, stt = dve.tensor_tensor, dve.tensor_scalar, dve.scalar_tensor_tensor
                T, B = slice(0, NS), slice(NS, P)

                def cmul(out_r, out_i, a_r, a_i, b_r, b_i, t):
                    ch.step(tt(out_r, a_r, b_r, ALU.mult))
                    ch.step(tt(t, a_i, b_i, ALU.mult))
                    ch.step(tt(out_r, out_r, t, ALU.subtract))
                    ch.step(tt(out_i, a_r, b_i, ALU.mult))
                    ch.step(tt(t, a_i, b_r, ALU.mult))
                    ch.step(tt(out_i, out_i, t, ALU.add))

                c6 = lambda i: coef[:, i, :]
                ch.step(dve.memset(pw[:, 0, 0, :], 1.0))
                ch.step(dve.memset(pw[:, 1, 0, :], 0.0))
                ch.step(tt(pw[:, 0, 1, :], mag[:, 0, :], rotor[:, 0, :], ALU.mult))
                ch.step(tt(pw[:, 1, 1, :], mag[:, 0, :], rotor[:, 1, :], ALU.mult))
                for j in range(2, CH + 1):
                    cmul(pw[:, 0, j, :], pw[:, 1, j, :], pw[:, 0, j - 1, :], pw[:, 1, j - 1, :], pw[:, 0, 1, :],
                         pw[:, 1, 1, :], c6(0))
                nr, ni, lr, li = c6(1), pw[:, 1, 1, :], lam[:, 0, :], lam[:, 1, :]
                ch.step(ts(nr, pw[:, 0, 1, :], -1.0, None, ALU.add))
                ch.step(tt(c6(0), lr, lr, ALU.mult))
                ch.step(tt(c6(2), li, li, ALU.mult))
                ch.step(tt(c6(0), c6(0), c6(2), ALU.add))
                ch.step(dve.reciprocal(c6(5), c6(0)))
                ch.step(tt(c6(2), nr, lr, ALU.mult))
                ch.step(tt(c6(0), ni, li, ALU.mult))
                ch.step(tt(c6(2), c6(2), c6(0), ALU.add))
                ch.step(tt(c6(2), c6(2), c6(5), ALU.mult))
                ch.step(tt(c6(3), ni, lr, ALU.mult))
                ch.step(tt(c6(0), nr, li, ALU.mult))
                ch.step(tt(c6(3), c6(3), c6(0), ALU.subtract))
                ch.step(tt(c6(3), c6(3), c6(5), ALU.mult))
                dve.wait_ge(loaded, 24 * 16)
                wide = lambda a: a.unsqueeze(2).broadcast_to([P, GROUPS, GH])
                cmul(bb[:, 0], bb[:, 1], b_in[:, 0], b_in[:, 1], wide(c6(2)), wide(c6(3)), tmp_b)
                dve.wait_ge(c_turned, 1)
                for i in range(2):
                    ch.step(dve.tensor_copy(cc[:, i].rearrange("p g h -> p (g h)"), bank[i][:]))
                for half, real, imag in ((T, 0, 1), (B, 1, 0)):
                    a_r, a_i = pw[half, 0], pw[half, 1]
                    top = half is T
                    ch.step(dve.tensor_copy(sg[half, 0], a_r if top else a_i))
                    ch.step(ts(sg[half, 1], a_i if top else a_r, -1.0 if top else 1.0, None, ALU.mult))
                    ch.step(ts(sg[half, 2], a_r if top else a_i, 1.0 if top else -1.0, None, ALU.mult))
                    ch.step(ts(sg[half, 3], a_i if top else a_r, -1.0, None, ALU.mult))
                dst = (c6(0), c6(1))
                cmul(dst[0], dst[1], rotor[:, 0, :], rotor[:, 1, :], rotor[:, 0, :], rotor[:, 1, :], c6(4))
                cmul(c6(2), c6(3), c6(0), c6(1), c6(0), c6(1), c6(4))
                cmul(rot[:, 0, 0, :], rot[:, 1, 0, :], c6(2), c6(3), c6(2), c6(3), c6(4))
                for l in range(1, 7):
                    cmul(rot[:, 0, l, :], rot[:, 1, l, :], rot[:, 0, l - 1, :], rot[:, 1, l - 1, :],
                         rot[:, 0, l - 1, :], rot[:, 1, l - 1, :], c6(4))
                ch.step(dve.memset(wbuf[:, :, 0:7, :], 0.0))
                ch.step(dve.memset(bpad[:], 0.0))
                ch.step(dve.memset(st[:, :, 0:1], 0.0))

                def half_tables(hf):
                    gsl = slice(hf * G, (hf + 1) * G)
                    def power(i, j0, j1):
                        return sg[:, i, j0:j1, gsl].unsqueeze(3).broadcast_to([P, j1 - j0, G, GH])
                    def val(t, i, n):
                        return t[:, i, gsl, :].unsqueeze(1).broadcast_to([P, n, G, GH])
                    t9 = tmp_w[:].rearrange("p (j g h) -> p j g h", j=CH + 1, g=G)
                    wv = wbuf[:, :, 7:16, :].rearrange("p g j h -> p j g h")
                    for j in range(CH + 1):
                        sel = slice(j, j + 1)
                        one = lambda t, i: t[:, i, gsl, :]
                        pj = lambda i: sg[:, i, j, gsl].unsqueeze(2).broadcast_to([P, G, GH])
                        dve.tensor_tensor(wbuf[:, :, 7 + j, :], one(cc, 0), pj(2), ALU.mult)
                        ins = dve.tensor_tensor(t9[:, j], one(cc, 1), pj(3), ALU.mult)
                    ch.step(ins)
                    for j in range(CH + 1):
                        ins = dve.tensor_tensor(wbuf[:, :, 7 + j, :], wbuf[:, :, 7 + j, :], t9[:, j], ALU.add)
                    ch.step(ins)
                    for j in range(CH):
                        one = lambda t, i: t[:, i, gsl, :]
                        pj = lambda i: sg[:, i, j, gsl].unsqueeze(2).broadcast_to([P, G, GH])
                        dve.tensor_tensor(vrev[:, :, 7 - j, :], one(bb, 0), pj(0), ALU.mult)
                        ins = dve.tensor_tensor(t9[:, j], one(bb, 1), pj(1), ALU.mult)
                    ch.step(ins)
                    for j in range(CH):
                        ins = dve.tensor_tensor(vrev[:, :, 7 - j, :], vrev[:, :, 7 - j, :], t9[:, j], ALU.add)
                    ch.step(ins)
                    ch.step(dve.memset(tr[:, 0, :, 0:1], 1.0))
                    ch.step(dve.memset(tr[:, 1, :, 0:1], 0.0))
                    for l in range(7):
                        n = 1 << l
                        r = lambda i: rot[:, i, l, gsl].unsqueeze(2).broadcast_to([P, G, n])
                        cmul(tr[:, 0, :, n:2 * n], tr[:, 1, :, n:2 * n], tr[:, 0, :, 0:n], tr[:, 1, :, 0:n], r(0), r(1),
                             tmp_t[:, :, 0:n])
                    ch.step(ts(tr[B, 1], tr[B, 1], -1.0, None, ALU.mult))

                for q in range(NQ):
                    if q % 4 == 0:
                        if q:
                            dve.wait_ge(y_done, q)
                        half_tables(q // 4)
                    gl = slice(4 * (q % 4), 4 * (q % 4) + 4)
                    gg = slice(4 * q, 4 * q + 4)
                    if q:
                        dve.wait_ge(m1_done, q)
                    dve.tensor_copy(bpad[:, :, 7, :], vrev[:, gl, 7, :]).then_inc(ready, 1)
                    dve.wait_ge(m3_turned, q + 1)
                    if q:
                        dve.wait_ge(w_done, q)
                    src = bank[0][:].rearrange("p (g n) -> p g n", g=4)
                    dve.tensor_copy(m3[:, 0], src)
                    dve.tensor_copy(m3[:, 1, :, 0:NS], src[:, :, NS:P])
                    dve.tensor_copy(m3[:, 1, :, NS:P], src[:, :, 0:NS]).then_inc(m3_back, 1)
                    dve.wait_ge(w_done, q + 1)
                    four = lambda b: bank[b][:].rearrange("p (g c) -> p g c", g=4)
                    if q:
                        dve.wait_ge(swapped, q)
                    ch.step(tt(z[:], four(2), tr[:, 0, gl], ALU.mult))
                    ch.step(tt(zt[:], four(3), tr[:, 1, gl], ALU.mult))
                    ch.step(tt(zt[:], z[:], zt[:], ALU.add))
                    for g in range(4):
                        ins = dve.tensor_tensor_scan(z[:, g, :], mag[:, 1, 4 * q + g:4 * q + g + 1].broadcast_to([P, CHUNKS]),
                                                     zt[:, g, :], 0.0, ALU.mult, ALU.add)
                    ins.then_inc(z_done, 1)
                    dve.wait_ge(swapped, q + 1)
                    ch.step(tt(zt[:], four(4), tr[:, 1, gl], ALU.mult))
                    if q:
                        dve.wait_ge(y_done, q)
                    ch.step(tt(st[:, :, 1:CHUNKS + 1], z[:], tr[:, 0, gl], ALU.mult))
                    tt(st[:, :, 1:CHUNKS + 1], st[:, :, 1:CHUNKS + 1], zt[:], ALU.subtract).then_inc(s_done, 1)
                    dve.wait_ge(y_done, q + 1)
                    ch.step(tt(uT[:, gg, :], uT[:, gg, :], dcol[:, gg].unsqueeze(2).broadcast_to([P, 4, CHUNKS]), ALU.mult))
                    tt(uT[:, gg, :], uT[:, gg, :], four(5), ALU.add).then_inc(y_read, 1)
                for q in range(NQ + 1):
                    if q < NQ:
                        dve.wait_ge(glu_done, q + 1)
                        if q >= 2:
                            dve.wait_ge(gated_done, q - 1)
                        tt(gate[:, q % 2], bank[6 + q % 2][:].rearrange("p (g c) -> p g c", g=4),
                           bcol[:, 4 * q:4 * q + 4].unsqueeze(2).broadcast_to([P, 4, CHUNKS]), ALU.add).then_inc(biased, 1)
                    if q:
                        dve.wait_ge(sig_done, q)
                        part = uT[:, 4 * q - 4:4 * q, :]
                        tt(part, part, gate[:, (q - 1) % 2], ALU.mult).then_inc(gated_done, 1)
                for t in range(4):
                    dve.wait_ge(mix_turned, t + 1)
                    dve.tensor_copy(mixT[:, t, :].rearrange("p (c j) -> p j c", j=CH)[:, 4:8, :],
                                    bank[3][:].rearrange("p (j c) -> p j c", j=4)).then_inc(mix_v, 1)


def s5_path(k, hT, mixT):
    with ExitStack() as ctx:
        rotor, lam, mag = (k.sb(n, [P, 2, GROUPS], ctx=ctx) for n in ("rotor", "lam", "mag"))
        dt = k.sb("dt", [P, GROUPS], ctx=ctx)
        sine_tables(k, k.cos_sin, rotor, lam, dt, mag)
        u_rows = k.sb("u_rows", [P, GROUPS, CH, GH], ctx=ctx)
        uT = k.sb("uT", [P, GROUPS, CHUNKS], ctx=ctx)
        project_u(k, hT, u_rows, uT)
        s5(k, uT, u_rows[:], mixT, rotor, lam, mag)


NORMED = HEADS * HD + HD
AT_V, AT_QI, AT_KI, AT_WI = NORMED, NORMED + HD, NORMED + HD + HEADS * HD, NORMED + 2 * HD + HEADS * HD


def project_rest(k, hT, qT, kT, v_rows, w_rows):
    nc, ap = k.nc, k.ap
    widths = (512, 512, QKV - 1024)
    with ExitStack() as ctx:
        w = k.sb("p_w", [P, KS, QKV], ctx=ctx)
        gains = k.sb("p_gains", [P, NORMED], ctx=ctx)
        line = [k.sb(f"p_line{i}", [P, REST], ctx=ctx) for i in range(2)]
        square = k.sb("p_square", [P, NORMED], ctx=ctx)
        stat = k.sb("p_stat", [P, 3, HEADS + 1], ctx=ctx)
        turn = k.sb("p_turn", [P, 4, 2, HEADS + 1, ROPE], ctx=ctx)
        ps = [k.ps(f"p_ps{i}", [P, 512], ctx=ctx) for i in range(3)]
        ps_t = [k.ps(f"p_ps_t{i}", [P, 512], ctx=ctx) for i in range(3)]
        w_in, gains_in, done, line_a, line_v = (k.sem(f"p_{n}") for n in ("w_in", "gains_in", "done", "line_a", "line_v"))
        squared, mean_done, root_done, line_done = (k.sem(f"p_{n}") for n in ("squared", "mean", "root", "line_done"))
        turned, back_a, back_v, chain = (k.sem(f"p_{n}") for n in ("turned", "back_a", "back_v", "chain"))
        with nc.Block() as block:

            @block.sync
            def _(sp):
                sp.dma_start(w[:], ap["hyb_w_in"][0][:, 512:512 + QKV].rearrange("(p s) n -> p s n", s=KS)).then_inc(w_in, 16)
                for h in range(HEADS):
                    sp.dma_start(gains[:, h * HD:(h + 1) * HD], spread(ap["attn_q_norm_g"][0])).then_inc(gains_in, 16)
                sp.dma_start(gains[:, HEADS * HD:], spread(ap["attn_k_norm_g"][0])).then_inc(gains_in, 16)

            @block.tensor
            def _(pe):
                pe.wait_ge(w_in, 16)

                def turn_line(i):
                    pe.wait_ge(line_done, i + 1)
                    if i:
                        pe.wait_ge(back_a, i)
                        pe.wait_ge(back_v, i)
                    src = line[i % 2]
                    for b in range(2):
                        for j in range(4):
                            pe.transpose(ps_t[b][:, j * P:(j + 1) * P], src[:, b * 640 + j * P:b * 640 + (j + 1) * P],
                                         k.c("ident"))
                        mm = pe.transpose(ps_t[2][:, b * P:(b + 1) * P], src[:, b * 640 + 512:b * 640 + 640], k.c("ident"))
                    mm.then_inc(turned, 1)

                for i in range(TILES):
                    if i:
                        pe.wait_ge(line_a, i)
                        pe.wait_ge(line_v, i)
                    for n, width in enumerate(widths):
                        for s in range(KS):
                            mm = pe.matmul(ps[n][:, 0:width], hT[:, s, i * P:(i + 1) * P],
                                           w[:, s, 512 * n:512 * n + width], start=(s == 0), stop=(s == KS - 1))
                    mm.then_inc(done, 1)
                    if i:
                        turn_line(i - 1)
                turn_line(TILES - 1)

            @block.scalar
            def _(act):
                def back(i):
                    act.wait_ge(turned, i + 1)
                    act.copy(qT[:, 0, :, i * P:(i + 1) * P], ps_t[0][:].rearrange("p (j t) -> p j t", j=4))
                    act.copy(kT[:, :, i * P:(i + 1) * P], ps_t[2][:, 0:2 * P].rearrange("p (j t) -> p j t", j=2)
                             ).then_inc(back_a, 1)

                for i in range(TILES):
                    act.wait_ge(done, i + 1)
                    if i >= 2:
                        act.wait_ge(turned, i - 1)
                    act.copy(line[i % 2][:, 0:512], ps[0][:])
                    act.copy(line[i % 2][:, 512:1024], ps[1][:]).then_inc(line_a, 1)
                    act.wait_ge(line_a, i + 1)
                    if i:
                        act.wait_ge(mean_done, i)
                    act.activation(square[:], line[i % 2][:, 0:NORMED], ACT.Square).then_inc(squared, 1)
                    act.wait_ge(mean_done, i + 1)
                    act.activation(stat[:, 2, :], stat[:, 1, :], ACT.Sqrt).then_inc(root_done, 1)
                    if i:
                        back(i - 1)
                back(TILES - 1)

            @block.vector
            def _(dve):
                ch = Chain(dve, chain)
                tt = dve.tensor_tensor

                def back(i):
                    dve.wait_ge(turned, i + 1)
                    dve.tensor_copy(qT[:, 1, :, i * P:(i + 1) * P], ps_t[1][:].rearrange("p (j t) -> p j t", j=4)
                                    ).then_inc(back_v, 1)

                dve.wait_ge(gains_in, 16 * (HEADS + 1))
                for i in range(TILES):
                    src = line[i % 2]
                    dve.wait_ge(done, i + 1)
                    if i >= 2:
                        dve.wait_ge(turned, i - 1)
                    dve.tensor_copy(src[:, 1024:QKV], ps[2][:, 0:QKV - 1024]).then_inc(line_v, 1)
                    dve.wait_ge(line_v, i + 1)
                    dve.wait_ge(line_a, i + 1)
                    ch.step(dve.tensor_copy(v_rows[:, i, :], src[:, AT_V:AT_V + HD]))
                    ch.step(dve.tensor_scalar(w_rows[:, i, :], src[:, AT_WI:AT_WI + HEADS], float(HEADS) ** -0.5, None,
                                              ALU.mult))
                    dve.wait_ge(squared, i + 1)
                    if i:
                        dve.wait_ge(root_done, i)
                    ch.step(dve.tensor_reduce(stat[:, 0, :], square[:].rearrange("p (h n) -> p h n", n=HD), AX, ALU.add))
                    dve.tensor_scalar(stat[:, 1, :], stat[:, 0, :], 1.0 / HD, EPS, ALU.mult, ALU.add).then_inc(mean_done, 1)
                    dve.wait_ge(root_done, i + 1)
                    ch.step(dve.reciprocal(stat[:, 0, :], stat[:, 2, :]))
                    heads = src[:, 0:NORMED].rearrange("p (h n) -> p h n", n=HD)
                    ch.step(tt(heads, heads, stat[:, 0, :].unsqueeze(2).broadcast_to([P, HEADS + 1, HD]), ALU.mult))
                    ch.step(tt(src[:, 0:NORMED], src[:, 0:NORMED], gains[:], ALU.mult))
                    rot = src[:].rearrange("p (b h n) -> p b h n", b=2, n=HD)[:, :, 0:HEADS + 1, :]
                    wave = lambda a: k.cos_sin[:, a, i, :].unsqueeze(1).unsqueeze(1).broadcast_to([P, 2, HEADS + 1, ROPE])
                    x1, x2 = rot[:, :, :, 0:ROPE], rot[:, :, :, ROPE:2 * ROPE]
                    tt(turn[:, 0], x1, wave(0), ALU.mult)
                    tt(turn[:, 1], x2, wave(1), ALU.mult)
                    tt(turn[:, 2], x1, wave(1), ALU.mult)
                    ch.step(tt(turn[:, 3], x2, wave(0), ALU.mult))
                    tt(x1, turn[:, 0], turn[:, 1], ALU.subtract)
                    ch.step(tt(x2, turn[:, 2], turn[:, 3], ALU.add))
                    dve.tensor_copy(src[:, AT_V:AT_V + HD], src[:, AT_V - HD:AT_V])
                    dve.tensor_copy(src[:, AT_WI:AT_WI + HD], src[:, AT_KI:AT_KI + HD]).then_inc(line_done, 1)
                    if i:
                        back(i - 1)
                back(TILES - 1)


def attention(k, qT, kT, v_rows, w_rows, mixT):
    nc = k.nc
    FREE_TILES = TOPK // P
    jobs = []
    for i in range(TILES):
        if i >= FREE_TILES:
            jobs += [(i, h, True) for h in range(HEADS)]
        jobs += [(i, h, False) for h in range(HEADS)]
    index_of = {j: n for n, j in enumerate([j for j in jobs if j[2]])}
    att_of = {j: n for n, j in enumerate([j for j in jobs if not j[2]])}
    with ExitStack() as ctx:
        relu = [k.sb(f"a_relu{i}", [P, SEQ], ctx=ctx) for i in range(2)]
        total = k.sb("a_total", [P, SEQ], ctx=ctx)
        work = k.sb("a_work", [P, SEQ], ctx=ctx)
        top8 = k.sb("a_top8", [P, 8], ctx=ctx)
        bias = k.sb("a_bias", [P, SEQ], ctx=ctx)
        score = [k.sb(f"a_score{i}", [P, SEQ], ctx=ctx) for i in range(2)]
        prob = [k.sb(f"a_prob{i}", [P, SEQ], ctx=ctx) for i in range(2)]
        probT = [k.sb(f"a_probT{i}", [P, SEQ], ctx=ctx) for i in range(2)]
        stat = k.sb("a_stat", [P, 4, 2], ctx=ctx)
        out = k.sb("a_out", [P, HEADS * HD], ctx=ctx)
        ps_s = [k.ps(f"a_ps_s{i}", [P, 1024], ctx=ctx) for i in range(2)]
        ps_t = k.ps("a_ps_t", [P, 1024], ctx=ctx)
        ps_o = [k.ps(f"a_ps_o{i}", [P, 512], ctx=ctx) for i in range(2)]
        ps_m = ps_o[1]
        index_done, att_done, relu_done, added = (k.sem(f"a_{n}") for n in ("index_done", "att_done", "relu_done", "added"))
        scored, max_done, exp_done, turned, back = (k.sem(f"a_{n}") for n in ("scored", "max", "exp", "turned", "back"))
        inv_done, pv_done, out_done, out_turned, mixed = (k.sem(f"a_{n}") for n in
                                                         ("inv", "pv", "out", "out_turned", "mixed"))
        chain = k.sem("a_chain")
        with nc.Block() as block:

            @block.tensor
            def _(pe):
                def scores(n):
                    i, h, indexer = jobs[n]
                    nk = P * (i + 1)
                    if n >= 2:
                        last = jobs[n - 2]
                        if last[2]:
                            pe.wait_ge(relu_done, index_of[last] + 1)
                        else:
                            pe.wait_ge(scored, att_of[last] + 1)
                    half = slice((h % 2) * HD, (h % 2) * HD + HD)
                    which = 1 if indexer else 0
                    for lo in range(0, nk, 512):
                        hi = min(nk, lo + 512)
                        mm = pe.matmul(ps_s[n % 2][:, lo:hi], qT[half, which, h // 2, i * P:(i + 1) * P],
                                       kT[half, which, lo:hi], start=True, stop=True)
                    mm.then_inc(index_done if indexer else att_done, 1)

                def values(n):
                    a = att_of[jobs[n]]
                    i, h, _ = jobs[n]
                    pe.wait_ge(exp_done, a + 1)
                    if a:
                        pe.wait_ge(back, a)
                    for j in range(i + 1):
                        mm = pe.transpose(ps_t[:, j * P:(j + 1) * P], prob[a % 2][:, j * P:(j + 1) * P], k.c("ident"))
                    mm.then_inc(turned, 1)
                    pe.wait_ge(back, a + 1)
                    if a >= 2:
                        pe.wait_ge(out_done, a - 1)
                    if h == 1 and i:
                        pe.wait_ge(mixed, i)
                    for j in range(i + 1):
                        mm = pe.matmul(ps_o[a % 2][:, 0:HD], probT[a % 2][:, j * P:(j + 1) * P],
                                       v_rows[:, j, :], start=(j == 0), stop=(j == i))
                    mm.then_inc(pv_done, 1)
                    if h == HEADS - 1:
                        pe.wait_ge(out_done, a + 1)
                        for j in range(4):
                            mm = pe.transpose(ps_m[:, j * P:(j + 1) * P], out[:, j * P:(j + 1) * P], k.c("ident"))
                        mm.then_inc(out_turned, 1)

                scores(0)
                for n in range(len(jobs)):
                    if n + 1 < len(jobs):
                        scores(n + 1)
                    if not jobs[n][2]:
                        values(n)

            @block.scalar
            def _(act):
                for n, job in enumerate(jobs):
                    i, h, indexer = job
                    nk = P * (i + 1)
                    if indexer:
                        a = index_of[job]
                        act.wait_ge(index_done, a + 1)
                        if a >= 2:
                            act.wait_ge(added, a - 1)
                        act.activation(relu[a % 2][:, 0:nk], ps_s[n % 2][:, 0:nk], ACT.Relu, scale=float(HD) ** -0.5
                                       ).then_inc(relu_done, 1)
                        continue
                    a = att_of[job]
                    act.wait_ge(max_done, a + 1)
                    if a >= 2:
                        act.wait_ge(turned, a - 1)
                    act.activation(prob[a % 2][:, 0:nk], score[a % 2][:, 0:nk], ACT.Exp, bias=stat[:, 1, a % 2:a % 2 + 1],
                                   accum_out=stat[:, 2, a % 2:a % 2 + 1]).then_inc(exp_done, 1)
                    act.wait_ge(turned, a + 1)
                    if a >= 2:
                        act.wait_ge(pv_done, a - 1)
                    act.copy(probT[a % 2][:, 0:nk], ps_t[:, 0:nk]).then_inc(back, 1)

            @block.vector
            def _(dve):
                ch = Chain(dve, chain)

                def finish(a):
                    i, h = a // HEADS, a % HEADS
                    dve.wait_ge(exp_done, a + 1)
                    dve.reciprocal(stat[:, 3, a % 2:a % 2 + 1], stat[:, 2, a % 2:a % 2 + 1]).then_inc(inv_done, 1)
                    dve.wait_ge(inv_done, a + 1)
                    dve.wait_ge(pv_done, a + 1)
                    if h == 0 and i:
                        dve.wait_ge(out_turned, i)
                    dve.tensor_scalar(out[:, h * HD:(h + 1) * HD], ps_o[a % 2][:, 0:HD],
                                      stat[:, 3, a % 2:a % 2 + 1], None, ALU.mult).then_inc(out_done, 1)
                    if h == HEADS - 1:
                        dve.wait_ge(out_turned, i + 1)
                        dve.tensor_copy(mixT[:, :, i * P:(i + 1) * P], ps_m[:].rearrange("p (j t) -> p j t", j=4)
                                        ).then_inc(mixed, 1)

                for i in range(TILES):
                    nk = P * (i + 1)
                    own = slice(i * P, nk)
                    if i < FREE_TILES:
                        if i:
                            ch.step(dve.memset(bias[:, 0:i * P], 0.0))
                        ch.step(dve.tensor_scalar(bias[:, own], k.c("causal"), 8.0, None, ALU.mult))
                    else:
                        for h in range(HEADS):
                            a = index_of[(i, h, True)]
                            dve.wait_ge(relu_done, a + 1)
                            w = w_rows[:, i, h:h + 1]
                            if h == 0:
                                ins = dve.tensor_scalar(total[:, 0:nk], relu[a % 2][:, 0:nk], w, None, ALU.mult)
                            else:
                                ins = dve.scalar_tensor_tensor(total[:, 0:nk], relu[a % 2][:, 0:nk], w, total[:, 0:nk],
                                                               ALU.mult, ALU.add)
                            ins.then_inc(added, 1)
                            dve.wait_ge(added, a + 1)
                        ch.step(dve.tensor_tensor(total[:, own], total[:, own], k.c("causal"), ALU.add))
                        src = total
                        for _ in range(TOPK // 8):
                            ch.step(dve.max(top8[:], src[:, 0:nk]))
                            ch.step(dve.match_replace(work[:, 0:nk], top8[:], src[:, 0:nk], -3e38))
                            src = work
                        ch.step(dve.tensor_scalar(bias[:, 0:nk], work[:, 0:nk], -2e38, 8.0 * NEG, ALU.is_gt, ALU.mult))
                    for h in range(HEADS):
                        a = att_of[(i, h, False)]
                        n = jobs.index((i, h, False))
                        dve.wait_ge(att_done, a + 1)
                        if a >= 2:
                            dve.wait_ge(exp_done, a - 1)
                        dve.tensor_tensor_reduce(score[a % 2][:, 0:nk], ps_s[n % 2][:, 0:nk], bias[:, 0:nk],
                                                 float(HD) ** -0.5, -3e38, ALU.add, ALU.max, stat[:, 0, a % 2:a % 2 + 1]
                                                 ).then_inc(scored, 1)
                        dve.wait_ge(scored, a + 1)
                        dve.tensor_scalar(stat[:, 1, a % 2:a % 2 + 1], stat[:, 0, a % 2:a % 2 + 1], -1.0, None, ALU.mult
                                          ).then_inc(max_done, 1)
                        if h:
                            finish(a - 1)
                    finish(a)


def hybrid_out(k, mix_ssm, mix_att):
    nc, ap = k.nc, k.ap
    with ExitStack() as ctx:
        w = k.sb("o_w", [P, KS, D], ctx=ctx)
        gate = k.sb("o_gate", [P, D], ctx=ctx)
        part = k.sb("o_part", [P, 2, D], ctx=ctx)
        ps = [k.ps(f"o_ps{i}", [P, 1024], ctx=ctx) for i in range(2)]
        w_in, done, gated_done, x_done = (k.sem(f"o_{n}") for n in ("w_in", "done", "gated", "x_done"))
        with nc.Block() as block:

            @block.sync
            def _(sp):
                sp.dma_start(w[:], ap["hyb_w_out"][0].rearrange("(s p) n -> p s n", p=P)).then_inc(w_in, 16)
                sp.dma_start(gate[:], spread(k.mod[0, 2])).then_inc(w_in, 16)

            @block.tensor
            def _(pe):
                pe.wait_ge(w_in, 32)
                for i in range(TILES):
                    if i >= 2:
                        pe.wait_ge(gated_done, i - 1)
                    for n in range(2):
                        for s in range(KS):
                            mix = mix_ssm if s < 4 else mix_att
                            mm = pe.matmul(ps[i % 2][:, n * 512:(n + 1) * 512], mix[:, s % 4, i * P:(i + 1) * P],
                                           w[:, s, n * 512:(n + 1) * 512], start=(s == 0), stop=(s == KS - 1))
                    mm.then_inc(done, 1)

            @block.vector
            def _(dve):
                dve.wait_ge(w_in, 32)
                for i in range(TILES):
                    dve.wait_ge(done, i + 1)
                    dve.tensor_tensor(part[:, i % 2], ps[i % 2][:], gate[:], ALU.mult).then_inc(gated_done, 1)
                    dve.wait_ge(gated_done, i + 1)
                    dve.tensor_tensor(k.x[:, i, :], k.x[:, i, :], part[:, i % 2], ALU.add).then_inc(x_done, 1)


def pool_mixer(k, h):
    nc, ap = k.nc, k.ap
    NW = len(WINDOWS)
    with ExitStack() as ctx:
        band = k.sb("l_band", [P, NW, 3, P], ctx=ctx)
        w = k.sb("l_w", [P, NW, 2, PG], ctx=ctx)
        gate = k.sb("l_gate", [P, D], ctx=ctx)
        scale = k.sb("l_scale", [P, D], ctx=ctx)
        pooled = [k.sb(f"l_pooled{i}", [P, KS, P], ctx=ctx) for i in range(2)]
        part = k.sb("l_part", [P, 2, D], ctx=ctx)
        ps_p = [k.ps(f"l_ps_p{i}", [P, 512], ctx=ctx) for i in range(2)]
        ps_y = [k.ps(f"l_ps_y{i}", [P, 1024], ctx=ctx) for i in range(2)]
        loaded, scaled, pool_done, pool_a, pool_v = (k.sem(f"l_{n}") for n in
                                                     ("loaded", "scaled", "pool_done", "pool_a", "pool_v"))
        done, gated_done, x_done = (k.sem(f"l_{n}") for n in ("done", "gated", "x_done"))
        with nc.Block() as block:

            @block.sync
            def _(sp):
                sp.dma_start(band[:].rearrange("p a b c -> p (a b c)"), ap["band"]).then_inc(loaded, 16)
                sp.dma_start(w[:].rearrange("p g c n -> p (g c) n"),
                             ap["pool_w"][0].rearrange("g (c p) n -> p (g c) n", p=P)).then_inc(loaded, 16)
                sp.dma_start(gate[:], spread(k.mod[2, 2])).then_inc(loaded, 16)
                sp.dma_start(scale[:], spread(ap["pool_scale"][0])).then_inc(loaded, 16)

            @block.tensor
            def _(pe):
                pe.wait_ge(loaded, 64)

                def pool(i):
                    if i:
                        pe.wait_ge(pool_a, i)
                        pe.wait_ge(pool_v, i)
                    for s in range(KS):
                        out = ps_p[s // 4][:, (s % 4) * P:(s % 4 + 1) * P]
                        cols = slice(s * P, (s + 1) * P)
                        mm = pe.matmul(out, h[:, i, cols], band[:, s // 2, 1 if i else 0, :], start=True, stop=(i == 0))
                        if i:
                            mm = pe.matmul(out, h[:, i - 1, cols], band[:, s // 2, 2, :], start=False, stop=True)
                    mm.then_inc(pool_done, 1)

                pool(0)
                for i in range(TILES):
                    pe.wait_ge(pool_a, i + 1)
                    pe.wait_ge(pool_v, i + 1)
                    if i + 1 < TILES:
                        pool(i + 1)
                    if i >= 2:
                        pe.wait_ge(gated_done, i - 1)
                    for g in range(NW):
                        for c in range(2):
                            mm = pe.matmul(ps_y[i % 2][:, g * PG:(g + 1) * PG], pooled[i % 2][:, 2 * g + c, :], w[:, g, c, :],
                                           start=(c == 0), stop=(c == 1))
                    mm.then_inc(done, 1)

            @block.scalar
            def _(act):
                for i in range(TILES):
                    act.wait_ge(pool_done, i + 1)
                    if i >= 2:
                        act.wait_ge(done, i - 1)
                    act.copy(pooled[i % 2][:, 0:4, :], ps_p[0][:].rearrange("p (s t) -> p s t", s=4)).then_inc(pool_a, 1)

            @block.vector
            def _(dve):
                dve.wait_ge(loaded, 64)
                dve.tensor_tensor(gate[:], gate[:], scale[:], ALU.mult).then_inc(scaled, 1)
                dve.wait_ge(scaled, 1)

                def pool_back(i):
                    dve.wait_ge(pool_done, i + 1)
                    if i >= 2:
                        dve.wait_ge(done, i - 1)
                    dve.tensor_copy(pooled[i % 2][:, 4:8, :], ps_p[1][:].rearrange("p (s t) -> p s t", s=4)
                                    ).then_inc(pool_v, 1)

                pool_back(0)
                for i in range(TILES):
                    if i + 1 < TILES:
                        pool_back(i + 1)
                    dve.wait_ge(done, i + 1)
                    dve.tensor_tensor(part[:, i % 2], ps_y[i % 2][:], gate[:], ALU.mult).then_inc(gated_done, 1)
                    dve.wait_ge(gated_done, i + 1)
                    dve.tensor_tensor(k.x[:, i, :], k.x[:, i, :], part[:, i % 2], ALU.add).then_inc(x_done, 1)


def hybrid_layer(k):
    with ExitStack() as ctx:
        mix_ssm = k.sb("mix_ssm", [P, 4, SEQ], ctx=ctx)
        rotor, lam, mag = (k.sb(n, [P, 2, GROUPS], ctx=ctx) for n in ("rotor", "lam", "mag"))
        dt = k.sb("dt", [P, GROUPS], ctx=ctx)
        cos_sin = k.cos_sin
        sine_tables(k, cos_sin, rotor, lam, dt, mag)
        uT = k.sb("uT", [P, GROUPS, CHUNKS], ctx=ctx)
        mix_att = uT[:].rearrange("p g c -> p (g c)").rearrange("p (s t) -> p s t", s=4)
        with ExitStack() as inner:
            hT = k.sb("hT", [P, KS, SEQ], ctx=inner)
            normalise(k, 0, None, "n0", True, hT=hT)
            with ExitStack() as sctx:
                u_rows = k.sb("u_rows", [P, GROUPS, CH, GH], ctx=sctx)
                project_u(k, hT, u_rows, uT)
                s5(k, uT, u_rows[:], mix_ssm, rotor, lam, mag)
            v_rows = k.sb("v_rows", [P, TILES, HD], ctx=inner)
            w_rows = k.sb("w_rows", [P, TILES, HEADS], ctx=inner)
            qT = k.sb("qT", [P, 2, 4, SEQ], ctx=inner)
            kT = k.sb("kT", [P, 2, SEQ], ctx=inner)
            project_rest(k, hT, qT, kT, v_rows, w_rows)
            attention(k, qT, kT, v_rows, w_rows, mix_att)
        hybrid_out(k, mix_ssm, mix_att)


def program(nc, ap, out):
    with ExitStack() as ctx:
        k = Core(nc, ctx, ap)
        load_and_modulate(k)
        hybrid_layer(k)
        k.recycle()
        moe(k, 0, 1, "m0")
        k.recycle()
        with ExitStack() as inner:
            h = k.sb("h1", [P, TILES, D], ctx=inner)
            normalise(k, 2, h, "n1", False)
            pool_mixer(k, h)
        moe(k, 1, 3, "m1", out=out[0])


_INS = ["x", "c", "positions", "mix_norm_g", "mix_mod_w", "mix_mod_b", "ffn_norm_g", "ffn_mod_w", "ffn_mod_b",
        "hyb_w_in", "hyb_w_out", "s5_lambda_re", "s5_lambda_im", "s5_log_dt", "s5_b_re", "s5_b_im", "s5_c_re",
        "s5_c_im", "s5_d", "s5_glu_w", "s5_glu_b", "attn_q_norm_g", "attn_k_norm_g", "pool_w", "pool_scale",
        "router_w", "router_bias", "exp_w_gate", "exp_w_up", "exp_w_down", "sh_w_gate", "sh_w_up", "sh_w_down"]


def kernel(**inputs):
    import concourse.bacc as bacc
    from concourse.bass_utils import run_bass_kernel_spmd

    nc = bacc.Bacc("TRN2", target_bir_lowering=False, num_devices=1)
    arrays, ap = {}, {}
    given = {n: np.ascontiguousarray(inputs[n]) for n in _INS}
    for name, a in {**given, "const": CONST, "band": BAND}.items():
        arrays[f"in_{name}"] = a
        ap[name] = nc.dram_tensor(f"in_{name}", a.shape, mybir.dt.from_np(a.dtype), kind="ExternalInput").ap()
    out = nc.dram_tensor("out_x", (1, SEQ, D), F32, kind="ExternalOutput").ap()
    program(nc, ap, out)
    r = run_bass_kernel_spmd(nc, [arrays], core_ids=[0])
    return r.results[0]["out_x"]
```

```python
from contextlib import ExitStack, nullcontext

import numpy as np

import concourse.bass as bass
from concourse import mybir

F32 = mybir.dt.float32
BF16 = mybir.dt.bfloat16
F32R = mybir.dt.float32r
I32 = mybir.dt.int32
U32 = mybir.dt.uint32
ALU = mybir.AluOpType
ACT = mybir.ActivationFunctionType
AX = mybir.AxisListType.X

P = 128
D = 1024
SEQ = 1024
TILES = SEQ // P
KS = D // P
EPS = 1e-6

GROUPS, GH, NS = 32, 16, 64
CH = P // GH
CHUNKS = SEQ // CH
HALF_G = GROUPS // 2

HEADS, HD = 8, 64
TOPK = 256
ROPE = 8
QKV = 1224
REST = 1280

WINDOWS = (2, 4, 8, 16)
PG = D // len(WINDOWS)

E, TK, F = 64, 8, 256
BLOCKS = 128
LOOKED = BLOCKS + 2
SURE = SEQ * TK // P
NEG = -1e30

TWO_PI = 2.0 * np.pi
PI_A = float(np.float32(6.28125))
PI_B = float(np.float32(TWO_PI - 6.28125))
PI_C = float(np.float32(TWO_PI - 6.28125 - float(np.float32(TWO_PI - 6.28125))))


def constants():
    i = np.arange(P)
    parts = {
        "ident": np.eye(P),
        "iota": np.tile(i, (P, 1)),
        "before": (i[:, None] < i[None, :]) * 1.0,
        "causal": np.where(i[None, :] <= i[:, None], 0.0, NEG),
        "swap": np.eye(P)[(i + NS) % P],
        "row": i[:, None] * 1.0,
        "token1": i[:, None] + P * np.arange(TILES)[None, :] + 1.0,
        "padrow": i[:, None] + SEQ + 1.0,
        "tie": np.tile((np.arange(8)[None, :] < np.arange(8)[:, None]).reshape(1, 64) * 1.0, (P, 1)),
        "freq": np.tile(np.power(np.float32(500000.0), -np.arange(0, 16, 2, dtype=np.float32) / 16), (P, 1)),
    }
    at, n, cols = {}, 0, []
    for name, a in parts.items():
        at[name] = (n, n + a.shape[1])
        n += a.shape[1]
        cols.append(a.astype(np.float32))
    return np.ascontiguousarray(np.concatenate(cols, 1)), at


def bands():
    out = np.zeros((P, len(WINDOWS), 3, P), np.float32)
    for w, win in enumerate(WINDOWS):
        for t in range(P):
            for back in range(win):
                s = t - back
                if s >= 0:
                    out[s, w, 0, t] = 1.0 / min(win, t + 1)
                    out[s, w, 1, t] = 1.0 / win
                else:
                    out[s + P, w, 2, t] = 1.0 / win
            out[t, w, 0, t] -= 1.0
            out[t, w, 1, t] -= 1.0
    return out.reshape(P, -1)


CONST, AT = constants()
BAND = bands()


class Chain:

    def __init__(self, eng, sem):
        self.eng, self.sem, self.n = eng, sem, 0

    def step(self, ins):
        self.n += 1
        ins.then_inc(self.sem, 1)
        self.eng.wait_ge(self.sem, self.n)


def bc(ap, shape):
    return ap.to_broadcast(shape)


def spread(row, n=P):
    return row.partition_broadcast(n)


class Core:

    def __init__(self, nc, ctx, ap):
        self.nc, self.ctx, self.ap = nc, ctx, ap
        self.sems = []
        self.x = None
        self.cst = self.sb("cst", [P, CONST.shape[1]])
        self.cos_sin = self.sb("cos_sin", [P, 2, TILES, ROPE])
        self.c_silu = self.sb("c_silu", [P, KS])
        self.ones = self.sb("ones", [P, 1])
        self.mod = nc.dram_tensor("mod_rows", (4, 3, D), F32).ap()
        self.mod_raw = nc.dram_tensor("mod_raw", (3, 3 * D), F32).ap()
        self.x_rows = nc.dram_tensor("x_rows", (SEQ, D), F32).ap()
        self.h_rows = nc.dram_tensor("h_rows", (SEQ + P, D), F32).ap()
        self.moe_acc = [nc.dram_tensor(f"moe_acc{i}", (SEQ + P, D), F32).ap() for i in range(2)]

    def sb(self, name, shape, dt=F32, ctx=None):
        return (ctx or self.ctx).enter_context(self.nc.sbuf_tensor(name, shape, dt))

    def ps(self, name, shape, dt=F32, ctx=None):
        return (ctx or self.ctx).enter_context(self.nc.psum_tensor(name, shape, dt))

    def hold_x(self, ctx, name):
        self.x = self.sb(name, [P, TILES, D], ctx=ctx)

    def sem(self, name):
        self.sems.append(self.nc.alloc_semaphore(name))
        return self.sems[-1]

    def recycle(self):
        self.nc.clear_and_free_semaphores(self.sems)
        self.nc.all_engine_barrier()
        self.sems = []

    def c(self, name):
        a, b = AT[name]
        return self.cst[:, a:b]


MOD_SOURCES = (("mix", 0), ("ffn", 0), ("mix", 1), ("ffn", 1))


def mod_weights(ap, m):
    which, layer = MOD_SOURCES[m]
    return ap[which + "_mod_w"][layer].rearrange("(p k) n -> k p n", k=KS)


def load_and_modulate(k):
    nc, ap = k.nc, k.ap
    RING = 4
    with ExitStack() as ctx:
        c_col = k.sb("c_col", [P, KS], ctx=ctx)
        ring = k.sb("mod_w_ring", [P, RING, 3 * D], ctx=ctx)
        acc = k.sb("mod_acc", [P, 3 * D], ctx=ctx)
        bias = k.sb("mod_bias", [1, 3 * D], ctx=ctx)
        gain = k.sb("mod_gain", [1, D], ctx=ctx)
        row = k.sb("mod_row", [1, 3 * D], ctx=ctx)
        total = [k.ps(f"mod_total{i}", [P, 512], ctx=ctx) for i in range(6)]
        small_in, x_in = k.sem("mod_small_in"), k.sem("x_in")
        w_in = [k.sem(f"mod_w_in{i}") for i in range(RING)]
        silu_done, w_used = k.sem("c_silu_done"), k.sem("mod_w_used")
        summed, row_out = k.sem("mod_summed"), k.sem("mod_row_out")
        row_done, chain = k.sem("mod_row_done"), k.sem("mod_chain")
        with nc.Block() as block:

            @block.sync
            def _(sp):
                sp.dma_start(c_col[:], ap["c"][0].rearrange("(p k) -> p k", k=KS)).then_inc(small_in, 16)
                sp.dma_start(k.cst[:], ap["const"]).then_inc(small_in, 16)
                sp.dma_start(bias[:], ap["mix_mod_b"][0].unsqueeze(0)).then_inc(small_in, 16)
                sp.dma_start(gain[:], ap["mix_norm_g"][0].unsqueeze(0)).then_inc(small_in, 16)
                rows = mod_weights(ap, 0)
                for s in range(KS):
                    if s >= RING:
                        sp.wait_ge(w_used, s - RING + 1)
                    sp.dma_start(ring[:, s % RING, :], rows[s]).then_inc(w_in[s % RING], 16)
                sp.dma_start(k.x[:], ap["x"][0].rearrange("(i p) d -> p i d", p=P)).then_inc(x_in, 16)
                sp.wait_ge(x_in, 16)
                sp.wait_ge(row_out, 16)

            @block.scalar
            def _(act):
                act.wait_ge(small_in, 4 * 16)
                nc.scalar.activation(k.c_silu[:], c_col[:], ACT.Silu).then_inc(silu_done, 1)
                act.wait_ge(row_done, 1)
                act.dma_start(k.mod[0].unsqueeze(0), row[:].rearrange("a (j d) -> a j d", j=3)).then_inc(row_out, 16)

            @block.vector
            def _(dve):
                ch = Chain(dve, chain)
                ch.step(nc.vector.memset(k.ones[:], 1.0))
                dve.wait_ge(silu_done, 1)
                for s in range(KS):
                    dve.wait_ge(w_in[s % RING], 16 * (s // RING + 1))
                    c = k.c_silu[:, s:s + 1]
                    if s == 0:
                        ins = nc.vector.tensor_scalar(acc[:], ring[:, s % RING, :], c, None, ALU.mult)
                    else:
                        dve.wait_ge(w_used, s)
                        ins = nc.vector.scalar_tensor_tensor(acc[:], ring[:, s % RING, :], c, acc[:], ALU.mult, ALU.add)
                    ins.then_inc(w_used, 1)
                dve.wait_ge(summed, 1)
                for i, (src, dst) in enumerate([(0, 1), (1, 0), (2, 2)]):
                    for h in range(2):
                        lo = src * D + h * 512
                        ins = nc.vector.tensor_tensor(row[:, dst * D + h * 512:dst * D + h * 512 + 512],
                                                      total[2 * src + h][0:1, :], bias[:, lo:lo + 512], ALU.add)
                ch.step(ins)
                ch.step(nc.vector.tensor_scalar(row[:, 0:D], row[:, 0:D], 1.0, None, ALU.add))
                nc.vector.tensor_tensor(row[:, 0:D], row[:, 0:D], gain[:], ALU.mult).then_inc(row_done, 1)

            @block.tensor
            def _(pe):
                pe.wait_ge(chain, 1)
                pe.wait_ge(w_used, KS)
                for i in range(6):
                    mm = nc.tensor.matmul(total[i][0:1, :], k.ones[:], acc[:, 512 * i:512 * i + 512],
                                          start=True, stop=True)
                mm.then_inc(summed, 1)


def normalise(k, m, h_out, name, permuted, hT=None, rows_out=False, extra=None):
    nc = k.nc
    with ExitStack() as ctx:
        gain = k.sb(name + "_gain", [P, D], ctx=ctx)
        shift = k.sb(name + "_shift", [P, D], ctx=ctx)
        squares = k.sb(name + "_sq", [P, D], ctx=ctx)
        stat = k.sb(name + "_stat", [P, 3, TILES], ctx=ctx)
        own = None if h_out is not None else k.sb(name + "_h", [P, 2, D], ctx=ctx)
        bank = [k.ps(f"{name}_bank{i}", [P, 512], ctx=ctx) for i in range(4)]
        rows_in, squared = k.sem(name + "_rows_in"), k.sem(name + "_squared")
        mean_done, root_done, inv_done = k.sem(name + "_mean"), k.sem(name + "_root"), k.sem(name + "_inv")
        scaled, h_done = k.sem(name + "_scaled"), k.sem(name + "_h_done")
        turned, copied_a, copied_v = k.sem(name + "_turned"), k.sem(name + "_copied_a"), k.sem(name + "_copied_v")
        stored = [k.sem(f"{name}_stored{i}") for i in range(2)] if rows_out else None

        def h(i):
            return h_out[:, i, :] if h_out is not None else own[:, i % 2, :]

        with nc.Block() as block:

            @block.sync
            def _(sp):
                sp.dma_start(gain[:], spread(k.mod[m, 0])).then_inc(rows_in, 16)
                sp.dma_start(shift[:], spread(k.mod[m, 1])).then_inc(rows_in, 16)
                if rows_out:
                    for i in range(TILES):
                        sp.wait_ge(h_done, i + 1)
                        sp.dma_start(k.h_rows[i * P:(i + 1) * P, :], h(i)).then_inc(stored[i % 2], 16)
                    for sem in stored:
                        sp.wait_ge(sem, 16 * (TILES // 2))
                if extra is not None:
                    extra(sp)

            @block.scalar
            def _(act):
                for i in range(TILES):
                    if i:
                        act.wait_ge(squared, i)
                    nc.scalar.activation(squares[:], k.x[:, i, :], ACT.Square,
                                         accum_out=stat[:, 0, i:i + 1]).then_inc(squared, 1)
                act.wait_ge(mean_done, 1)
                nc.scalar.activation(stat[:, 2, :], stat[:, 1, :], ACT.Sqrt).then_inc(root_done, 1)
                if hT is not None:
                    for i in range(TILES):
                        act.wait_ge(turned, 2 * i + 1)
                        nc.scalar.copy(hT[:, 0:4, i * P:(i + 1) * P],
                                       bank[2 * (i % 2)][:].rearrange("p (s t) -> p s t", s=4)).then_inc(copied_a, 1)

            @block.vector
            def _(dve):
                dve.wait_ge(squared, TILES)
                nc.vector.tensor_scalar(stat[:, 1, :], stat[:, 0, :], 1.0 / D, EPS, ALU.mult,
                                        ALU.add).then_inc(mean_done, 1)
                dve.wait_ge(root_done, 1)
                nc.vector.reciprocal(stat[:, 0, :], stat[:, 2, :]).then_inc(inv_done, 1)
                dve.wait_ge(inv_done, 1)
                dve.wait_ge(rows_in, 32)

                def copy_back(i):
                    dve.wait_ge(turned, 2 * i + 2)
                    nc.vector.tensor_copy(hT[:, 4:8, i * P:(i + 1) * P],
                                          bank[2 * (i % 2) + 1][:].rearrange("p (s t) -> p s t", s=4)).then_inc(copied_v, 1)

                for i in range(TILES):
                    if h_out is None and i >= 2:
                        if hT is not None:
                            dve.wait_ge(turned, 2 * (i - 1))
                        if rows_out:
                            dve.wait_ge(stored[i % 2], 16 * (i // 2))
                    nc.vector.scalar_tensor_tensor(squares[:], k.x[:, i, :], stat[:, 0, i:i + 1], gain[:],
                                                   ALU.mult, ALU.mult).then_inc(scaled, 1)
                    dve.wait_ge(scaled, i + 1)
                    if permuted:
                        out = h(i).rearrange("t (s p) -> t p s", s=KS)
                        a = squares[:].rearrange("t (p s) -> t p s", s=KS)
                        b = shift[:].rearrange("t (p s) -> t p s", s=KS)
                    else:
                        out, a, b = h(i), squares[:], shift[:]
                    nc.vector.tensor_tensor(out, a, b, ALU.add).then_inc(h_done, 1)
                    dve.wait_ge(h_done, i + 1)
                    if hT is not None and i:
                        copy_back(i - 1)
                if hT is not None:
                    copy_back(TILES - 1)

            @block.tensor
            def _(pe):
                if hT is None:
                    return
                for i in range(TILES):
                    pe.wait_ge(h_done, i + 1)
                    if i >= 2:
                        pe.wait_ge(copied_a, i - 1)
                        pe.wait_ge(copied_v, i - 1)
                    for half in range(2):
                        for s in range(4):
                            mm = nc.tensor.transpose(bank[2 * (i % 2) + half][:, s * P:(s + 1) * P],
                                                     h(i)[:, (4 * half + s) * P:(4 * half + s + 1) * P], k.c("ident"))
                        mm.then_inc(turned, 1)


class Routes:

    def __init__(self, k, ctx, name):
        row = lambda n, size=LOOKED: k.sb(f"{name}_{n}", [1, size], I32, ctx=ctx)
        self.token = k.sb(name + "_slot_token", [P, LOOKED], U32, ctx=ctx)
        self.weight = k.sb(name + "_slot_weight", [P, LOOKED], ctx=ctx)
        self.number = row("block_number")
        self.following = row("following")
        self.expert = row("ordinal_expert", P)
        self.count = row("counts", 2)


def route(k, layer, hT, routes, name):
    nc, ap = k.nc, k.ap
    TE = TILES * E
    with ExitStack() as ctx:
        w = k.sb(name + "_w", [P, KS, E], ctx=ctx)
        bias = k.sb(name + "_bias", [P, E], ctx=ctx)
        score, sel, mask = (k.sb(f"{name}_{n}", [P, TE], ctx=ctx) for n in ("score", "sel", "mask"))
        tmp, tmp2 = (k.sb(f"{name}_{n}", [P, TE], ctx=ctx) for n in ("tmp", "tmp2"))
        best2 = k.sb(name + "_best2", [P, TE], ctx=ctx)
        group = k.sb(name + "_group", [P, 64], ctx=ctx)
        rank = k.sb(name + "_rank", [P, 64], ctx=ctx)
        top8 = k.sb(name + "_top8", [P, TILES, TK], ctx=ctx)
        total = k.sb(name + "_total", [P, TILES], ctx=ctx)
        mask16 = k.sb(name + "_mask16", [P, TILES, E], BF16, ctx=ctx)
        seen16 = k.sb(name + "_seen16", [P, TILES + 1, E], BF16, ctx=ctx)
        before16 = k.sb(name + "_before16", [P, P], BF16, ctx=ctx)
        ones16 = k.sb(name + "_ones16", [P, P], BF16, ctx=ctx)
        ones64 = k.sb(name + "_ones64", [P, E], ctx=ctx)
        whole = k.sb(name + "_whole", [P, TE], I32, ctx=ctx)
        nblk, end, start = (k.sb(f"{name}_{n}", [P, E], ctx=ctx) for n in ("nblk", "end", "start"))
        col = k.sb(name + "_col", [P, 2], ctx=ctx)
        holds, held = (k.sb(f"{name}_{n}", [P, E], ctx=ctx) for n in ("holds", "held"))
        line = k.sb(name + "_line", [1, 8, BLOCKS], ctx=ctx)
        line_i = k.sb(name + "_line_i", [1, BLOCKS], I32, ctx=ctx)
        slot_p, slot_b, weight8 = (k.sb(f"{name}_{n}", [P, 64], ctx=ctx) for n in ("slot_p", "slot_b", "weight8"))
        eq = k.sb(name + "_eq", [P, TK, E], ctx=ctx)
        hot_p = k.sb(name + "_hot_p", [P, 2, TK, P], ctx=ctx)
        hot_b = k.sb(name + "_hot_b", [P, 2, TK, 2, P], ctx=ctx)
        blocks = k.sb(name + "_blocks", [P, TK, P], ctx=ctx)
        pad = k.sb(name + "_pad", [P, BLOCKS], ctx=ctx)
        ps_logit = k.ps(name + "_ps_logit", [P, TE], ctx=ctx)
        ps_rank = k.ps(name + "_ps_rank", [P, TE], ctx=ctx)
        ps_count = k.ps(name + "_ps_count", [P, 512], ctx=ctx)
        ps_line = k.ps(name + "_ps_line", [P, 512], ctx=ctx)
        ps_table = k.ps(name + "_ps_table", [P, 512], ctx=ctx)
        w_in, logits, scored = k.sem(name + "_w_in"), k.sem(name + "_logits"), k.sem(name + "_scored")
        masked, ranked, col_done, lined = (k.sem(f"{name}_{n}") for n in ("masked", "ranked", "col", "lined"))
        hot, tabled, chain = k.sem(name + "_hot"), k.sem(name + "_tabled"), k.sem(name + "_chain")

        def grid(t, n=E):
            return t[:].rearrange("p (i e) -> p i e", i=TILES)

        with nc.Block() as block:

            @block.sync
            def _(sp):
                sp.dma_start(w[:], ap["router_w"][layer].rearrange("(p s) e -> p s e", s=KS)).then_inc(w_in, 16)
                sp.dma_start(bias[:], spread(ap["router_bias"][layer])).then_inc(w_in, 16)

            @block.scalar
            def _(act):
                act.wait_ge(logits, 1)
                nc.scalar.activation(score[:], ps_logit[:], ACT.Sigmoid).then_inc(scored, 1)

            @block.tensor
            def _(pe):
                pe.wait_ge(w_in, 32)
                for i in range(TILES):
                    for s in range(KS):
                        mm = nc.tensor.matmul(ps_logit[:, i * E:(i + 1) * E], hT[:, s, i * P:(i + 1) * P], w[:, s, :],
                                              start=(s == 0), stop=(s == KS - 1))
                mm.then_inc(logits, 1)
                pe.wait_ge(masked, 1)
                for i in range(TILES):
                    out = ps_rank[:, i * E:(i + 1) * E]
                    nc.tensor.matmul(out, before16[:], mask16[:, i, :], start=True, stop=False)
                    nc.tensor.matmul(out, ones16[:], seen16[:, i, :], start=False, stop=True)
                nc.tensor.matmul(ps_count[:, 0:E], ones16[:], seen16[:, TILES, :], start=True,
                                 stop=True).then_inc(ranked, 1)
                pe.wait_ge(col_done, 1)
                for n in range(2):
                    mm = nc.tensor.matmul(ps_line[0:1, n * P:(n + 1) * P], col[:, n:n + 1], k.c("ident"), start=True,
                                          stop=True)
                mm.then_inc(lined, 1)
                for i in range(TILES):
                    pe.wait_ge(hot, i + 1)
                    for j in range(TK):
                        mm = nc.tensor.matmul(ps_table[:, 0:2 * P], hot_p[:, i % 2, j, :],
                                              hot_b[:, i % 2, j, :, :].rearrange("p a b -> p (a b)"),
                                              start=(i == 0 and j == 0), stop=(i == TILES - 1 and j == TK - 1))
                    mm.then_inc(tabled, 1)

            @block.vector
            def _(dve):
                v = nc.vector
                ch = Chain(dve, chain)
                ch.step(v.memset(ones16[:], 1.0))
                ch.step(v.memset(ones64[:], 1.0))
                ch.step(v.memset(seen16[:, 0, :], 0.0))
                ch.step(v.tensor_copy(before16[:], k.c("before")))
                dve.wait_ge(w_in, 32)
                dve.wait_ge(scored, 1)
                ch.step(v.tensor_tensor(grid(sel), grid(score), bias[:].unsqueeze(1).broadcast_to([P, TILES, E]), ALU.add))
                for n in range(64):
                    ins = v.max(best2[:, n * 8:n * 8 + 8], sel[:, n * 8:n * 8 + 8])
                ch.step(ins)
                best = best2[:].rearrange("p (n j) -> p n j", j=8)
                ch.step(v.tensor_tensor(group[:].unsqueeze(2), best[:, :, 0:1], best[:, :, 1:2], ALU.add))
                other = group[:].rearrange("p (i g) -> p i g", g=8).unsqueeze(2).broadcast_to([P, 8, 8, 8])
                mine = group[:].rearrange("p (i g) -> p i g", g=8).unsqueeze(3).broadcast_to([P, 8, 8, 8])
                four = lambda t: t[:].rearrange("p (i g h) -> p i g h", g=8, h=8)
                ch.step(v.tensor_tensor(four(tmp), other, mine, ALU.is_gt))
                ch.step(v.tensor_tensor(four(tmp2), other, mine, ALU.is_equal))
                ch.step(v.tensor_tensor(grid(tmp2), grid(tmp2), k.c("tie").unsqueeze(1).broadcast_to([P, TILES, 64]), ALU.mult))
                ch.step(v.tensor_tensor(tmp[:], tmp[:], tmp2[:], ALU.add))
                ch.step(v.tensor_reduce(rank[:], tmp[:].rearrange("p (n j) -> p n j", j=8), AX, ALU.add))
                ch.step(v.tensor_scalar(rank[:], rank[:], 3.5, None, ALU.is_lt))
                wide = rank[:].unsqueeze(2).broadcast_to([P, 64, 8])
                eight = lambda t: t[:].rearrange("p (n j) -> p n j", j=8)
                ch.step(v.tensor_tensor(eight(sel), eight(sel), wide, ALU.mult))
                ch.step(v.tensor_scalar(rank[:], rank[:], -NEG, NEG, ALU.mult, ALU.add))
                ch.step(v.tensor_tensor(eight(sel), eight(sel), wide, ALU.add))
                for i in range(TILES):
                    ins = v.max(top8[:, i, :], sel[:, i * E:(i + 1) * E])
                ch.step(ins)
                for i in range(TILES):
                    ins = v.match_replace(tmp[:, i * E:(i + 1) * E], top8[:, i, :], sel[:, i * E:(i + 1) * E], -3e38)
                ch.step(ins)
                ch.step(v.tensor_scalar(mask[:], tmp[:], -2e38, None, ALU.is_lt))
                ch.step(v.tensor_copy(mask16[:], grid(mask)))
                for i in range(TILES):
                    ins = v.tensor_tensor(seen16[:, i + 1, :], seen16[:, i, :], mask16[:, i, :], ALU.add)
                    if i < TILES - 1:
                        ch.step(ins)
                ins.then_inc(masked, 1)
                ch.step(v.tensor_tensor(score[:], score[:], mask[:], ALU.mult))
                ch.step(v.tensor_reduce(total[:], grid(score), AX, ALU.add))
                ch.step(v.reciprocal(total[:], total[:]))
                ch.step(v.tensor_scalar(total[:], total[:], 2.5, None, ALU.mult))
                ch.step(v.tensor_tensor(grid(score), grid(score), total[:].unsqueeze(2).broadcast_to([P, TILES, E]), ALU.mult))
                dve.wait_ge(ranked, 1)
                ch.step(v.tensor_scalar(whole[:, 0:E], ps_count[:, 0:E], 1.0 / P, 127.0 / 256, ALU.mult, ALU.add))
                ch.step(v.tensor_copy(nblk[:], whole[:, 0:E]))
                ch.step(v.tensor_tensor_scan(end[:], ones64[:], nblk[:], 0.0, ALU.mult, ALU.add))
                ch.step(v.tensor_tensor(start[:], end[:], nblk[:], ALU.subtract))
                ch.step(v.tensor_scalar(holds[:], nblk[:], 0.0, None, ALU.is_gt))
                ch.step(v.tensor_tensor_scan(held[:], ones64[:], holds[:], 0.0, ALU.mult, ALU.add))
                ch.step(v.tensor_scalar(ones64[:], end[:], k.c("row"), 0.0, ALU.is_le, ALU.add, accum_out=col[:, 0:1]))
                ch.step(v.tensor_scalar(ones64[:], held[:], k.c("row"), 0.0, ALU.is_le, ALU.add, accum_out=col[:, 1:2]))
                v.tensor_scalar(col[:], col[:], E - 1.0, None, ALU.min).then_inc(col_done, 1)
                ch.step(v.tensor_copy(routes.count[:, 0:1], end[0:1, E - 1:E]))
                ch.step(v.tensor_copy(routes.count[:, 1:2], held[0:1, E - 1:E]))
                ch.step(v.tensor_scalar(whole[:], ps_rank[:], 1.0 / P, -127.0 / 256, ALU.mult, ALU.add))
                ch.step(v.tensor_copy(tmp[:], whole[:]))
                ch.step(v.tensor_scalar(tmp[:], tmp[:], -(127.0 * P + P - 1), 1.0, ALU.mult, ALU.add))
                ch.step(v.scalar_tensor_tensor(tmp2[:], ps_rank[:], float(P), tmp[:], ALU.mult, ALU.add))
                ch.step(v.tensor_tensor(grid(tmp2), grid(tmp2), start[:].unsqueeze(1).broadcast_to([P, TILES, E]), ALU.add))
                ch.step(v.tensor_tensor(tmp2[:], tmp2[:], mask[:], ALU.mult))
                for i in range(TILES):
                    ins = v.max(top8[:, i, :], tmp2[:, i * E:(i + 1) * E])
                ch.step(ins)
                for i in range(TILES):
                    keys = tmp2[:, i * E:(i + 1) * E].unsqueeze(1).broadcast_to([P, TK, E])
                    mine = top8[:, i, :].unsqueeze(2).broadcast_to([P, TK, E])
                    gates = score[:, i * E:(i + 1) * E].unsqueeze(1).broadcast_to([P, TK, E])
                    ch.step(v.tensor_tensor(eq[:], keys, mine, ALU.is_equal))
                    ch.step(v.tensor_tensor(eq[:], eq[:], gates, ALU.mult))
                    ch.step(v.tensor_reduce(weight8[:, i * TK:(i + 1) * TK], eq[:], AX, ALU.add))
                flat8 = top8[:].rearrange("p i j -> p (i j)")
                ch.step(v.tensor_scalar(rank[:], flat8, -1.0, None, ALU.add))
                ch.step(v.tensor_scalar(whole[:, 0:64], rank[:], 1.0 / P, -127.0 / 256, ALU.mult, ALU.add))
                ch.step(v.tensor_copy(slot_p[:], whole[:, 0:64]))
                ch.step(v.scalar_tensor_tensor(slot_b[:], slot_p[:], -float(P), rank[:], ALU.mult, ALU.add))
                dve.wait_ge(lined, 1)
                r = lambda n: line[:, n, :]
                ch.step(v.tensor_copy(line[:, 0:2, :], ps_line[0:1, 0:2 * P].rearrange("p (a b) -> p a b", a=2)))
                ch.step(v.tensor_copy(routes.expert[:], r(1)))
                ch.step(v.memset(r(1), 1.0))
                ch.step(v.tensor_tensor(line[:, 1, 1:BLOCKS], line[:, 0, 1:BLOCKS], line[:, 0, 0:BLOCKS - 1], ALU.not_equal))
                ch.step(v.memset(r(2), 1.0))
                ch.step(v.tensor_tensor_scan(r(3), r(2), r(1), 0.0, ALU.mult, ALU.add))
                ch.step(v.tensor_copy(routes.number[:, 0:BLOCKS], r(3)))
                ch.step(v.tensor_scalar(r(6), k.c("iota")[0:1, :], end[0:1, E - 1:E], None, ALU.is_lt))
                ch.step(v.tensor_scalar(r(7), r(3), held[0:1, E - 1:E], None, ALU.is_lt))
                ch.step(v.tensor_tensor(r(6), r(6), r(7), ALU.mult))
                ch.step(v.tensor_tensor(r(6), r(6), r(1), ALU.mult))
                ch.step(v.tensor_tensor(routes.following[:, 0:BLOCKS], r(6), r(3), ALU.mult))
                ch.step(v.memset(routes.following[:, BLOCKS:LOOKED], 0))
                across = k.c("iota").unsqueeze(1).broadcast_to([P, TK, P])
                for i in range(TILES):
                    u = i % 2
                    if i >= 2:
                        dve.wait_ge(tabled, i - 1)
                    lo, hi = i * TK, (i + 1) * TK
                    v.tensor_tensor(hot_p[:, u], across, slot_p[:, lo:hi].unsqueeze(2).broadcast_to([P, TK, P]), ALU.is_equal)
                    ch.step(v.tensor_tensor(blocks[:], across, slot_b[:, lo:hi].unsqueeze(2).broadcast_to([P, TK, P]),
                                            ALU.is_equal))
                    v.tensor_scalar(hot_b[:, u, :, 0, :], blocks[:], k.c("token1")[:, i:i + 1], None, ALU.mult)
                    ins = v.tensor_tensor(hot_b[:, u, :, 1, :], blocks[:],
                                          weight8[:, lo:hi].unsqueeze(2).broadcast_to([P, TK, P]), ALU.mult)
                    ins.then_inc(hot, 1)
                    dve.wait_ge(hot, i + 1)
                dve.wait_ge(tabled, TILES)
                ch.step(v.tensor_scalar(pad[:], ps_table[:, 0:P], 0.0, k.c("padrow"), ALU.is_equal, ALU.mult))
                ch.step(v.scalar_tensor_tensor(pad[:], ps_table[:, 0:P], -1.0, pad[:], ALU.add, ALU.add))
                ch.step(v.tensor_copy(routes.token[:, 0:BLOCKS], pad[:]))
                ch.step(v.tensor_copy(routes.weight[:, 0:BLOCKS], ps_table[:, P:2 * P]))


def gated(nc, gate_up, silu, out_hidden):
    return nc.vector.tensor_tensor(out_hidden.rearrange("t (c p) -> t p c", c=2),
                                   silu.rearrange("t (p c) -> t p c", c=2),
                                   gate_up[:, F:2 * F].rearrange("t (p c) -> t p c", c=2), ALU.mult)


def shared_expert(k, layer, hT, name):
    nc, ap = k.nc, k.ap
    acc = k.moe_acc[layer]
    with ExitStack() as ctx:
        wg, wu = (k.sb(f"{name}_{n}", [P, KS, F], ctx=ctx) for n in ("wg", "wu"))
        wd = k.sb(name + "_wd", [P, 2, D], ctx=ctx)
        silu = k.sb(name + "_silu", [P, F], ctx=ctx)
        hidden = k.sb(name + "_hidden", [P, F], ctx=ctx)
        hidT = k.sb(name + "_hidT", [P, 2, P], ctx=ctx)
        y = k.sb(name + "_y", [P, 2, D], ctx=ctx)
        zero = k.sb(name + "_zero", [P, D], ctx=ctx)
        ps_gu = [k.ps(f"{name}_ps_gu{i}", [P, 512], ctx=ctx) for i in range(2)]
        ps_t = k.ps(name + "_ps_t", [P, 512], ctx=ctx)
        ps_y = [k.ps(f"{name}_ps_y{i}", [P, 512], ctx=ctx) for i in range(2)]
        w_in, gu_done, silu_done, hid_done = (k.sem(f"{name}_{n}") for n in ("w_in", "gu", "silu", "hid"))
        turned, hidT_done, y_done = (k.sem(f"{name}_{n}") for n in ("turned", "hidT", "y_done"))
        y_act, y_dve, zeroed = (k.sem(f"{name}_{n}") for n in ("y_act", "y_dve", "zeroed"))
        y_out = [k.sem(f"{name}_y_out{i}") for i in range(2)]
        zero_out = k.sem(name + "_zero_out")
        with nc.Block() as block:

            @block.sync
            def _(sp):
                sp.dma_start(wg[:], ap["sh_w_gate"][layer].rearrange("(p s) f -> p s f", s=KS)).then_inc(w_in, 16)
                sp.dma_start(wu[:], ap["sh_w_up"][layer].rearrange("(p s) f -> p s f", s=KS)).then_inc(w_in, 16)
                sp.dma_start(wd[:], ap["sh_w_down"][layer].rearrange("(p c) n -> p c n", c=2)).then_inc(w_in, 16)
                sp.wait_ge(zeroed, 1)
                sp.dma_start(acc[SEQ:SEQ + P, :], zero[:]).then_inc(zero_out, 16)
                sp.dma_start(k.h_rows[SEQ:SEQ + P, :], zero[:]).then_inc(zero_out, 16)
                for i in range(TILES):
                    sp.wait_ge(y_act, i + 1)
                    sp.wait_ge(y_dve, i + 1)
                    sp.dma_start(acc[i * P:(i + 1) * P, :], y[:, i % 2, :]).then_inc(y_out[i % 2], 16)
                for sem in y_out:
                    sp.wait_ge(sem, 16 * (TILES // 2))
                sp.wait_ge(zero_out, 32)

            @block.tensor
            def _(pe):
                def gate_up(i):
                    for half, w in enumerate((wg, wu)):
                        for s in range(KS):
                            mm = nc.tensor.matmul(ps_gu[i % 2][:, half * F:(half + 1) * F], hT[:, s, i * P:(i + 1) * P],
                                                  w[:, s, :], start=(s == 0), stop=(s == KS - 1))
                    mm.then_inc(gu_done, 1)

                pe.wait_ge(w_in, 48)
                gate_up(0)
                for i in range(TILES):
                    if i + 1 < TILES:
                        gate_up(i + 1)
                    pe.wait_ge(hid_done, i + 1)
                    for c in range(2):
                        mm = nc.tensor.transpose(ps_t[:, c * P:(c + 1) * P], hidden[:, c * P:(c + 1) * P], k.c("ident"))
                    mm.then_inc(turned, 1)
                    pe.wait_ge(hidT_done, i + 1)
                    if i:
                        pe.wait_ge(y_act, i)
                        pe.wait_ge(y_dve, i)
                    for n in range(2):
                        for c in range(2):
                            mm = nc.tensor.matmul(ps_y[n][:], hidT[:, c, :], wd[:, c, n * 512:(n + 1) * 512],
                                                  start=(c == 0), stop=(c == 1))
                    mm.then_inc(y_done, 1)

            @block.scalar
            def _(act):
                for i in range(TILES):
                    act.wait_ge(gu_done, i + 1)
                    if i:
                        act.wait_ge(hid_done, i)
                    nc.scalar.activation(silu[:], ps_gu[i % 2][:, 0:F], ACT.Silu).then_inc(silu_done, 1)
                    act.wait_ge(y_done, i + 1)
                    if i >= 2:
                        act.wait_ge(y_out[i % 2], 16 * (i // 2))
                    nc.scalar.copy(y[:, i % 2, 0:512], ps_y[0][:]).then_inc(y_act, 1)

            @block.vector
            def _(dve):
                nc.vector.memset(zero[:], 0.0).then_inc(zeroed, 1)
                for i in range(TILES):
                    dve.wait_ge(silu_done, i + 1)
                    if i:
                        dve.wait_ge(turned, i)
                    gated(nc, ps_gu[i % 2], silu[:], hidden[:]).then_inc(hid_done, 1)
                    dve.wait_ge(turned, i + 1)
                    nc.vector.tensor_copy(hidT[:], ps_t[:, 0:2 * P].rearrange("p (c t) -> p c t", c=2)).then_inc(hidT_done, 1)
                    dve.wait_ge(y_done, i + 1)
                    if i >= 2:
                        dve.wait_ge(y_out[i % 2], 16 * (i // 2))
                    nc.vector.tensor_copy(y[:, i % 2, 512:1024], ps_y[1][:]).then_inc(y_dve, 1)


def experts(k, layer, routes, name):
    nc, ap = k.nc, k.ap
    acc = k.moe_acc[layer]
    W = KS * F
    STAGES = 3
    with ExitStack() as ctx:
        stage = k.sb(name + "_stage", [P, STAGES, 3, W], ctx=ctx)
        gu_hi, gu_lo = (k.sb(f"{name}_{n}", [P, 2, KS, 2, F], F32R, ctx=ctx) for n in ("gu_hi", "gu_lo"))
        dn_hi, dn_lo = (k.sb(f"{name}_{n}", [P, 2, 2, D], F32R, ctx=ctx) for n in ("dn_hi", "dn_lo"))
        rows = [k.sb(f"{name}_rows{i}", [P, D], ctx=ctx) for i in range(2)]
        rows_hi, rows_lo = (k.sb(f"{name}_{n}", [P, KS, P], F32R, ctx=ctx) for n in ("rows_hi", "rows_lo"))
        gather_at = [k.sb(f"{name}_gather_at{i}", [P, 1], U32, ctx=ctx) for i in range(2)]
        add_at = k.sb(name + "_add_at", [P, 1], U32, ctx=ctx)
        silu = k.sb(name + "_silu", [P, F], ctx=ctx)
        hidden = k.sb(name + "_hidden", [P, F], ctx=ctx)
        hid_hi = [k.sb(f"{name}_hid_hi{i}", [P, 2, P], F32R, ctx=ctx) for i in range(2)]
        hid_lo = [k.sb(f"{name}_hid_lo{i}", [P, 2, P], F32R, ctx=ctx) for i in range(2)]
        y = [k.sb(f"{name}_y{i}", [P, D], ctx=ctx) for i in range(2)]
        ps_x = [k.ps(f"{name}_ps_x{i}", [P, 512], ctx=ctx) for i in range(2)]
        ps_gu = k.ps(name + "_ps_gu", [P, 512], ctx=ctx)
        ps_t = k.ps(name + "_ps_t", [P, 512], ctx=ctx)
        ps_y = [k.ps(f"{name}_ps_y{i}", [P, 512], ctx=ctx) for i in range(2)]
        w_in = [[k.sem(f"{name}_w_in{h}{j}") for j in range(3)] for h in range(2)]
        gu_landed, dn_landed = k.sem(name + "_gu_landed"), k.sem(name + "_dn_landed")
        rows_in = [k.sem(f"{name}_rows_in{i}") for i in range(2)]
        gu_rounded, dn_rounded, gu_split, dn_split = (k.sem(f"{name}_{n}") for n in
                                                      ("gu_rounded", "dn_rounded", "gu_split", "dn_split"))
        rows_turned, rows_rounded, rows_split = (k.sem(f"{name}_{n}") for n in ("rows_turned", "rows_rounded", "rows_split"))
        gu_done, silu_done, hid_done = (k.sem(f"{name}_{n}") for n in ("gu_done", "silu_done", "hid_done"))
        hid_turned, hid_rounded, hid_split = (k.sem(f"{name}_{n}") for n in ("hid_turned", "hid_rounded", "hid_split"))
        y_done, y_act, y_dve = (k.sem(f"{name}_{n}") for n in ("y_done", "y_act", "y_dve"))
        added, gather_set, add_set, pool_steps = (k.sem(f"{name}_{n}") for n in ("added", "gather_set", "add_set", "pool_steps"))

        def zero(b):
            return isinstance(b, int) and b == 0

        def when(eng, b, n, sure):
            return nullcontext() if sure else eng.If(b < n)

        def look(eng, table, at, low, high):
            return eng.value_load(table[0:1, bass.ds(at, 1)], min_val=low, max_val=high)

        def schedule(eng, step):
            n = look(eng, routes.count, 0, SURE, BLOCKS - 1)
            step(0, 0, n, True)
            step(1, 1, n, True)
            with eng.Fori(1, SURE // 2 - 1) as i:
                for half in range(2):
                    step(2 * i + half, half, n, True)
            with eng.Fori(SURE // 2 - 1, BLOCKS // 2) as i:
                with eng.If(2 * i < n + 1):
                    for half in range(2):
                        step(2 * i + half, half, n, False)
                    look(eng, routes.count, 0, SURE, BLOCKS - 1)
            return n

        def staged(place, j):
            piece = stage[:, bass.ds(place, 1), j, :].squeeze(1)
            return piece.rearrange("p (s f) -> p s f", f=F if j < 2 else D)

        def placed(t_gu, t_dn, half, j):
            return t_gu[:, bass.ds(half, 1), :, j, :].squeeze(1) if j < 2 else t_dn[:, bass.ds(half, 1)].squeeze(1)

        with nc.Block() as block:

            @block.sync
            def _(sp):
                sources = [ap[n][layer].rearrange("e (p s) f -> e p (s f)", p=P)
                           for n in ("exp_w_gate", "exp_w_up", "exp_w_down")]

                def load(o, place, parity, pieces):
                    e = look(sp, routes.expert, o, 0, E - 1)
                    for j in pieces:
                        if not isinstance(o, int) or o >= STAGES:
                            if j < 2:
                                sp.wait_ge(gu_split, 2 * (o - STAGES) + 1 + j)
                            else:
                                sp.wait_ge(dn_split, o - STAGES + 1)
                        sp.dma_start(stage[:, place, j, :], sources[j][bass.ds(e, 1)].squeeze(0)
                                     ).then_inc(w_in[parity][j], 16)

                def pass_on(o, parity, pieces):
                    for j in pieces:
                        sp.wait_ge(w_in[parity][j], 8 * (o - parity) + 16)
                        sp.sem_inc(gu_landed if j < 2 else dn_landed, 1)

                n = look(sp, routes.count, 1, TK, E)
                for o in range(4):
                    load(o, o % STAGES, o % 2, (0, 1))
                    if o >= 1:
                        load(o - 1, (o - 1) % STAGES, (o - 1) % 2, (2,))
                        pass_on(o - 1, (o - 1) % 2, (0, 1))
                    if o >= 2:
                        pass_on(o - 2, (o - 2) % 2, (2,))
                with sp.Fori(0, (E + 2 - 4 + 5) // 6) as i:
                    for u in range(6):
                        o = 6 * i + (4 + u)
                        with sp.If(o < n):
                            load(o, (4 + u) % STAGES, u % 2, (0, 1))
                        with sp.If(o < n + 1):
                            load(o - 1, (3 + u) % STAGES, (u + 1) % 2, (2,))
                            pass_on(o - 1, (u + 1) % 2, (0, 1))
                        with sp.If(o < n + 2):
                            pass_on(o - 2, u % 2, (2,))

            @block.gpsimd
            def _(pool):
                def gather(b, half, first=False):
                    if not first:
                        pool.wait_ge(rows_turned, 2 * (b - 1))
                    pool.tensor_copy(gather_at[half][:], routes.token[:, bass.ds(b, 1)]).then_inc(gather_set, 1)
                    pool.wait_ge(gather_set, b + 1)
                    pool.sem_inc(pool_steps, 1)
                    pool.indirect_dma_start(out=rows[half][:], out_offset=None, in_=k.h_rows,
                                            in_offset=bass.IndirectOffsetOnAxis(ap=gather_at[half][:], axis=0)
                                            ).then_inc(rows_in[half], 16)

                def add(b, half):
                    if not zero(b):
                        pool.wait_ge(added, 16 * b)
                    pool.tensor_copy(add_at[:], routes.token[:, bass.ds(b, 1)]).then_inc(add_set, 1)
                    pool.wait_ge(add_set, b + 1)
                    pool.wait_ge(y_act, b + 1)
                    pool.wait_ge(y_dve, b + 1)
                    pool.sem_inc(pool_steps, 1)
                    pool.indirect_dma_start(out=acc, out_offset=bass.IndirectOffsetOnAxis(ap=add_at[:], axis=0),
                                            in_=y[half][:], in_offset=None, compute_op=ALU.add).then_inc(added, 16)

                def rest_of_down(half, place, number):
                    pool.wait_ge(dn_rounded, number)
                    pool.tensor_tensor(placed(None, dn_lo, half, 2), staged(place, 2), placed(None, dn_hi, half, 2).bitcast(F32),
                                       ALU.subtract).then_inc(dn_split, 1)

                def step(b, half, n, sure):
                    with when(pool, b + 2, n, sure):
                        gather(b + 2, half)
                    if not zero(b):
                        after = look(pool, routes.following, b - 1, 0, E - 1)
                        with pool.If(after > 0):
                            rest_of_down(after % 2, after % STAGES, after + 1)
                        with when(pool, b - 1, n, sure):
                            add(b - 1, 1 - half)

                gather(0, 0, first=True)
                gather(1, 1, first=True)
                rest_of_down(0, 0, 1)
                n = schedule(pool, step)
                pool.wait_ge(added, 16 * n)

            @block.tensor
            def _(pe):
                def turn_rows(b, half):
                    pe.wait_ge(rows_in[half], 16 * (b // 2 + 1) if isinstance(b, int) else 8 * (b - half) + 16)
                    if not zero(b):
                        pe.wait_ge(rows_split, 2 * b)
                    for bank in range(2):
                        for s in range(4):
                            mm = pe.transpose(ps_x[bank][:, s * P:(s + 1) * P],
                                              rows[half][:, (4 * bank + s) * P:(4 * bank + s + 1) * P], k.c("ident"))
                        mm.then_inc(rows_turned, 1)

                def gate_up(b):
                    number = look(pe, routes.number, b, 1, E)
                    at = (number + 1) % 2
                    pe.wait_ge(gu_split, 2 * number)
                    pe.wait_ge(rows_split, 2 * (b + 1))
                    passes = ((rows_hi, gu_hi), (rows_hi, gu_lo), (rows_lo, gu_hi))
                    for n, (x, w) in enumerate(passes):
                        for s in range(KS):
                            mm = pe.matmul(ps_gu[:], x[:, s, :],
                                           w[:, bass.ds(at, 1), s].squeeze(1).rearrange("p a f -> p (a f)"),
                                           start=(n == 0 and s == 0), stop=(n == 2 and s == KS - 1))
                    mm.then_inc(gu_done, 1)

                def down(b, half, j, number, at):
                    if j == 0:
                        pe.wait_ge(dn_split, number)
                        pe.wait_ge(hid_split, b + 1)
                    if not zero(b):
                        pe.wait_ge(y_dve if j else y_act, b)
                    passes = ((hid_hi, dn_hi), (hid_hi, dn_lo), (hid_lo, dn_hi))
                    for n, (x, w) in enumerate(passes):
                        for c in range(2):
                            mm = pe.matmul(ps_y[j][:], x[half][:, c, :],
                                           w[:, bass.ds(at, 1), c, j * 512:(j + 1) * 512].squeeze(1),
                                           start=(n == 0 and c == 0), stop=(n == 2 and c == 1))
                    mm.then_inc(y_done, 1)

                def turn_hidden(b):
                    pe.wait_ge(hid_done, b + 1)
                    for c in range(2):
                        mm = pe.transpose(ps_t[:, c * P:(c + 1) * P], hidden[:, c * P:(c + 1) * P], k.c("ident"))
                    mm.then_inc(hid_turned, 1)

                def step(b, half, n, sure):
                    with when(pe, b, n, sure):
                        gate_up(b)
                    if not zero(b):
                        number = look(pe, routes.number, b - 1, 1, E)
                        at = (number + 1) % 2
                    with when(pe, b + 1, n, sure):
                        turn_rows(b + 1, 1 - half)
                    if not zero(b):
                        with when(pe, b - 1, n, sure):
                            down(b - 1, 1 - half, 0, number, at)
                    with when(pe, b, n, sure):
                        turn_hidden(b)
                    if not zero(b):
                        with when(pe, b - 1, n, sure):
                            down(b - 1, 1 - half, 1, number, at)

                turn_rows(0, 0)
                schedule(pe, step)

            @block.scalar
            def _(act):
                def round_rows(b):
                    act.wait_ge(rows_turned, 2 * (b + 1))
                    if not zero(b):
                        act.wait_ge(gu_done, b)
                    for bank in range(2):
                        act.copy(rows_hi[:, 4 * bank:4 * bank + 4, :],
                                 ps_x[bank][:].rearrange("p (s t) -> p s t", s=4)).then_inc(rows_rounded, 1)

                def silu_of(b):
                    act.wait_ge(gu_done, b + 1)
                    if not zero(b):
                        act.wait_ge(hid_done, b)
                    act.activation(silu[:], ps_gu[:, 0:F], ACT.Silu).then_inc(silu_done, 1)

                def y_back(b, half):
                    act.wait_ge(y_done, 2 * b + 1)
                    if not isinstance(b, int) or b >= 2:
                        act.wait_ge(added, 16 * (b - 1))
                    act.activation(y[half][:, 0:512], ps_y[0][:], ACT.Copy,
                                   scale=routes.weight[:, bass.ds(b, 1)]).then_inc(y_act, 1)

                def round_weights(half, place, o, j, sem):
                    act.wait_ge(gu_landed, 2 * o + j + 1) if j < 2 else act.wait_ge(dn_landed, o + 1)
                    act.copy(placed(gu_hi, dn_hi, half, j), staged(place, j)).then_inc(sem, 1)

                def round_gate_up(b, after):
                    with act.If(after > 0):
                        if not zero(b):
                            act.wait_ge(gu_done, b)
                        for j in range(2):
                            round_weights(after % 2, after % STAGES, after, j, gu_rounded)

                def step(b, half, n, sure):
                    after = look(act, routes.following, b, 0, E - 1)
                    after_next = look(act, routes.following, b + 1, 0, E - 1)
                    with when(act, b, n, sure):
                        silu_of(b)
                    with when(act, b + 1, n, sure):
                        round_rows(b + 1)
                    if not zero(b):
                        with when(act, b - 1, n, sure):
                            y_back(b - 1, 1 - half)
                    round_gate_up(b + 1, after_next)
                    with act.If(after > 0):
                        if not zero(b):
                            act.wait_ge(y_done, 2 * b)
                        round_weights(after % 2, after % STAGES, after, 2, dn_rounded)

                for j in range(3):
                    round_weights(0, 0, 0, j, gu_rounded if j < 2 else dn_rounded)
                round_gate_up(0, look(act, routes.following, 0, 0, E - 1))
                round_rows(0)
                schedule(act, step)

            @block.vector
            def _(dve):
                def rest_of_rows(b):
                    for bank in range(2):
                        dve.wait_ge(rows_rounded, 2 * b + bank + 1)
                        part = slice(4 * bank, 4 * bank + 4)
                        dve.tensor_tensor(rows_lo[:, part, :], ps_x[bank][:].rearrange("p (s t) -> p s t", s=4),
                                          rows_hi[:, part, :].bitcast(F32), ALU.subtract).then_inc(rows_split, 1)

                def hidden_of(b):
                    dve.wait_ge(silu_done, b + 1)
                    if not zero(b):
                        dve.wait_ge(hid_turned, b)
                    gated(nc, ps_gu, silu[:], hidden[:]).then_inc(hid_done, 1)

                def split_hidden(b, half):
                    dve.wait_ge(hid_turned, b + 1)
                    src = ps_t[:, 0:2 * P].rearrange("p (c t) -> p c t", c=2)
                    dve.tensor_copy(hid_hi[half][:], src).then_inc(hid_rounded, 1)
                    dve.wait_ge(hid_rounded, b + 1)
                    dve.tensor_tensor(hid_lo[half][:], src, hid_hi[half][:].bitcast(F32), ALU.subtract).then_inc(hid_split, 1)

                def y_back(b, half):
                    dve.wait_ge(y_done, 2 * b + 2)
                    if not isinstance(b, int) or b >= 2:
                        dve.wait_ge(added, 16 * (b - 1))
                    dve.tensor_scalar(y[half][:, 512:1024], ps_y[1][:], routes.weight[:, bass.ds(b, 1)], None,
                                      ALU.mult).then_inc(y_dve, 1)

                def rest_of_weights(half, place, number):
                    for j in range(2):
                        dve.wait_ge(gu_rounded, 2 * number - 1 + j)
                        dve.tensor_tensor(placed(gu_lo, None, half, j), staged(place, j),
                                          placed(gu_hi, None, half, j).bitcast(F32), ALU.subtract).then_inc(gu_split, 1)

                def rests_after(b):
                    after = look(dve, routes.following, b, 0, E - 1)
                    with dve.If(after > 0):
                        rest_of_weights(after % 2, after % STAGES, after + 1)

                def step(b, half, n, sure):
                    with when(dve, b, n, sure):
                        hidden_of(b)
                    with when(dve, b + 1, n, sure):
                        rest_of_rows(b + 1)
                    with when(dve, b, n, sure):
                        split_hidden(b, half)
                    if not zero(b):
                        with when(dve, b - 1, n, sure):
                            y_back(b - 1, 1 - half)
                    rests_after(b + 1)

                rest_of_weights(0, 0, 1)
                rests_after(0)
                rest_of_rows(0)
                schedule(dve, step)


def moe_residual(k, layer, m, name, out=None):
    nc = k.nc
    acc = k.moe_acc[layer]
    NB = 4
    with ExitStack() as ctx:
        gate = k.sb(name + "_gate", [P, D], ctx=ctx)
        part = k.sb(name + "_part", [P, NB, D], ctx=ctx)
        gate_in, gated_done, x_done = (k.sem(f"{name}_{n}") for n in ("gate_in", "gated", "x_done"))
        part_in = [k.sem(f"{name}_part_in{i}") for i in range(NB)]
        out_done = k.sem(name + "_out")
        with nc.Block() as block:

            @block.sync
            def _(sp):
                sp.dma_start(gate[:], spread(k.mod[m, 2])).then_inc(gate_in, 16)
                for i in range(TILES):
                    if i >= NB:
                        sp.wait_ge(x_done, i - NB + 1)
                    sp.dma_start(k.x[:, i, :], k.x_rows[i * P:(i + 1) * P, :]).then_inc(part_in[i % NB], 16)
                    sp.dma_start(part[:, i % NB, :], acc[i * P:(i + 1) * P, :]).then_inc(part_in[i % NB], 16)

            @block.vector
            def _(dve):
                dve.wait_ge(gate_in, 16)
                for i in range(TILES):
                    dve.wait_ge(part_in[i % NB], 32 * (i // NB + 1))
                    nc.vector.tensor_tensor(part[:, i % NB, :], part[:, i % NB, :], gate[:], ALU.mult).then_inc(gated_done, 1)
                    dve.wait_ge(gated_done, i + 1)
                    nc.vector.tensor_tensor(k.x[:, i, :], k.x[:, i, :], part[:, i % NB, :], ALU.add).then_inc(x_done, 1)

            @block.scalar
            def _(act):
                if out is None:
                    return
                for i in range(TILES):
                    act.wait_ge(x_done, i + 1)
                    act.dma_start(out[i * P:(i + 1) * P, :], k.x[:, i, :]).then_inc(out_done, 16)
                act.wait_ge(out_done, 16 * TILES)


def moe_front(k, layer, m, name, routes):
    with ExitStack() as inner:
        hT = k.sb(name + "_hT", [P, KS, SEQ], ctx=inner)
        spilled = k.sem(name + "_spilled")

        def spill(sp):
            sp.dma_start(k.x_rows.rearrange("(i p) d -> p i d", p=P), k.x[:]).then_inc(spilled, 16)
            sp.wait_ge(spilled, 16)

        normalise(k, m, None, name + "_n", True, hT=hT, rows_out=True, extra=spill)
        route(k, layer, hT, routes, name + "_r")
        shared_expert(k, layer, hT, name + "_s")


def project_u(k, hT, u_rows, uT):
    nc, ap = k.nc, k.ap
    W5 = GROUPS * GH
    with ExitStack() as ctx:
        w = k.sb("u_w", [P, KS, W5], ctx=ctx)
        ps = [k.ps(f"u_ps{i}", [P, 512], ctx=ctx) for i in range(2)]
        ps_t = [k.ps(f"u_ps_t{i}", [P, 512], ctx=ctx) for i in range(2)]
        w_in, done, copied, turned, back = (k.sem(f"u_{n}") for n in ("w_in", "done", "copied", "turned", "back"))
        with nc.Block() as block:

            @block.sync
            def _(sp):
                sp.dma_start(w[:], ap["hyb_w_in"][0][:, 0:W5].rearrange("(p s) n -> p s n", s=KS)).then_inc(w_in, 16)

            @block.tensor
            def _(pe):
                pe.wait_ge(w_in, 16)
                for j in range(CH):
                    if j >= 2:
                        pe.wait_ge(copied, j - 1)
                    for s in range(KS):
                        mm = pe.matmul(ps[j % 2][:], hT[:, s, j:SEQ:CH], w[:, s, :], start=(s == 0), stop=(s == KS - 1))
                    mm.then_inc(done, 1)
                pe.wait_ge(copied, CH)
                for q in range(GROUPS // 4):
                    if q >= 2:
                        pe.wait_ge(back, q - 1)
                    for g in range(4):
                        mm = pe.transpose(ps_t[q % 2][:, g * P:(g + 1) * P],
                                          u_rows[:, 4 * q + g].rearrange("c j h -> c (j h)"), k.c("ident"))
                    mm.then_inc(turned, 1)

            @block.scalar
            def _(act):
                for j in range(CH):
                    act.wait_ge(done, j + 1)
                    act.copy(u_rows[:, :, j, :], ps[j % 2][:].rearrange("c (g h) -> c g h", h=GH)).then_inc(copied, 1)

            @block.vector
            def _(dve):
                for q in range(GROUPS // 4):
                    dve.wait_ge(turned, q + 1)
                    dve.tensor_copy(uT[:, 4 * q:4 * q + 4, :], ps_t[q % 2][:].rearrange("p (g c) -> p g c", g=4)
                                    ).then_inc(back, 1)


def sine_tables(k, cos_sin, rotor, lam, dt, mag):
    nc, ap = k.nc, k.ap
    N = TILES * ROPE + GROUPS
    with ExitStack() as ctx:
        pos = k.sb("st_pos", [P, TILES], I32, ctx=ctx)
        pos_f = k.sb("st_pos_f", [P, TILES], ctx=ctx)
        lam_in = k.sb("st_lam_in", [GROUPS, 2, 2, NS], ctx=ctx)
        ang = k.sb("st_ang", [P, N], ctx=ctx)
        turns = k.sb("st_turns", [P, N], I32, ctx=ctx)
        turns_f = k.sb("st_turns_f", [P, N], ctx=ctx)
        co = k.sb("st_co", [P, N], ctx=ctx)
        both = k.sb("st_both", [P, 2, N], ctx=ctx)
        decay = k.sb("st_decay", [P, GROUPS], ctx=ctx)
        ps = k.ps("st_ps", [P, 512], ctx=ctx)
        loaded, turned, dt_done, ready, waves, chain = (k.sem(f"st_{n}") for n in
                                                        ("loaded", "turned", "dt", "ready", "waves", "chain"))
        with nc.Block() as block:

            @block.sync
            def _(sp):
                sp.dma_start(dt[:], spread(ap["s5_log_dt"][0])).then_inc(loaded, 16)
                for half in range(2):
                    sp.dma_start(lam_in[:, 0, half, :], ap["s5_lambda_re"][0]).then_inc(loaded, 16)
                    sp.dma_start(lam_in[:, 1, half, :], ap["s5_lambda_im"][0]).then_inc(loaded, 16)
                with nc.allow_non_contiguous_dma(reason="1024 positions"):
                    sp.dma_start(pos[:], ap["positions"][0].rearrange("(i p) -> p i", p=P)).then_inc(loaded, 16)

            @block.tensor
            def _(pe):
                pe.wait_ge(loaded, 96)
                for i in range(2):
                    mm = pe.transpose(ps[:, i * GROUPS:(i + 1) * GROUPS], lam_in[:, i].rearrange("g a p -> g (a p)"),
                                      k.c("ident")[0:GROUPS, 0:GROUPS])
                mm.then_inc(turned, 1)

            @block.scalar
            def _(act):
                act.wait_ge(loaded, 96)
                act.activation(dt[:], dt[:], ACT.Exp).then_inc(dt_done, 1)
                act.wait_ge(ready, 1)
                act.activation(mag[:, 0, :], decay[:], ACT.Exp)
                act.activation(mag[:, 1, :], decay[:], ACT.Exp, scale=float(CH)).then_inc(waves, 1)
                act.wait_ge(ready, 2)
                act.activation(both[:, 0, :], co[:], ACT.Sin)
                act.activation(both[:, 1, :], ang[:], ACT.Sin).then_inc(waves, 1)

            @block.vector
            def _(dve):
                ch = Chain(dve, chain)
                dve.wait_ge(turned, 1)
                ch.step(dve.tensor_copy(lam[:], ps[:, 0:2 * GROUPS].rearrange("p (a g) -> p a g", a=2)))
                dve.wait_ge(dt_done, 1)
                ch.step(dve.tensor_copy(pos_f[:], pos[:]))
                ch.step(dve.tensor_tensor(ang[:, 0:64].rearrange("p (i r) -> p i r", r=ROPE),
                                          pos_f[:].unsqueeze(2).broadcast_to([P, TILES, ROPE]),
                                          k.c("freq").unsqueeze(1).broadcast_to([P, TILES, ROPE]), ALU.mult))
                ch.step(dve.tensor_tensor(ang[:, 64:N], lam[:, 1, :], dt[:], ALU.mult))
                dve.tensor_tensor(decay[:], lam[:, 0, :], dt[:], ALU.mult).then_inc(ready, 1)
                ch.step(dve.tensor_scalar(turns[:], ang[:], float(1.0 / TWO_PI), None, ALU.mult))
                ch.step(dve.tensor_copy(turns_f[:], turns[:]))
                for part in (PI_A, PI_B, PI_C):
                    ch.step(dve.scalar_tensor_tensor(ang[:], turns_f[:], -part, ang[:], ALU.mult, ALU.add))
                ch.step(dve.tensor_scalar(ang[:], ang[:], 3.1415925, -3.1415925, ALU.min, ALU.max))
                ch.step(dve.scalar_tensor_tensor(co[:], ang[:], -1.0, ang[:], ALU.mult, ALU.max))
                dve.tensor_scalar(co[:], co[:], -1.0, float(np.pi / 2), ALU.mult, ALU.add).then_inc(ready, 1)
                dve.wait_ge(waves, 2)
                ch.step(dve.tensor_copy(cos_sin[:], both[:, :, 0:64].rearrange("p a (i r) -> p a i r", r=ROPE)))
                ch.step(dve.tensor_copy(rotor[:], both[:, :, 64:N]))


def s5(k, uT, rows, mixT, rotor, lam, mag):
    nc, ap = k.nc, k.ap
    G = HALF_G
    NQ = GROUPS // 4
    with ExitStack() as ctx:
        sbt = lambda n, shape: k.sb("s5_" + n, shape, ctx=ctx)
        cc = sbt("c", [P, 2, GROUPS, GH])
        bb = sbt("b", [P, 2, GROUPS, GH])
        coef = sbt("coef", [P, 6, GROUPS])
        pw = sbt("pw", [P, 2, CH + 1, GROUPS])
        sg = sbt("sg", [P, 4, CH + 1, GROUPS])
        wbuf = sbt("wbuf", [P, G, 16, GH])
        vrev = sbt("vrev", [P, G, CH, GH])
        tmp_w = sbt("tmp_w", [P, (CH + 1) * G * GH])
        rot = sbt("rot", [P, 2, 7, GROUPS])
        tr = sbt("tr", [P, 2, G, CHUNKS])
        tmp_t = sbt("tmp_t", [P, G, CHUNKS // 2])
        bpad = sbt("bpad", [P, 4, 15, GH])
        m3 = sbt("m3", [P, 2, 4, P])
        m1 = sbt("m1", [P, 4, P])
        z = sbt("z", [P, 4, CHUNKS])
        zt = sbt("zt", [P, 4, CHUNKS])
        st = sbt("st", [P, 4, CHUNKS + 1])
        dcol = sbt("dcol", [P, GROUPS])
        bcol = sbt("bcol", [P, GROUPS])
        b_in = tmp_w[:, 0:1024].rearrange("p (a g h) -> p a g h", a=2, h=GH)
        tmp_b = tmp_w[:, 1024:1536].rearrange("p (g h) -> p g h", h=GH)
        c_in = tmp_t[:].rearrange("p g c -> p (g c)").rearrange("p (a t u n) -> p a t u n", a=2, t=4, u=2)
        glu = rows.rearrange("p g j h -> p g (j h)")
        out_rows = rows.rearrange("p g j h -> p (g j h)").rearrange("c (j n) -> c j n", j=CH)
        gate = sbt("gate", [P, 2, 4, CHUNKS])
        bank = [k.ps(f"s5_ps{i}", [P, 512], ctx=ctx) for i in range(8)]
        loaded, glu_clear, glu_in, c_turned, chain = (k.sem(f"s5_{n}") for n in
                                                      ("loaded", "glu_clear", "glu_in", "c_turned", "chain"))
        ready, m3_turned, m3_back, m1_done, m1_back = (k.sem(f"s5_{n}") for n in
                                                       ("ready", "m3_turned", "m3_back", "m1_done", "m1_back"))
        w_done, z_done, swapped, s_done, y_done, y_read = (k.sem(f"s5_{n}") for n in
                                                           ("w_done", "z_done", "swapped", "s_done", "y_done", "y_read"))
        gelu_done, glu_done, biased, sig_done, gated_done = (k.sem(f"s5_{n}") for n in
                                                             ("gelu", "glu_done", "biased", "sig", "gated"))
        y_turned, y_rows, mix_turned, mix_a, mix_v = (k.sem(f"s5_{n}") for n in
                                                      ("y_turned", "y_rows", "mix_turned", "mix_a", "mix_v"))

        with nc.Block() as block:

            @block.sync
            def _(sp):
                with nc.allow_non_contiguous_dma(reason="small tables of the S5 heads"):
                    for half in range(2):
                        for i, n in enumerate(("s5_b_re", "s5_b_im")):
                            sp.dma_start(b_in[half * NS:(half + 1) * NS, i], ap[n][0].rearrange("g p h -> p g h")
                                         ).then_inc(loaded, 16)
                        for i, n in enumerate(("s5_c_re", "s5_c_im")):
                            sp.dma_start(c_in[:, i, :, half, :], ap[n][0].rearrange("(t g) h p -> (g h) t p", t=4)
                                         ).then_inc(loaded, 16)
                    for j in range(CH):
                        sp.dma_start(dcol[j * GH:(j + 1) * GH, :], ap["s5_d"][0].rearrange("g h -> h g")).then_inc(loaded, 16)
                        sp.dma_start(bcol[j * GH:(j + 1) * GH, :], ap["s5_glu_b"][0].rearrange("g h -> h g")
                                     ).then_inc(loaded, 16)
                    sp.wait_ge(glu_clear, 1)
                    for j in range(CH):
                        sp.dma_start(glu[j * GH:(j + 1) * GH, :, j * GH:(j + 1) * GH],
                                     ap["s5_glu_w"][0].rearrange("g h e -> h g e")).then_inc(glu_in, 16)

            @block.gpsimd
            def _(pool):
                pool.memset(glu, 0.0).then_inc(glu_clear, 1)

            @block.tensor
            def _(pe):
                ident = k.c("ident")
                pe.wait_ge(loaded, 24 * 16)
                for i in range(2):
                    for t in range(4):
                        mm = pe.transpose(bank[i][:, t * P:(t + 1) * P], c_in[:, i, t].rearrange("q a p -> q (a p)"), ident)
                mm.then_inc(c_turned, 1)
                for q in range(NQ):
                    gs = [4 * (q % 4) + g for g in range(4)]
                    pe.wait_ge(ready, q + 1)
                    if q:
                        pe.wait_ge(m3_back, q)
                        pe.wait_ge(m1_back, q)
                    for g in range(4):
                        mm = pe.transpose(bank[0][:, g * P:(g + 1) * P], vrev[:, gs[g]].rearrange("p j h -> p (j h)"), ident)
                    mm.then_inc(m3_turned, 1)
                    for g in range(4):
                        bp = bpad[:, g].rearrange("p j h -> p (j h)")
                        wb = wbuf[:, gs[g]].rearrange("p j h -> p (j h)")
                        for j in range(CH):
                            mm = pe.matmul(bank[1][:, g * P:(g + 1) * P], bp[:, (7 - j) * GH:(7 - j) * GH + P],
                                           wb[:, (7 - j) * GH:(7 - j) * GH + P], start=(j == 0), stop=(j == CH - 1))
                    mm.then_inc(m1_done, 1)
                    pe.wait_ge(m3_back, q + 1)
                    if q:
                        pe.wait_ge(z_done, q)
                    for v in range(2):
                        for g in range(4):
                            mm = pe.matmul(bank[2 + v][:, g * P:(g + 1) * P], m3[:, v, g, :], uT[:, 4 * q + g, :],
                                           start=True, stop=True)
                    mm.then_inc(w_done, 1)
                    pe.wait_ge(z_done, q + 1)
                    if q:
                        pe.wait_ge(s_done, q)
                    pe.matmul(bank[4][:], k.c("swap"), z[:].rearrange("p g c -> p (g c)"), start=True,
                              stop=True).then_inc(swapped, 1)
                    pe.wait_ge(s_done, q + 1)
                    pe.wait_ge(m1_back, q + 1)
                    if q:
                        pe.wait_ge(y_read, q)
                    for g in range(4):
                        out = bank[5][:, g * P:(g + 1) * P]
                        pe.matmul(out, m1[:, g, :], uT[:, 4 * q + g, :], start=True, stop=False)
                        mm = pe.matmul(out, wbuf[:, gs[g], 8:16].rearrange("p j h -> p (j h)"), st[:, g, 0:CHUNKS],
                                       start=False, stop=True)
                    mm.then_inc(y_done, 1)
                pe.wait_ge(gelu_done, NQ)
                pe.wait_ge(glu_in, 16 * CH)
                for q in range(NQ):
                    if q >= 2:
                        pe.wait_ge(biased, q - 1)
                    for g in range(4):
                        mm = pe.matmul(bank[6 + q % 2][:, g * P:(g + 1) * P], glu[:, 4 * q + g, :], uT[:, 4 * q + g, :],
                                       start=True, stop=True)
                    mm.then_inc(glu_done, 1)
                for q in range(NQ):
                    pe.wait_ge(gated_done, q + 1)
                    if q >= 2:
                        pe.wait_ge(y_rows, q - 1)
                    for g in range(4):
                        mm = pe.transpose(bank[q % 2][:, g * P:(g + 1) * P], uT[:, 4 * q + g, :], ident)
                    mm.then_inc(y_turned, 1)
                pe.wait_ge(y_rows, NQ)
                for t in range(4):
                    if t:
                        pe.wait_ge(mix_a, t)
                        pe.wait_ge(mix_v, t)
                    for j in range(CH):
                        mm = pe.transpose(bank[2 + j // 4][:, (j % 4) * P:(j % 4 + 1) * P], out_rows[:, j, t * P:(t + 1) * P], ident)
                    mm.then_inc(mix_turned, 1)

            @block.scalar
            def _(act):
                for q in range(NQ):
                    act.wait_ge(m1_done, q + 1)
                    if q:
                        act.wait_ge(y_done, q)
                    act.copy(m1[:].rearrange("p g n -> p (g n)"), bank[1][:]).then_inc(m1_back, 1)
                    act.wait_ge(y_read, q + 1)
                    part = uT[:, 4 * q:4 * q + 4, :]
                    act.activation(part, part, ACT.Gelu_apprx_tanh).then_inc(gelu_done, 1)
                for q in range(NQ):
                    act.wait_ge(biased, q + 1)
                    act.activation(gate[:, q % 2], gate[:, q % 2], ACT.Sigmoid).then_inc(sig_done, 1)
                for q in range(NQ):
                    act.wait_ge(y_turned, q + 1)
                    act.copy(out_rows[:, :, 4 * q * GH:4 * (q + 1) * GH].rearrange("c j (g h) -> c g j h", g=4),
                             bank[q % 2][:].rearrange("c (g j h) -> c g j h", g=4, j=CH)).then_inc(y_rows, 1)
                for t in range(4):
                    act.wait_ge(mix_turned, t + 1)
                    act.copy(mixT[:, t, :].rearrange("p (c j) -> p j c", j=CH)[:, 0:4, :],
                             bank[2][:].rearrange("p (j c) -> p j c", j=4)).then_inc(mix_a, 1)

            @block.vector
            def _(dve):
                ch = Chain(dve, chain)
                tt, ts, stt = dve.tensor_tensor, dve.tensor_scalar, dve.scalar_tensor_tensor
                T, B = slice(0, NS), slice(NS, P)

                def cmul(out_r, out_i, a_r, a_i, b_r, b_i, t):
                    ch.step(tt(out_r, a_r, b_r, ALU.mult))
                    ch.step(tt(t, a_i, b_i, ALU.mult))
                    ch.step(tt(out_r, out_r, t, ALU.subtract))
                    ch.step(tt(out_i, a_r, b_i, ALU.mult))
                    ch.step(tt(t, a_i, b_r, ALU.mult))
                    ch.step(tt(out_i, out_i, t, ALU.add))

                c6 = lambda i: coef[:, i, :]
                ch.step(dve.memset(pw[:, 0, 0, :], 1.0))
                ch.step(dve.memset(pw[:, 1, 0, :], 0.0))
                ch.step(tt(pw[:, 0, 1, :], mag[:, 0, :], rotor[:, 0, :], ALU.mult))
                ch.step(tt(pw[:, 1, 1, :], mag[:, 0, :], rotor[:, 1, :], ALU.mult))
                for j in range(2, CH + 1):
                    cmul(pw[:, 0, j, :], pw[:, 1, j, :], pw[:, 0, j - 1, :], pw[:, 1, j - 1, :], pw[:, 0, 1, :],
                         pw[:, 1, 1, :], c6(0))
                nr, ni, lr, li = c6(1), pw[:, 1, 1, :], lam[:, 0, :], lam[:, 1, :]
                ch.step(ts(nr, pw[:, 0, 1, :], -1.0, None, ALU.add))
                ch.step(tt(c6(0), lr, lr, ALU.mult))
                ch.step(tt(c6(2), li, li, ALU.mult))
                ch.step(tt(c6(0), c6(0), c6(2), ALU.add))
                ch.step(dve.reciprocal(c6(5), c6(0)))
                ch.step(tt(c6(2), nr, lr, ALU.mult))
                ch.step(tt(c6(0), ni, li, ALU.mult))
                ch.step(tt(c6(2), c6(2), c6(0), ALU.add))
                ch.step(tt(c6(2), c6(2), c6(5), ALU.mult))
                ch.step(tt(c6(3), ni, lr, ALU.mult))
                ch.step(tt(c6(0), nr, li, ALU.mult))
                ch.step(tt(c6(3), c6(3), c6(0), ALU.subtract))
                ch.step(tt(c6(3), c6(3), c6(5), ALU.mult))
                dve.wait_ge(loaded, 24 * 16)
                wide = lambda a: a.unsqueeze(2).broadcast_to([P, GROUPS, GH])
                cmul(bb[:, 0], bb[:, 1], b_in[:, 0], b_in[:, 1], wide(c6(2)), wide(c6(3)), tmp_b)
                dve.wait_ge(c_turned, 1)
                for i in range(2):
                    ch.step(dve.tensor_copy(cc[:, i].rearrange("p g h -> p (g h)"), bank[i][:]))
                for half, real, imag in ((T, 0, 1), (B, 1, 0)):
                    a_r, a_i = pw[half, 0], pw[half, 1]
                    top = half is T
                    ch.step(dve.tensor_copy(sg[half, 0], a_r if top else a_i))
                    ch.step(ts(sg[half, 1], a_i if top else a_r, -1.0 if top else 1.0, None, ALU.mult))
                    ch.step(ts(sg[half, 2], a_r if top else a_i, 1.0 if top else -1.0, None, ALU.mult))
                    ch.step(ts(sg[half, 3], a_i if top else a_r, -1.0, None, ALU.mult))
                dst = (c6(0), c6(1))
                cmul(dst[0], dst[1], rotor[:, 0, :], rotor[:, 1, :], rotor[:, 0, :], rotor[:, 1, :], c6(4))
                cmul(c6(2), c6(3), c6(0), c6(1), c6(0), c6(1), c6(4))
                cmul(rot[:, 0, 0, :], rot[:, 1, 0, :], c6(2), c6(3), c6(2), c6(3), c6(4))
                for l in range(1, 7):
                    cmul(rot[:, 0, l, :], rot[:, 1, l, :], rot[:, 0, l - 1, :], rot[:, 1, l - 1, :],
                         rot[:, 0, l - 1, :], rot[:, 1, l - 1, :], c6(4))
                ch.step(dve.memset(wbuf[:, :, 0:7, :], 0.0))
                ch.step(dve.memset(bpad[:], 0.0))
                ch.step(dve.memset(st[:, :, 0:1], 0.0))

                def half_tables(hf):
                    gsl = slice(hf * G, (hf + 1) * G)
                    def power(i, j0, j1):
                        return sg[:, i, j0:j1, gsl].unsqueeze(3).broadcast_to([P, j1 - j0, G, GH])
                    def val(t, i, n):
                        return t[:, i, gsl, :].unsqueeze(1).broadcast_to([P, n, G, GH])
                    t9 = tmp_w[:].rearrange("p (j g h) -> p j g h", j=CH + 1, g=G)
                    wv = wbuf[:, :, 7:16, :].rearrange("p g j h -> p j g h")
                    for j in range(CH + 1):
                        sel = slice(j, j + 1)
                        one = lambda t, i: t[:, i, gsl, :]
                        pj = lambda i: sg[:, i, j, gsl].unsqueeze(2).broadcast_to([P, G, GH])
                        dve.tensor_tensor(wbuf[:, :, 7 + j, :], one(cc, 0), pj(2), ALU.mult)
                        ins = dve.tensor_tensor(t9[:, j], one(cc, 1), pj(3), ALU.mult)
                    ch.step(ins)
                    for j in range(CH + 1):
                        ins = dve.tensor_tensor(wbuf[:, :, 7 + j, :], wbuf[:, :, 7 + j, :], t9[:, j], ALU.add)
                    ch.step(ins)
                    for j in range(CH):
                        one = lambda t, i: t[:, i, gsl, :]
                        pj = lambda i: sg[:, i, j, gsl].unsqueeze(2).broadcast_to([P, G, GH])
                        dve.tensor_tensor(vrev[:, :, 7 - j, :], one(bb, 0), pj(0), ALU.mult)
                        ins = dve.tensor_tensor(t9[:, j], one(bb, 1), pj(1), ALU.mult)
                    ch.step(ins)
                    for j in range(CH):
                        ins = dve.tensor_tensor(vrev[:, :, 7 - j, :], vrev[:, :, 7 - j, :], t9[:, j], ALU.add)
                    ch.step(ins)
                    ch.step(dve.memset(tr[:, 0, :, 0:1], 1.0))
                    ch.step(dve.memset(tr[:, 1, :, 0:1], 0.0))
                    for l in range(7):
                        n = 1 << l
                        r = lambda i: rot[:, i, l, gsl].unsqueeze(2).broadcast_to([P, G, n])
                        cmul(tr[:, 0, :, n:2 * n], tr[:, 1, :, n:2 * n], tr[:, 0, :, 0:n], tr[:, 1, :, 0:n], r(0), r(1),
                             tmp_t[:, :, 0:n])
                    ch.step(ts(tr[B, 1], tr[B, 1], -1.0, None, ALU.mult))

                for q in range(NQ):
                    if q % 4 == 0:
                        if q:
                            dve.wait_ge(y_done, q)
                        half_tables(q // 4)
                    gl = slice(4 * (q % 4), 4 * (q % 4) + 4)
                    gg = slice(4 * q, 4 * q + 4)
                    if q:
                        dve.wait_ge(m1_done, q)
                    dve.tensor_copy(bpad[:, :, 7, :], vrev[:, gl, 7, :]).then_inc(ready, 1)
                    dve.wait_ge(m3_turned, q + 1)
                    if q:
                        dve.wait_ge(w_done, q)
                    src = bank[0][:].rearrange("p (g n) -> p g n", g=4)
                    dve.tensor_copy(m3[:, 0], src)
                    dve.tensor_copy(m3[:, 1, :, 0:NS], src[:, :, NS:P])
                    dve.tensor_copy(m3[:, 1, :, NS:P], src[:, :, 0:NS]).then_inc(m3_back, 1)
                    dve.wait_ge(w_done, q + 1)
                    four = lambda b: bank[b][:].rearrange("p (g c) -> p g c", g=4)
                    if q:
                        dve.wait_ge(swapped, q)
                    ch.step(tt(z[:], four(2), tr[:, 0, gl], ALU.mult))
                    ch.step(tt(zt[:], four(3), tr[:, 1, gl], ALU.mult))
                    ch.step(tt(zt[:], z[:], zt[:], ALU.add))
                    for g in range(4):
                        ins = dve.tensor_tensor_scan(z[:, g, :], mag[:, 1, 4 * q + g:4 * q + g + 1].broadcast_to([P, CHUNKS]),
                                                     zt[:, g, :], 0.0, ALU.mult, ALU.add)
                    ins.then_inc(z_done, 1)
                    dve.wait_ge(swapped, q + 1)
                    ch.step(tt(zt[:], four(4), tr[:, 1, gl], ALU.mult))
                    if q:
                        dve.wait_ge(y_done, q)
                    ch.step(tt(st[:, :, 1:CHUNKS + 1], z[:], tr[:, 0, gl], ALU.mult))
                    tt(st[:, :, 1:CHUNKS + 1], st[:, :, 1:CHUNKS + 1], zt[:], ALU.subtract).then_inc(s_done, 1)
                    dve.wait_ge(y_done, q + 1)
                    ch.step(tt(uT[:, gg, :], uT[:, gg, :], dcol[:, gg].unsqueeze(2).broadcast_to([P, 4, CHUNKS]), ALU.mult))
                    tt(uT[:, gg, :], uT[:, gg, :], four(5), ALU.add).then_inc(y_read, 1)
                for q in range(NQ + 1):
                    if q < NQ:
                        dve.wait_ge(glu_done, q + 1)
                        if q >= 2:
                            dve.wait_ge(gated_done, q - 1)
                        tt(gate[:, q % 2], bank[6 + q % 2][:].rearrange("p (g c) -> p g c", g=4),
                           bcol[:, 4 * q:4 * q + 4].unsqueeze(2).broadcast_to([P, 4, CHUNKS]), ALU.add).then_inc(biased, 1)
                    if q:
                        dve.wait_ge(sig_done, q)
                        part = uT[:, 4 * q - 4:4 * q, :]
                        tt(part, part, gate[:, (q - 1) % 2], ALU.mult).then_inc(gated_done, 1)
                for t in range(4):
                    dve.wait_ge(mix_turned, t + 1)
                    dve.tensor_copy(mixT[:, t, :].rearrange("p (c j) -> p j c", j=CH)[:, 4:8, :],
                                    bank[3][:].rearrange("p (j c) -> p j c", j=4)).then_inc(mix_v, 1)


NORMED = HEADS * HD + HD
AT_V, AT_QI, AT_KI, AT_WI = NORMED, NORMED + HD, NORMED + HD + HEADS * HD, NORMED + 2 * HD + HEADS * HD


def project_rest(k, hT, qT, kT, v_rows, w_rows):
    nc, ap = k.nc, k.ap
    widths = (512, 512, QKV - 1024)
    with ExitStack() as ctx:
        w = k.sb("p_w", [P, KS, QKV], ctx=ctx)
        gains = k.sb("p_gains", [P, NORMED], ctx=ctx)
        line = [k.sb(f"p_line{i}", [P, REST], ctx=ctx) for i in range(2)]
        square = k.sb("p_square", [P, NORMED], ctx=ctx)
        stat = k.sb("p_stat", [P, 3, HEADS + 1], ctx=ctx)
        turn = k.sb("p_turn", [P, 4, 2, HEADS + 1, ROPE], ctx=ctx)
        ps = [k.ps(f"p_ps{i}", [P, 512], ctx=ctx) for i in range(3)]
        ps_t = [k.ps(f"p_ps_t{i}", [P, 512], ctx=ctx) for i in range(3)]
        w_in, gains_in, done, line_a, line_v = (k.sem(f"p_{n}") for n in ("w_in", "gains_in", "done", "line_a", "line_v"))
        squared, mean_done, root_done, line_done = (k.sem(f"p_{n}") for n in ("squared", "mean", "root", "line_done"))
        turned, back_a, back_v, chain = (k.sem(f"p_{n}") for n in ("turned", "back_a", "back_v", "chain"))
        with nc.Block() as block:

            @block.sync
            def _(sp):
                sp.dma_start(w[:], ap["hyb_w_in"][0][:, 512:512 + QKV].rearrange("(p s) n -> p s n", s=KS)).then_inc(w_in, 16)
                for h in range(HEADS):
                    sp.dma_start(gains[:, h * HD:(h + 1) * HD], spread(ap["attn_q_norm_g"][0])).then_inc(gains_in, 16)
                sp.dma_start(gains[:, HEADS * HD:], spread(ap["attn_k_norm_g"][0])).then_inc(gains_in, 16)

            @block.tensor
            def _(pe):
                pe.wait_ge(w_in, 16)

                def turn_line(i):
                    pe.wait_ge(line_done, i + 1)
                    if i:
                        pe.wait_ge(back_a, i)
                        pe.wait_ge(back_v, i)
                    src = line[i % 2]
                    for b in range(2):
                        for j in range(4):
                            pe.transpose(ps_t[b][:, j * P:(j + 1) * P], src[:, b * 640 + j * P:b * 640 + (j + 1) * P],
                                         k.c("ident"))
                        mm = pe.transpose(ps_t[2][:, b * P:(b + 1) * P], src[:, b * 640 + 512:b * 640 + 640], k.c("ident"))
                    mm.then_inc(turned, 1)

                for i in range(TILES):
                    if i:
                        pe.wait_ge(line_a, i)
                        pe.wait_ge(line_v, i)
                    for n, width in enumerate(widths):
                        for s in range(KS):
                            mm = pe.matmul(ps[n][:, 0:width], hT[:, s, i * P:(i + 1) * P],
                                           w[:, s, 512 * n:512 * n + width], start=(s == 0), stop=(s == KS - 1))
                    mm.then_inc(done, 1)
                    if i:
                        turn_line(i - 1)
                turn_line(TILES - 1)

            @block.scalar
            def _(act):
                def back(i):
                    act.wait_ge(turned, i + 1)
                    act.copy(qT[:, 0, :, i * P:(i + 1) * P], ps_t[0][:].rearrange("p (j t) -> p j t", j=4))
                    act.copy(kT[:, :, i * P:(i + 1) * P], ps_t[2][:, 0:2 * P].rearrange("p (j t) -> p j t", j=2)
                             ).then_inc(back_a, 1)

                for i in range(TILES):
                    act.wait_ge(done, i + 1)
                    if i >= 2:
                        act.wait_ge(turned, i - 1)
                    act.copy(line[i % 2][:, 0:512], ps[0][:])
                    act.copy(line[i % 2][:, 512:1024], ps[1][:]).then_inc(line_a, 1)
                    act.wait_ge(line_a, i + 1)
                    if i:
                        act.wait_ge(mean_done, i)
                    act.activation(square[:], line[i % 2][:, 0:NORMED], ACT.Square).then_inc(squared, 1)
                    act.wait_ge(mean_done, i + 1)
                    act.activation(stat[:, 2, :], stat[:, 1, :], ACT.Sqrt).then_inc(root_done, 1)
                    if i:
                        back(i - 1)
                back(TILES - 1)

            @block.vector
            def _(dve):
                ch = Chain(dve, chain)
                tt = dve.tensor_tensor

                def back(i):
                    dve.wait_ge(turned, i + 1)
                    dve.tensor_copy(qT[:, 1, :, i * P:(i + 1) * P], ps_t[1][:].rearrange("p (j t) -> p j t", j=4)
                                    ).then_inc(back_v, 1)

                dve.wait_ge(gains_in, 16 * (HEADS + 1))
                for i in range(TILES):
                    src = line[i % 2]
                    dve.wait_ge(done, i + 1)
                    if i >= 2:
                        dve.wait_ge(turned, i - 1)
                    dve.tensor_copy(src[:, 1024:QKV], ps[2][:, 0:QKV - 1024]).then_inc(line_v, 1)
                    dve.wait_ge(line_v, i + 1)
                    dve.wait_ge(line_a, i + 1)
                    ch.step(dve.tensor_copy(v_rows[:, i, :], src[:, AT_V:AT_V + HD]))
                    ch.step(dve.tensor_scalar(w_rows[:, i, :], src[:, AT_WI:AT_WI + HEADS], float(HEADS) ** -0.5, None,
                                              ALU.mult))
                    dve.wait_ge(squared, i + 1)
                    if i:
                        dve.wait_ge(root_done, i)
                    ch.step(dve.tensor_reduce(stat[:, 0, :], square[:].rearrange("p (h n) -> p h n", n=HD), AX, ALU.add))
                    dve.tensor_scalar(stat[:, 1, :], stat[:, 0, :], 1.0 / HD, EPS, ALU.mult, ALU.add).then_inc(mean_done, 1)
                    dve.wait_ge(root_done, i + 1)
                    ch.step(dve.reciprocal(stat[:, 0, :], stat[:, 2, :]))
                    heads = src[:, 0:NORMED].rearrange("p (h n) -> p h n", n=HD)
                    ch.step(tt(heads, heads, stat[:, 0, :].unsqueeze(2).broadcast_to([P, HEADS + 1, HD]), ALU.mult))
                    ch.step(tt(src[:, 0:NORMED], src[:, 0:NORMED], gains[:], ALU.mult))
                    rot = src[:].rearrange("p (b h n) -> p b h n", b=2, n=HD)[:, :, 0:HEADS + 1, :]
                    wave = lambda a: k.cos_sin[:, a, i, :].unsqueeze(1).unsqueeze(1).broadcast_to([P, 2, HEADS + 1, ROPE])
                    x1, x2 = rot[:, :, :, 0:ROPE], rot[:, :, :, ROPE:2 * ROPE]
                    tt(turn[:, 0], x1, wave(0), ALU.mult)
                    tt(turn[:, 1], x2, wave(1), ALU.mult)
                    tt(turn[:, 2], x1, wave(1), ALU.mult)
                    ch.step(tt(turn[:, 3], x2, wave(0), ALU.mult))
                    tt(x1, turn[:, 0], turn[:, 1], ALU.subtract)
                    ch.step(tt(x2, turn[:, 2], turn[:, 3], ALU.add))
                    dve.tensor_copy(src[:, AT_V:AT_V + HD], src[:, AT_V - HD:AT_V])
                    dve.tensor_copy(src[:, AT_WI:AT_WI + HD], src[:, AT_KI:AT_KI + HD]).then_inc(line_done, 1)
                    if i:
                        back(i - 1)
                back(TILES - 1)


def attention(k, qT, kT, v_rows, w_rows, mixT, w_ring):
    nc = k.nc
    FREE_TILES = TOPK // P
    jobs = []
    for i in range(TILES):
        if i >= FREE_TILES:
            jobs += [(i, h, True) for h in range(HEADS)]
        jobs += [(i, h, False) for h in range(HEADS)]
    index_of = {j: n for n, j in enumerate([j for j in jobs if j[2]])}
    att_of = {j: n for n, j in enumerate([j for j in jobs if not j[2]])}
    with ExitStack() as ctx:
        relu = [k.sb(f"a_relu{i}", [P, SEQ], ctx=ctx) for i in range(2)]
        total = k.sb("a_total", [P, SEQ], ctx=ctx)
        work = k.sb("a_work", [P, SEQ], ctx=ctx)
        top8 = k.sb("a_top8", [P, 8], ctx=ctx)
        bias = k.sb("a_bias", [P, SEQ], ctx=ctx)
        score = [k.sb(f"a_score{i}", [P, SEQ], ctx=ctx) for i in range(2)]
        prob = [k.sb(f"a_prob{i}", [P, SEQ], ctx=ctx) for i in range(2)]
        probT = [k.sb(f"a_probT{i}", [P, SEQ], ctx=ctx) for i in range(2)]
        stat = k.sb("a_stat", [P, 4, 2], ctx=ctx)
        out = k.sb("a_out", [P, HEADS * HD], ctx=ctx)
        ps_s = [k.ps(f"a_ps_s{i}", [P, 1024], ctx=ctx) for i in range(2)]
        ps_t = k.ps("a_ps_t", [P, 1024], ctx=ctx)
        ps_o = [k.ps(f"a_ps_o{i}", [P, 512], ctx=ctx) for i in range(2)]
        ps_m = ps_o[1]
        index_done, att_done, relu_done, added = (k.sem(f"a_{n}") for n in ("index_done", "att_done", "relu_done", "added"))
        scored, max_done, exp_done, turned, back = (k.sem(f"a_{n}") for n in ("scored", "max", "exp", "turned", "back"))
        inv_done, pv_done, out_done, out_turned, mixed = (k.sem(f"a_{n}") for n in
                                                         ("inv", "pv", "out", "out_turned", "mixed"))
        chain = k.sem("a_chain")
        mod_acc = k.sb("a_mod_acc", [P, 3, 3 * D], ctx=ctx)
        FOLDS = 3 * 6
        w_in, w_used = [k.sem(f"a_w_in{i}") for i in range(2)], k.sem("a_w_used")
        w_scaled, folded, raw_copied, raw_out = (k.sem(f"a_{n}") for n in ("w_scaled", "folded", "raw_copied", "raw_out"))
        with nc.Block() as block:

            @block.sync
            def _(sp):
                for n in range(3 * KS):
                    if n >= 2:
                        sp.wait_ge(w_used, n - 1)
                    sp.dma_start(w_ring[:, n % 2, :], mod_weights(k.ap, 1 + n // KS)[n % KS]).then_inc(w_in[n % 2], 16)
                for m in range(3):
                    sp.wait_ge(raw_copied, 6 * (m + 1))
                    sp.dma_start(k.mod_raw[m].unsqueeze(0), w_ring[0:1, m % 2, :]).then_inc(raw_out, 16)
                sp.wait_ge(raw_out, 3 * 16)

            @block.gpsimd
            def _(pool):
                for n in range(3 * KS):
                    acc, w = mod_acc[:, n // KS, :], w_ring[:, n % 2, :]
                    s = n % KS
                    pool.wait_ge(w_in[n % 2], 16 * (n // 2 + 1))
                    pool.tensor_scalar(w if s else acc, w, k.c_silu[:, s:s + 1], None, ALU.mult).then_inc(w_scaled, 1)
                    pool.wait_ge(w_scaled, n + 1)
                    if s:
                        pool.tensor_tensor(acc, acc, w, ALU.add).then_inc(w_used, 1)
                    else:
                        pool.sem_inc(w_used, 1)
                    pool.wait_ge(w_used, n + 1)

            @block.tensor
            def _(pe):
                def scores(n):
                    i, h, indexer = jobs[n]
                    nk = P * (i + 1)
                    if n >= 2:
                        last = jobs[n - 2]
                        if last[2]:
                            pe.wait_ge(relu_done, index_of[last] + 1)
                        else:
                            pe.wait_ge(scored, att_of[last] + 1)
                    half = slice((h % 2) * HD, (h % 2) * HD + HD)
                    which = 1 if indexer else 0
                    for lo in range(0, nk, 512):
                        hi = min(nk, lo + 512)
                        mm = pe.matmul(ps_s[n % 2][:, lo:hi], qT[half, which, h // 2, i * P:(i + 1) * P],
                                       kT[half, which, lo:hi], start=True, stop=True)
                    mm.then_inc(index_done if indexer else att_done, 1)

                def values(n):
                    a = att_of[jobs[n]]
                    i, h, _ = jobs[n]
                    pe.wait_ge(exp_done, a + 1)
                    if a:
                        pe.wait_ge(back, a)
                    for j in range(i + 1):
                        mm = pe.transpose(ps_t[:, j * P:(j + 1) * P], prob[a % 2][:, j * P:(j + 1) * P], k.c("ident"))
                    mm.then_inc(turned, 1)
                    pe.wait_ge(back, a + 1)
                    if a >= 2:
                        pe.wait_ge(out_done, a - 1)
                    if h == 1 and i:
                        pe.wait_ge(mixed, i)
                    for j in range(i + 1):
                        mm = pe.matmul(ps_o[a % 2][:, 0:HD], probT[a % 2][:, j * P:(j + 1) * P],
                                       v_rows[:, j, :], start=(j == 0), stop=(j == i))
                    mm.then_inc(pv_done, 1)
                    if h == HEADS - 1:
                        pe.wait_ge(out_done, a + 1)
                        for j in range(4):
                            mm = pe.transpose(ps_m[:, j * P:(j + 1) * P], out[:, j * P:(j + 1) * P], k.c("ident"))
                        mm.then_inc(out_turned, 1)

                def fold():
                    pe.wait_ge(w_used, 3 * KS)
                    pe.wait_ge(back, HEADS * (TILES - 1))
                    for n in range(FOLDS):
                        if n >= 2:
                            pe.wait_ge(raw_copied, n - 1)
                        pe.matmul(ps_t[0:1, n % 2 * 512:n % 2 * 512 + 512], k.ones[:],
                                  mod_acc[:, n // 6, n % 6 * 512:n % 6 * 512 + 512], start=True, stop=True
                                  ).then_inc(folded, 1)

                scores(0)
                for n in range(len(jobs)):
                    if n + 1 < len(jobs):
                        scores(n + 1)
                        if jobs[n + 1] == (TILES - 1, 0, False):
                            fold()
                    if not jobs[n][2]:
                        values(n)

            @block.scalar
            def _(act):
                for n, job in enumerate(jobs):
                    i, h, indexer = job
                    nk = P * (i + 1)
                    if indexer:
                        a = index_of[job]
                        act.wait_ge(index_done, a + 1)
                        if a >= 2:
                            act.wait_ge(added, a - 1)
                        act.activation(relu[a % 2][:, 0:nk], ps_s[n % 2][:, 0:nk], ACT.Relu, scale=float(HD) ** -0.5
                                       ).then_inc(relu_done, 1)
                        continue
                    a = att_of[job]
                    if (i, h) == (TILES - 1, 0):
                        for n_fold in range(FOLDS):
                            act.wait_ge(folded, n_fold + 1)
                            if n_fold == 12:
                                act.wait_ge(raw_out, 32)
                            act.copy(w_ring[0:1, n_fold // 6 % 2, n_fold % 6 * 512:n_fold % 6 * 512 + 512],
                                     ps_t[0:1, n_fold % 2 * 512:n_fold % 2 * 512 + 512]).then_inc(raw_copied, 1)
                    act.wait_ge(max_done, a + 1)
                    if a >= 2:
                        act.wait_ge(turned, a - 1)
                    act.activation(prob[a % 2][:, 0:nk], score[a % 2][:, 0:nk], ACT.Exp, bias=stat[:, 1, a % 2:a % 2 + 1],
                                   accum_out=stat[:, 2, a % 2:a % 2 + 1]).then_inc(exp_done, 1)
                    act.wait_ge(turned, a + 1)
                    if a >= 2:
                        act.wait_ge(pv_done, a - 1)
                    act.copy(probT[a % 2][:, 0:nk], ps_t[:, 0:nk]).then_inc(back, 1)

            @block.vector
            def _(dve):
                ch = Chain(dve, chain)

                def finish(a):
                    i, h = a // HEADS, a % HEADS
                    dve.wait_ge(exp_done, a + 1)
                    dve.reciprocal(stat[:, 3, a % 2:a % 2 + 1], stat[:, 2, a % 2:a % 2 + 1]).then_inc(inv_done, 1)
                    dve.wait_ge(inv_done, a + 1)
                    dve.wait_ge(pv_done, a + 1)
                    if h == 0 and i:
                        dve.wait_ge(out_turned, i)
                    dve.tensor_scalar(out[:, h * HD:(h + 1) * HD], ps_o[a % 2][:, 0:HD],
                                      stat[:, 3, a % 2:a % 2 + 1], None, ALU.mult).then_inc(out_done, 1)
                    if h == HEADS - 1:
                        dve.wait_ge(out_turned, i + 1)
                        dve.tensor_copy(mixT[:, :, i * P:(i + 1) * P], ps_m[:].rearrange("p (j t) -> p j t", j=4)
                                        ).then_inc(mixed, 1)

                for i in range(TILES):
                    nk = P * (i + 1)
                    own = slice(i * P, nk)
                    if i < FREE_TILES:
                        if i:
                            ch.step(dve.memset(bias[:, 0:i * P], 0.0))
                        ch.step(dve.tensor_scalar(bias[:, own], k.c("causal"), 8.0, None, ALU.mult))
                    else:
                        for h in range(HEADS):
                            a = index_of[(i, h, True)]
                            dve.wait_ge(relu_done, a + 1)
                            w = w_rows[:, i, h:h + 1]
                            if h == 0:
                                ins = dve.tensor_scalar(total[:, 0:nk], relu[a % 2][:, 0:nk], w, None, ALU.mult)
                            else:
                                ins = dve.scalar_tensor_tensor(total[:, 0:nk], relu[a % 2][:, 0:nk], w, total[:, 0:nk],
                                                               ALU.mult, ALU.add)
                            ins.then_inc(added, 1)
                            dve.wait_ge(added, a + 1)
                        ch.step(dve.tensor_tensor(total[:, own], total[:, own], k.c("causal"), ALU.add))
                        src = total
                        for _ in range(TOPK // 8):
                            ch.step(dve.max(top8[:], src[:, 0:nk]))
                            ch.step(dve.match_replace(work[:, 0:nk], top8[:], src[:, 0:nk], -3e38))
                            src = work
                        ch.step(dve.tensor_scalar(bias[:, 0:nk], work[:, 0:nk], -2e38, 8.0 * NEG, ALU.is_gt, ALU.mult))
                    for h in range(HEADS):
                        a = att_of[(i, h, False)]
                        n = jobs.index((i, h, False))
                        dve.wait_ge(att_done, a + 1)
                        if a >= 2:
                            dve.wait_ge(exp_done, a - 1)
                        dve.tensor_tensor_reduce(score[a % 2][:, 0:nk], ps_s[n % 2][:, 0:nk], bias[:, 0:nk],
                                                 float(HD) ** -0.5, -3e38, ALU.add, ALU.max, stat[:, 0, a % 2:a % 2 + 1]
                                                 ).then_inc(scored, 1)
                        dve.wait_ge(scored, a + 1)
                        dve.tensor_scalar(stat[:, 1, a % 2:a % 2 + 1], stat[:, 0, a % 2:a % 2 + 1], -1.0, None, ALU.mult
                                          ).then_inc(max_done, 1)
                        if h:
                            finish(a - 1)
                    finish(a)


def hybrid_out(k, mix_ssm, mix_att):
    nc, ap = k.nc, k.ap
    with ExitStack() as ctx:
        w = k.sb("o_w", [P, KS, D], ctx=ctx)
        gate = k.sb("o_gate", [P, D], ctx=ctx)
        part = k.sb("o_part", [P, 2, D], ctx=ctx)
        raw = k.sb("o_raw", [P, 3, 3, 8], ctx=ctx)
        bias = k.sb("o_bias", [P, 3, 3, 8], ctx=ctx)
        gain = k.sb("o_gain", [P, 3, 8], ctx=ctx)
        ps = [k.ps(f"o_ps{i}", [P, 1024], ctx=ctx) for i in range(2)]
        w_in, done, gated_done, x_done = (k.sem(f"o_{n}") for n in ("w_in", "done", "gated", "x_done"))
        small_in, x_in, rows_done, rows_out, chain = (k.sem(f"o_{n}") for n in
                                                      ("small_in", "x_in", "rows_done", "rows_out", "chain"))
        with nc.Block() as block:

            @block.sync
            def _(sp):
                with nc.allow_non_contiguous_dma(reason="modulation rows, eight columns a partition"):
                    for m in range(3):
                        which, layer = MOD_SOURCES[m + 1]
                        sp.dma_start(raw[:, m], k.mod_raw[m].rearrange("(j p c) -> p j c", j=3, c=8)).then_inc(small_in, 16)
                        sp.dma_start(bias[:, m], ap[which + "_mod_b"][layer].rearrange("(j p c) -> p j c", j=3, c=8)
                                     ).then_inc(small_in, 16)
                        sp.dma_start(gain[:, m], ap[which + "_norm_g"][layer].rearrange("(p c) -> p c", c=8)
                                     ).then_inc(small_in, 16)
                sp.dma_start(w[:], ap["hyb_w_out"][0].rearrange("(s p) n -> p s n", p=P)).then_inc(w_in, 16)
                sp.dma_start(gate[:], spread(k.mod[0, 2])).then_inc(w_in, 16)
                sp.dma_start(k.x[:], ap["x"][0].rearrange("(i p) d -> p i d", p=P)).then_inc(x_in, 16)
                sp.wait_ge(rows_done, 1)
                with nc.allow_non_contiguous_dma(reason="modulation rows, eight columns a partition"):
                    for src, dst in ((1, 0), (0, 1), (2, 2)):
                        for m in range(3):
                            sp.dma_start(k.mod[m + 1, dst].rearrange("(p c) -> p c", c=8), raw[:, m, src, :]
                                         ).then_inc(rows_out, 16)
                sp.wait_ge(rows_out, 9 * 16)

            @block.tensor
            def _(pe):
                pe.wait_ge(w_in, 32)
                for i in range(TILES):
                    if i >= 2:
                        pe.wait_ge(gated_done, i - 1)
                    for n in range(2):
                        for s in range(KS):
                            mix = mix_ssm if s < 4 else mix_att
                            mm = pe.matmul(ps[i % 2][:, n * 512:(n + 1) * 512], mix[:, s % 4, i * P:(i + 1) * P],
                                           w[:, s, n * 512:(n + 1) * 512], start=(s == 0), stop=(s == KS - 1))
                    mm.then_inc(done, 1)

            @block.vector
            def _(dve):
                ch = Chain(dve, chain)
                dve.wait_ge(small_in, 9 * 16)
                ch.step(dve.tensor_tensor(raw[:], raw[:], bias[:], ALU.add))
                dve.scalar_tensor_tensor(raw[:, :, 1, :], raw[:, :, 1, :], 1.0, gain[:], ALU.add, ALU.mult
                                         ).then_inc(rows_done, 1)
                dve.wait_ge(w_in, 32)
                dve.wait_ge(x_in, 16)
                for i in range(TILES):
                    dve.wait_ge(done, i + 1)
                    dve.tensor_tensor(part[:, i % 2], ps[i % 2][:], gate[:], ALU.mult).then_inc(gated_done, 1)
                    dve.wait_ge(gated_done, i + 1)
                    dve.tensor_tensor(k.x[:, i, :], k.x[:, i, :], part[:, i % 2], ALU.add).then_inc(x_done, 1)


def pool_mixer(k, h):
    nc, ap = k.nc, k.ap
    NW = len(WINDOWS)
    with ExitStack() as ctx:
        band = k.sb("l_band", [P, NW, 3, P], ctx=ctx)
        w = k.sb("l_w", [P, NW, 2, PG], ctx=ctx)
        gate = k.sb("l_gate", [P, D], ctx=ctx)
        scale = k.sb("l_scale", [P, D], ctx=ctx)
        pooled = [k.sb(f"l_pooled{i}", [P, KS, P], ctx=ctx) for i in range(2)]
        part = k.sb("l_part", [P, 2, D], ctx=ctx)
        ps_p = [k.ps(f"l_ps_p{i}", [P, 512], ctx=ctx) for i in range(2)]
        ps_y = [k.ps(f"l_ps_y{i}", [P, 1024], ctx=ctx) for i in range(2)]
        loaded, scaled, pool_done, pool_a, pool_v = (k.sem(f"l_{n}") for n in
                                                     ("loaded", "scaled", "pool_done", "pool_a", "pool_v"))
        done, gated_done, x_done = (k.sem(f"l_{n}") for n in ("done", "gated", "x_done"))
        with nc.Block() as block:

            @block.sync
            def _(sp):
                sp.dma_start(band[:].rearrange("p a b c -> p (a b c)"), ap["band"]).then_inc(loaded, 16)
                sp.dma_start(w[:].rearrange("p g c n -> p (g c) n"),
                             ap["pool_w"][0].rearrange("g (c p) n -> p (g c) n", p=P)).then_inc(loaded, 16)
                sp.dma_start(gate[:], spread(k.mod[2, 2])).then_inc(loaded, 16)
                sp.dma_start(scale[:], spread(ap["pool_scale"][0])).then_inc(loaded, 16)

            @block.tensor
            def _(pe):
                pe.wait_ge(loaded, 64)

                def pool(i):
                    if i:
                        pe.wait_ge(pool_a, i)
                        pe.wait_ge(pool_v, i)
                    for s in range(KS):
                        out = ps_p[s // 4][:, (s % 4) * P:(s % 4 + 1) * P]
                        cols = slice(s * P, (s + 1) * P)
                        mm = pe.matmul(out, h[:, i, cols], band[:, s // 2, 1 if i else 0, :], start=True, stop=(i == 0))
                        if i:
                            mm = pe.matmul(out, h[:, i - 1, cols], band[:, s // 2, 2, :], start=False, stop=True)
                    mm.then_inc(pool_done, 1)

                pool(0)
                for i in range(TILES):
                    pe.wait_ge(pool_a, i + 1)
                    pe.wait_ge(pool_v, i + 1)
                    if i + 1 < TILES:
                        pool(i + 1)
                    if i >= 2:
                        pe.wait_ge(gated_done, i - 1)
                    for g in range(NW):
                        for c in range(2):
                            mm = pe.matmul(ps_y[i % 2][:, g * PG:(g + 1) * PG], pooled[i % 2][:, 2 * g + c, :], w[:, g, c, :],
                                           start=(c == 0), stop=(c == 1))
                    mm.then_inc(done, 1)

            @block.scalar
            def _(act):
                for i in range(TILES):
                    act.wait_ge(pool_done, i + 1)
                    if i >= 2:
                        act.wait_ge(done, i - 1)
                    act.copy(pooled[i % 2][:, 0:4, :], ps_p[0][:].rearrange("p (s t) -> p s t", s=4)).then_inc(pool_a, 1)

            @block.vector
            def _(dve):
                dve.wait_ge(loaded, 64)
                dve.tensor_tensor(gate[:], gate[:], scale[:], ALU.mult).then_inc(scaled, 1)
                dve.wait_ge(scaled, 1)

                def pool_back(i):
                    dve.wait_ge(pool_done, i + 1)
                    if i >= 2:
                        dve.wait_ge(done, i - 1)
                    dve.tensor_copy(pooled[i % 2][:, 4:8, :], ps_p[1][:].rearrange("p (s t) -> p s t", s=4)
                                    ).then_inc(pool_v, 1)

                pool_back(0)
                for i in range(TILES):
                    if i + 1 < TILES:
                        pool_back(i + 1)
                    dve.wait_ge(done, i + 1)
                    dve.tensor_tensor(part[:, i % 2], ps_y[i % 2][:], gate[:], ALU.mult).then_inc(gated_done, 1)
                    dve.wait_ge(gated_done, i + 1)
                    dve.tensor_tensor(k.x[:, i, :], k.x[:, i, :], part[:, i % 2], ALU.add).then_inc(x_done, 1)


def hybrid_layer(k, ctx):
    uT = k.sb("uT", [P, GROUPS, CHUNKS], ctx=ctx)
    mix_ssm = k.sb("mix_ssm", [P, 4, SEQ], ctx=ctx)
    mix_att = uT[:].rearrange("p g c -> p (g c)").rearrange("p (s t) -> p s t", s=4)
    with ExitStack() as inner:
        hT = k.sb("hT", [P, KS, SEQ], ctx=inner)
        with ExitStack() as first:
            k.hold_x(first, "x_first")
            load_and_modulate(k)
            normalise(k, 0, None, "n0", True, hT=hT)
        with ExitStack() as heads:
            rotor, lam, mag = (k.sb(n, [P, 2, GROUPS], ctx=heads) for n in ("rotor", "lam", "mag"))
            dt = k.sb("dt", [P, GROUPS], ctx=heads)
            sine_tables(k, k.cos_sin, rotor, lam, dt, mag)
            u_rows = k.sb("u_rows", [P, GROUPS, CH, GH], ctx=heads)
            project_u(k, hT, u_rows, uT)
            s5(k, uT, u_rows[:], mix_ssm, rotor, lam, mag)
        v_rows = k.sb("v_rows", [P, TILES, HD], ctx=inner)
        w_rows = k.sb("w_rows", [P, TILES, HEADS], ctx=inner)
        qT = k.sb("qT", [P, 2, 4, SEQ], ctx=inner)
        kT = k.sb("kT", [P, 2, SEQ], ctx=inner)
        project_rest(k, hT, qT, kT, v_rows, w_rows)
        w_ring = hT[:].rearrange("p s t -> p (s t)")[:, 0:6 * D].rearrange("p (r n) -> p r n", r=2)
        attention(k, qT, kT, v_rows, w_rows, mix_att, w_ring)
    k.hold_x(ctx, "x0")
    hybrid_out(k, mix_ssm, mix_att)


def program(nc, ap, out):
    with ExitStack() as ctx:
        k = Core(nc, ctx, ap)
        with ExitStack() as part:
            routes = Routes(k, part, "m0")
            with ExitStack() as inner:
                hybrid_layer(k, inner)
                k.recycle()
                moe_front(k, 0, 1, "m0", routes)
            experts(k, 0, routes, "m0_e")
        k.recycle()
        with ExitStack() as part:
            routes = Routes(k, part, "m1")
            with ExitStack() as inner:
                k.hold_x(inner, "x1")
                moe_residual(k, 0, 1, "m0_x")
                with ExitStack() as mixer:
                    h = k.sb("h1", [P, TILES, D], ctx=mixer)
                    normalise(k, 2, h, "n1", False)
                    pool_mixer(k, h)
                moe_front(k, 1, 3, "m1", routes)
            k.recycle()
            experts(k, 1, routes, "m1_e")
        with ExitStack() as part:
            k.hold_x(part, "x2")
            moe_residual(k, 1, 3, "m1_x", out=out[0])


_INS = ["x", "c", "positions", "mix_norm_g", "mix_mod_w", "mix_mod_b", "ffn_norm_g", "ffn_mod_w", "ffn_mod_b",
        "hyb_w_in", "hyb_w_out", "s5_lambda_re", "s5_lambda_im", "s5_log_dt", "s5_b_re", "s5_b_im", "s5_c_re",
        "s5_c_im", "s5_d", "s5_glu_w", "s5_glu_b", "attn_q_norm_g", "attn_k_norm_g", "pool_w", "pool_scale",
        "router_w", "router_bias", "exp_w_gate", "exp_w_up", "exp_w_down", "sh_w_gate", "sh_w_up", "sh_w_down"]


def kernel(**inputs):
    import concourse.bacc as bacc
    from concourse.bass_utils import run_bass_kernel_spmd

    nc = bacc.Bacc("TRN2", target_bir_lowering=False, num_devices=1)
    arrays, ap = {}, {}
    given = {n: np.ascontiguousarray(inputs[n]) for n in _INS}
    for name, a in {**given, "const": CONST, "band": BAND}.items():
        arrays[f"in_{name}"] = a
        ap[name] = nc.dram_tensor(f"in_{name}", a.shape, mybir.dt.from_np(a.dtype), kind="ExternalInput").ap()
    out = nc.dram_tensor("out_x", (1, SEQ, D), F32, kind="ExternalOutput").ap()
    program(nc, ap, out)
    r = run_bass_kernel_spmd(nc, [arrays], core_ids=[0])
    return r.results[0]["out_x"]
```

```python
from contextlib import ExitStack, nullcontext

import numpy as np

import concourse.bass as bass
from concourse import mybir

F32 = mybir.dt.float32
BF16 = mybir.dt.bfloat16
F32R = mybir.dt.float32r
I32 = mybir.dt.int32
U32 = mybir.dt.uint32
ALU = mybir.AluOpType
ACT = mybir.ActivationFunctionType
AX = mybir.AxisListType.X

P = 128
D = 1024
SEQ = 1024
TILES = SEQ // P
KS = D // P
EPS = 1e-6

GROUPS, GH, NS = 32, 16, 64
CH = P // GH
CHUNKS = SEQ // CH
HALF_G = GROUPS // 2

HEADS, HD = 8, 64
TOPK = 256
ROPE = 8
QKV = 1224
REST = 1280

WINDOWS = (2, 4, 8, 16)
PG = D // len(WINDOWS)

E, TK, F = 64, 8, 256
BLOCKS = 128
LOOKED = BLOCKS + 2
SURE = SEQ * TK // P
NEG = -1e30

TWO_PI = 2.0 * np.pi
PI_A = float(np.float32(6.28125))
PI_B = float(np.float32(TWO_PI - 6.28125))
PI_C = float(np.float32(TWO_PI - 6.28125 - float(np.float32(TWO_PI - 6.28125))))


def constants():
    i = np.arange(P)
    parts = {
        "ident": np.eye(P),
        "iota": np.tile(i, (P, 1)),
        "before": (i[:, None] < i[None, :]) * 1.0,
        "causal": np.where(i[None, :] <= i[:, None], 0.0, NEG),
        "swap": np.eye(P)[(i + NS) % P],
        "row": i[:, None] * 1.0,
        "token1": i[:, None] + P * np.arange(TILES)[None, :] + 1.0,
        "padrow": i[:, None] + SEQ + 1.0,
        "tie": np.tile((np.arange(8)[None, :] < np.arange(8)[:, None]).reshape(1, 64) * 1.0, (P, 1)),
        "freq": np.tile(np.power(np.float32(500000.0), -np.arange(0, 16, 2, dtype=np.float32) / 16), (P, 1)),
    }
    at, n, cols = {}, 0, []
    for name, a in parts.items():
        at[name] = (n, n + a.shape[1])
        n += a.shape[1]
        cols.append(a.astype(np.float32))
    return np.ascontiguousarray(np.concatenate(cols, 1)), at


def bands():
    out = np.zeros((P, len(WINDOWS), 3, P), np.float32)
    for w, win in enumerate(WINDOWS):
        for t in range(P):
            for back in range(win):
                s = t - back
                if s >= 0:
                    out[s, w, 0, t] = 1.0 / min(win, t + 1)
                    out[s, w, 1, t] = 1.0 / win
                else:
                    out[s + P, w, 2, t] = 1.0 / win
            out[t, w, 0, t] -= 1.0
            out[t, w, 1, t] -= 1.0
    return out.reshape(P, -1)


CONST, AT = constants()
BAND = bands()


class Chain:

    def __init__(self, eng, sem):
        self.eng, self.sem, self.n = eng, sem, 0

    def step(self, ins):
        self.n += 1
        ins.then_inc(self.sem, 1)
        self.eng.wait_ge(self.sem, self.n)


def spread(row, n=P):
    return row.partition_broadcast(n)


class Core:

    def __init__(self, nc, ctx, ap):
        self.nc, self.ctx, self.ap = nc, ctx, ap
        self.sems = []
        self.x = None
        self.cst = self.sb("cst", [P, CONST.shape[1]])
        self.cos_sin = self.sb("cos_sin", [P, 2, TILES, ROPE])
        self.c_silu = self.sb("c_silu", [P, KS])
        self.ones = self.sb("ones", [P, 1])
        self.squares = self.sb("x_squares", [P, TILES])
        self.mod = nc.dram_tensor("mod_rows", (4, 3, D), F32).ap()
        self.mod_raw = nc.dram_tensor("mod_raw", (3, 3 * D), F32).ap()
        self.x_rows = nc.dram_tensor("x_rows", (SEQ, D), F32).ap()
        self.h_rows = nc.dram_tensor("h_rows", (SEQ + P, D), F32).ap()
        self.moe_acc = [nc.dram_tensor(f"moe_acc{i}", (SEQ + P, D), F32).ap() for i in range(2)]

    def sb(self, name, shape, dt=F32, ctx=None):
        return (ctx or self.ctx).enter_context(self.nc.sbuf_tensor(name, shape, dt))

    def ps(self, name, shape, dt=F32, ctx=None):
        return (ctx or self.ctx).enter_context(self.nc.psum_tensor(name, shape, dt))

    def hold_x(self, ctx, name):
        self.x = self.sb(name, [P, TILES, D], ctx=ctx)

    def sem(self, name):
        self.sems.append(self.nc.alloc_semaphore(name))
        return self.sems[-1]

    def sum_squares(self, act, scratch, ready, last):
        for i in range(TILES):
            act.wait_ge(ready, i + 1)
            if i:
                act.wait_ge(last, i)
            act.activation(scratch, self.x[:, i, :], ACT.Square, accum_out=self.squares[:, i:i + 1]).then_inc(last, 1)

    def recycle(self):
        self.nc.clear_and_free_semaphores(self.sems)
        self.nc.all_engine_barrier()
        self.sems = []

    def c(self, name):
        a, b = AT[name]
        return self.cst[:, a:b]


MOD_SOURCES = (("mix", 0), ("ffn", 0), ("mix", 1), ("ffn", 1))


def mod_weights(ap, m):
    which, layer = MOD_SOURCES[m]
    return ap[which + "_mod_w"][layer].rearrange("(p k) n -> k p n", k=KS)


def load_and_modulate(k):
    nc, ap = k.nc, k.ap
    RING = 3
    with ExitStack() as ctx:
        c_col = k.sb("c_col", [P, KS], ctx=ctx)
        ring = k.sb("mod_w_ring", [P, RING, 3 * D], ctx=ctx)
        acc = k.sb("mod_acc", [P, 3 * D], ctx=ctx)
        bias = k.sb("mod_bias", [1, 3 * D], ctx=ctx)
        gain = k.sb("mod_gain", [1, D], ctx=ctx)
        row = k.sb("mod_row", [1, 3 * D], ctx=ctx)
        scratch = k.sb("mod_scratch", [P, D], ctx=ctx)
        total = [k.ps(f"mod_total{i}", [P, 512], ctx=ctx) for i in range(6)]
        small_in, x_in = k.sem("mod_small_in"), k.sem("x_in")
        w_in = [k.sem(f"mod_w_in{i}") for i in range(RING)]
        silu_done, w_used = k.sem("c_silu_done"), k.sem("mod_w_used")
        summed, row_out = k.sem("mod_summed"), k.sem("mod_row_out")
        row_done, chain, squared = k.sem("mod_row_done"), k.sem("mod_chain"), k.sem("mod_squared")
        with nc.Block() as block:

            @block.sync
            def _(sp):
                sp.dma_start(c_col[:], ap["c"][0].rearrange("(p k) -> p k", k=KS)).then_inc(small_in, 16)
                sp.dma_start(k.cst[:], ap["const"]).then_inc(small_in, 16)
                sp.dma_start(bias[:], ap["mix_mod_b"][0].unsqueeze(0)).then_inc(small_in, 16)
                sp.dma_start(gain[:], ap["mix_norm_g"][0].unsqueeze(0)).then_inc(small_in, 16)
                sp.dma_start(k.x[:], ap["x"][0].rearrange("(i p) d -> p i d", p=P)).then_inc(x_in, 16)
                rows = mod_weights(ap, 0)
                for s in range(KS):
                    if s >= RING:
                        sp.wait_ge(w_used, s - RING + 1)
                    sp.dma_start(ring[:, s % RING, :], rows[s]).then_inc(w_in[s % RING], 16)
                sp.wait_ge(x_in, 16)
                sp.wait_ge(row_out, 16)

            @block.scalar
            def _(act):
                act.wait_ge(small_in, 4 * 16)
                nc.scalar.activation(k.c_silu[:], c_col[:], ACT.Silu).then_inc(silu_done, 1)
                act.wait_ge(x_in, 16)
                for i in range(TILES):
                    if i:
                        act.wait_ge(squared, i)
                    act.activation(scratch[:], k.x[:, i, :], ACT.Square, accum_out=k.squares[:, i:i + 1]
                                   ).then_inc(squared, 1)
                act.wait_ge(row_done, 1)
                act.dma_start(k.mod[0].unsqueeze(0), row[:].rearrange("a (j d) -> a j d", j=3)).then_inc(row_out, 16)

            @block.vector
            def _(dve):
                ch = Chain(dve, chain)
                ch.step(nc.vector.memset(k.ones[:], 1.0))
                dve.wait_ge(silu_done, 1)
                for s in range(KS):
                    dve.wait_ge(w_in[s % RING], 16 * (s // RING + 1))
                    c = k.c_silu[:, s:s + 1]
                    if s == 0:
                        ins = nc.vector.tensor_scalar(acc[:], ring[:, s % RING, :], c, None, ALU.mult)
                    else:
                        dve.wait_ge(w_used, s)
                        ins = nc.vector.scalar_tensor_tensor(acc[:], ring[:, s % RING, :], c, acc[:], ALU.mult, ALU.add)
                    ins.then_inc(w_used, 1)
                dve.wait_ge(summed, 1)
                for i, (src, dst) in enumerate([(0, 1), (1, 0), (2, 2)]):
                    for h in range(2):
                        lo = src * D + h * 512
                        ins = nc.vector.tensor_tensor(row[:, dst * D + h * 512:dst * D + h * 512 + 512],
                                                      total[2 * src + h][0:1, :], bias[:, lo:lo + 512], ALU.add)
                ch.step(ins)
                ch.step(nc.vector.tensor_scalar(row[:, 0:D], row[:, 0:D], 1.0, None, ALU.add))
                nc.vector.tensor_tensor(row[:, 0:D], row[:, 0:D], gain[:], ALU.mult).then_inc(row_done, 1)

            @block.tensor
            def _(pe):
                pe.wait_ge(chain, 1)
                pe.wait_ge(w_used, KS)
                for i in range(6):
                    mm = nc.tensor.matmul(total[i][0:1, :], k.ones[:], acc[:, 512 * i:512 * i + 512],
                                          start=True, stop=True)
                mm.then_inc(summed, 1)


def normalise(k, m, h_out, name, permuted, hT=None, rows_out=False, extra=None):
    nc = k.nc
    with ExitStack() as ctx:
        gain = k.sb(name + "_gain", [P, D], ctx=ctx)
        shift = k.sb(name + "_shift", [P, D], ctx=ctx)
        scaled_x = k.sb(name + "_scaled_x", [P, D], ctx=ctx)
        stat = k.sb(name + "_stat", [P, 3, TILES], ctx=ctx)
        own = None if h_out is not None else k.sb(name + "_h", [P, 2, D], ctx=ctx)
        bank = [k.ps(f"{name}_bank{i}", [P, 512], ctx=ctx) for i in range(4)]
        rows_in = k.sem(name + "_rows_in")
        mean_done, root_done, inv_done = k.sem(name + "_mean"), k.sem(name + "_root"), k.sem(name + "_inv")
        scaled, h_done = k.sem(name + "_scaled"), k.sem(name + "_h_done")
        turned, copied = k.sem(name + "_turned"), k.sem(name + "_copied")
        stored = [k.sem(f"{name}_stored{i}") for i in range(2)] if rows_out else None

        def h(i):
            return h_out[:, i, :] if h_out is not None else own[:, i % 2, :]

        with nc.Block() as block:

            @block.sync
            def _(sp):
                sp.dma_start(gain[:], spread(k.mod[m, 0])).then_inc(rows_in, 16)
                sp.dma_start(shift[:], spread(k.mod[m, 1])).then_inc(rows_in, 16)
                if extra is not None:
                    extra(sp)
                if rows_out:
                    for i in range(TILES):
                        sp.wait_ge(h_done, i + 1)
                        sp.dma_start(k.h_rows[i * P:(i + 1) * P, :], h(i)).then_inc(stored[i % 2], 16)
                    for sem in stored:
                        sp.wait_ge(sem, 16 * (TILES // 2))

            @block.scalar
            def _(act):
                act.wait_ge(mean_done, 1)
                nc.scalar.activation(stat[:, 2, :], stat[:, 1, :], ACT.Sqrt).then_inc(root_done, 1)
                if hT is not None:
                    for i in range(TILES):
                        for half in range(2):
                            act.wait_ge(turned, 2 * i + half + 1)
                            act.copy(hT[:, 4 * half:4 * half + 4, i * P:(i + 1) * P],
                                     bank[2 * (i % 2) + half][:].rearrange("p (s t) -> p s t", s=4)).then_inc(copied, 1)

            @block.vector
            def _(dve):
                nc.vector.tensor_scalar(stat[:, 1, :], k.squares[:], 1.0 / D, EPS, ALU.mult,
                                        ALU.add).then_inc(mean_done, 1)
                dve.wait_ge(root_done, 1)
                nc.vector.reciprocal(stat[:, 0, :], stat[:, 2, :]).then_inc(inv_done, 1)
                dve.wait_ge(inv_done, 1)
                dve.wait_ge(rows_in, 32)

                for i in range(TILES):
                    if h_out is None and i >= 2:
                        if hT is not None:
                            dve.wait_ge(turned, 2 * (i - 1))
                        if rows_out:
                            dve.wait_ge(stored[i % 2], 16 * (i // 2))
                    nc.vector.scalar_tensor_tensor(scaled_x[:], k.x[:, i, :], stat[:, 0, i:i + 1], gain[:],
                                                   ALU.mult, ALU.mult).then_inc(scaled, 1)
                    dve.wait_ge(scaled, i + 1)
                    if permuted:
                        out = h(i).rearrange("t (s p) -> t p s", s=KS)
                        a = scaled_x[:].rearrange("t (p s) -> t p s", s=KS)
                        b = shift[:].rearrange("t (p s) -> t p s", s=KS)
                    else:
                        out, a, b = h(i), scaled_x[:], shift[:]
                    nc.vector.tensor_tensor(out, a, b, ALU.add).then_inc(h_done, 1)
                    dve.wait_ge(h_done, i + 1)

            @block.tensor
            def _(pe):
                if hT is None:
                    return
                for i in range(TILES):
                    pe.wait_ge(h_done, i + 1)
                    if i >= 2:
                        pe.wait_ge(copied, 2 * (i - 1))
                    for half in range(2):
                        for s in range(4):
                            mm = nc.tensor.transpose(bank[2 * (i % 2) + half][:, s * P:(s + 1) * P],
                                                     h(i)[:, (4 * half + s) * P:(4 * half + s + 1) * P], k.c("ident"))
                        mm.then_inc(turned, 1)


class Routes:

    def __init__(self, k, ctx, name):
        row = lambda n, size=LOOKED: k.sb(f"{name}_{n}", [1, size], I32, ctx=ctx)
        self.token = k.sb(name + "_slot_token", [P, LOOKED], U32, ctx=ctx)
        self.weight = k.sb(name + "_slot_weight", [P, LOOKED], ctx=ctx)
        self.number = row("block_number")
        self.following = row("following")
        self.expert = row("ordinal_expert", P)
        self.count = row("counts", 2)


def route_and_share(k, layer, hT, routes, name, spilled):
    nc, ap = k.nc, k.ap
    acc = k.moe_acc[layer]
    TE = TILES * E
    SHARED_FIRST = 3
    with ExitStack() as ctx:
        w = k.sb(name + "_w", [P, KS, E], ctx=ctx)
        bias = k.sb(name + "_bias", [P, E], ctx=ctx)
        score, sel, mask = (k.sb(f"{name}_{n}", [P, TE], ctx=ctx) for n in ("score", "sel", "mask"))
        tmp, tmp2 = (k.sb(f"{name}_{n}", [P, TE], ctx=ctx) for n in ("tmp", "tmp2"))
        best2 = k.sb(name + "_best2", [P, TE], ctx=ctx)
        group = k.sb(name + "_group", [P, 64], ctx=ctx)
        rank = k.sb(name + "_rank", [P, 64], ctx=ctx)
        top8 = k.sb(name + "_top8", [P, TILES, TK], ctx=ctx)
        total = k.sb(name + "_total", [P, TILES], ctx=ctx)
        mask16 = k.sb(name + "_mask16", [P, TILES, E], BF16, ctx=ctx)
        seen16 = k.sb(name + "_seen16", [P, TILES + 1, E], BF16, ctx=ctx)
        before16 = k.sb(name + "_before16", [P, P], BF16, ctx=ctx)
        ones16 = k.sb(name + "_ones16", [P, P], BF16, ctx=ctx)
        ones64 = k.sb(name + "_ones64", [P, E], ctx=ctx)
        whole = k.sb(name + "_whole", [P, TE], I32, ctx=ctx)
        nblk, end, start = (k.sb(f"{name}_{n}", [P, E], ctx=ctx) for n in ("nblk", "end", "start"))
        col = k.sb(name + "_col", [P, 2], ctx=ctx)
        holds, held = (k.sb(f"{name}_{n}", [P, E], ctx=ctx) for n in ("holds", "held"))
        line = k.sb(name + "_line", [1, 8, BLOCKS], ctx=ctx)
        slot_p, slot_b, weight8 = (k.sb(f"{name}_{n}", [P, 64], ctx=ctx) for n in ("slot_p", "slot_b", "weight8"))
        eq = k.sb(name + "_eq", [P, TK, E], ctx=ctx)
        hot_p = k.sb(name + "_hot_p", [P, 2, TK, P], ctx=ctx)
        hot_b = k.sb(name + "_hot_b", [P, 2, TK, 2, P], ctx=ctx)
        blocks = k.sb(name + "_blocks", [P, TK, P], ctx=ctx)
        pad = k.sb(name + "_pad", [P, BLOCKS], ctx=ctx)
        ps_logit = k.ps(name + "_ps_logit", [P, TE], ctx=ctx)
        ps_rank = k.ps(name + "_ps_rank", [P, TE], ctx=ctx)
        ps_table = k.ps(name + "_ps_table", [P, 512], ctx=ctx)
        ps_count, ps_line = ps_table, ps_table[:, 256:512]
        wg, wu = (k.sb(f"{name}_{n}", [P, KS, F], ctx=ctx) for n in ("wg", "wu"))
        wd = k.sb(name + "_wd", [P, 2, D], ctx=ctx)
        silu, up, hidden = (k.sb(f"{name}_{n}", [P, F], ctx=ctx) for n in ("silu", "up", "hidden"))
        hidT = k.sb(name + "_hidT", [P, 2, P], ctx=ctx)
        y = k.sb(name + "_y", [P, 2, D], ctx=ctx)
        zero = k.sb(name + "_zero", [P, D], ctx=ctx)
        ps_gu = k.ps(name + "_ps_gu", [P, 512], ctx=ctx)
        ps_t = k.ps(name + "_ps_t", [P, 512], ctx=ctx)
        ps_y = k.ps(name + "_ps_y", [P, 1024], ctx=ctx)
        sw_in, gu_done, silu_done, hid_done = (k.sem(f"{name}_{n}") for n in ("sw_in", "gu", "silu", "hid"))
        turned, hidT_done, y_done = (k.sem(f"{name}_{n}") for n in ("turned", "hidT", "y_done"))
        y_back, zeroed, zero_out = (k.sem(f"{name}_{n}") for n in ("y_back", "zeroed", "zero_out"))
        y_out = [k.sem(f"{name}_y_out{i}") for i in range(2)]
        w_in, logits, scored = k.sem(name + "_w_in"), k.sem(name + "_logits"), k.sem(name + "_scored")
        masked, ranked, col_done, lined = (k.sem(f"{name}_{n}") for n in ("masked", "ranked", "col", "lined"))
        hot, tabled, chain = k.sem(name + "_hot"), k.sem(name + "_tabled"), k.sem(name + "_chain")

        def grid(t):
            return t[:].rearrange("p (i e) -> p i e", i=TILES)

        with nc.Block() as block:

            @block.sync
            def _(sp):
                sp.dma_start(w[:], ap["router_w"][layer].rearrange("(p s) e -> p s e", s=KS)).then_inc(w_in, 16)
                sp.dma_start(bias[:], spread(ap["router_bias"][layer])).then_inc(w_in, 16)
                sp.dma_start(wg[:], ap["sh_w_gate"][layer].rearrange("(p s) f -> p s f", s=KS)).then_inc(sw_in, 16)
                sp.dma_start(wu[:], ap["sh_w_up"][layer].rearrange("(p s) f -> p s f", s=KS)).then_inc(sw_in, 16)
                sp.dma_start(wd[:], ap["sh_w_down"][layer].rearrange("(p c) n -> p c n", c=2)).then_inc(sw_in, 16)
                sp.wait_ge(zeroed, 1)
                sp.dma_start(acc[SEQ:SEQ + P, :], zero[:]).then_inc(zero_out, 16)
                sp.dma_start(k.h_rows[SEQ:SEQ + P, :], zero[:]).then_inc(zero_out, 16)
                for i in range(TILES):
                    sp.wait_ge(y_back, i + 1)
                    sp.dma_start(acc[i * P:(i + 1) * P, :], y[:, i % 2, :]).then_inc(y_out[i % 2], 16)
                for sem in y_out:
                    sp.wait_ge(sem, 16 * (TILES // 2))
                sp.wait_ge(zero_out, 32)
                sp.wait_ge(spilled, 16)

            @block.gpsimd
            def _(pool):
                pool.memset(zero[:], 0.0).then_inc(zeroed, 1)
                for i in range(TILES):
                    pool.wait_ge(silu_done, i + 1)
                    if i:
                        pool.wait_ge(turned, i)
                    pool.tensor_tensor(hidden[:].rearrange("t (c p) -> t p c", c=2),
                                       silu[:].rearrange("t (p c) -> t p c", c=2),
                                       up[:].rearrange("t (p c) -> t p c", c=2), ALU.mult).then_inc(hid_done, 1)

            @block.scalar
            def _(act):
                act.wait_ge(logits, 1)
                nc.scalar.activation(score[:], ps_logit[:], ACT.Sigmoid).then_inc(scored, 1)

                def back(i):
                    act.wait_ge(turned, i + 1)
                    act.copy(hidT[:], ps_t[:, 0:2 * P].rearrange("p (c t) -> p c t", c=2)).then_inc(hidT_done, 1)
                    act.wait_ge(y_done, i + 1)
                    if i >= 2:
                        act.wait_ge(y_out[i % 2], 16 * (i // 2))
                    act.copy(y[:, i % 2, :], ps_y[:]).then_inc(y_back, 1)

                for i in range(TILES):
                    act.wait_ge(gu_done, i + 1)
                    if i:
                        act.wait_ge(hid_done, i)
                    act.copy(up[:], ps_gu[:, F:2 * F])
                    act.activation(silu[:], ps_gu[:, 0:F], ACT.Silu).then_inc(silu_done, 1)
                    if i:
                        back(i - 1)
                back(TILES - 1)

            @block.tensor
            def _(pe):
                def shared_gate_up(i):
                    if i:
                        pe.wait_ge(silu_done, i)
                    for half, weights in enumerate((wg, wu)):
                        for s in range(KS):
                            mm = pe.matmul(ps_gu[:, half * F:(half + 1) * F], hT[:, s, i * P:(i + 1) * P],
                                           weights[:, s, :], start=(s == 0), stop=(s == KS - 1))
                    mm.then_inc(gu_done, 1)

                def shared_down(i):
                    pe.wait_ge(hid_done, i + 1)
                    for c in range(2):
                        mm = pe.transpose(ps_t[:, c * P:(c + 1) * P], hidden[:, c * P:(c + 1) * P], k.c("ident"))
                    mm.then_inc(turned, 1)
                    pe.wait_ge(hidT_done, i + 1)
                    if i:
                        pe.wait_ge(y_back, i)
                    for n in range(2):
                        for c in range(2):
                            mm = pe.matmul(ps_y[:, n * 512:(n + 1) * 512], hidT[:, c, :], wd[:, c, n * 512:(n + 1) * 512],
                                           start=(c == 0), stop=(c == 1))
                    mm.then_inc(y_done, 1)

                def shared(tiles):
                    for i in tiles:
                        if i < TILES:
                            shared_gate_up(i)
                        if i:
                            shared_down(i - 1)

                pe.wait_ge(w_in, 32)
                for i in range(TILES):
                    for s in range(KS):
                        mm = nc.tensor.matmul(ps_logit[:, i * E:(i + 1) * E], hT[:, s, i * P:(i + 1) * P], w[:, s, :],
                                              start=(s == 0), stop=(s == KS - 1))
                mm.then_inc(logits, 1)
                pe.wait_ge(sw_in, 48)
                shared(range(SHARED_FIRST))
                pe.wait_ge(masked, 1)
                for i in range(TILES):
                    out = ps_rank[:, i * E:(i + 1) * E]
                    nc.tensor.matmul(out, before16[:], mask16[:, i, :], start=True, stop=False)
                    nc.tensor.matmul(out, ones16[:], seen16[:, i, :], start=False, stop=True)
                nc.tensor.matmul(ps_count[:, 0:E], ones16[:], seen16[:, TILES, :], start=True,
                                 stop=True).then_inc(ranked, 1)
                pe.wait_ge(col_done, 1)
                for n in range(2):
                    mm = nc.tensor.matmul(ps_line[0:1, n * P:(n + 1) * P], col[:, n:n + 1], k.c("ident"), start=True,
                                          stop=True)
                mm.then_inc(lined, 1)
                shared(range(SHARED_FIRST, TILES + 1))
                for i in range(TILES):
                    pe.wait_ge(hot, i + 1)
                    for j in range(TK):
                        mm = nc.tensor.matmul(ps_table[:, 0:2 * P], hot_p[:, i % 2, j, :],
                                              hot_b[:, i % 2, j, :, :].rearrange("p a b -> p (a b)"),
                                              start=(i == 0 and j == 0), stop=(i == TILES - 1 and j == TK - 1))
                    mm.then_inc(tabled, 1)

            @block.vector
            def _(dve):
                v = nc.vector
                ch = Chain(dve, chain)
                ch.step(v.memset(ones16[:], 1.0))
                ch.step(v.memset(ones64[:], 1.0))
                ch.step(v.memset(seen16[:, 0, :], 0.0))
                ch.step(v.tensor_copy(before16[:], k.c("before")))
                dve.wait_ge(w_in, 32)
                dve.wait_ge(scored, 1)
                ch.step(v.tensor_tensor(grid(sel), grid(score), bias[:].unsqueeze(1).broadcast_to([P, TILES, E]), ALU.add))
                for n in range(64):
                    ins = v.max(best2[:, n * 8:n * 8 + 8], sel[:, n * 8:n * 8 + 8])
                ch.step(ins)
                best = best2[:].rearrange("p (n j) -> p n j", j=8)
                ch.step(v.tensor_tensor(group[:].unsqueeze(2), best[:, :, 0:1], best[:, :, 1:2], ALU.add))
                other = group[:].rearrange("p (i g) -> p i g", g=8).unsqueeze(2).broadcast_to([P, 8, 8, 8])
                mine = group[:].rearrange("p (i g) -> p i g", g=8).unsqueeze(3).broadcast_to([P, 8, 8, 8])
                four = lambda t: t[:].rearrange("p (i g h) -> p i g h", g=8, h=8)
                ch.step(v.tensor_tensor(four(tmp), other, mine, ALU.is_gt))
                ch.step(v.tensor_tensor(four(tmp2), other, mine, ALU.is_equal))
                ch.step(v.tensor_tensor(grid(tmp2), grid(tmp2), k.c("tie").unsqueeze(1).broadcast_to([P, TILES, 64]), ALU.mult))
                ch.step(v.tensor_tensor(tmp[:], tmp[:], tmp2[:], ALU.add))
                ch.step(v.tensor_reduce(rank[:], tmp[:].rearrange("p (n j) -> p n j", j=8), AX, ALU.add))
                ch.step(v.tensor_scalar(rank[:], rank[:], 3.5, None, ALU.is_lt))
                wide = rank[:].unsqueeze(2).broadcast_to([P, 64, 8])
                eight = lambda t: t[:].rearrange("p (n j) -> p n j", j=8)
                ch.step(v.tensor_tensor(eight(sel), eight(sel), wide, ALU.mult))
                ch.step(v.tensor_scalar(rank[:], rank[:], -NEG, NEG, ALU.mult, ALU.add))
                ch.step(v.tensor_tensor(eight(sel), eight(sel), wide, ALU.add))
                for i in range(TILES):
                    ins = v.max(top8[:, i, :], sel[:, i * E:(i + 1) * E])
                ch.step(ins)
                for i in range(TILES):
                    ins = v.match_replace(tmp[:, i * E:(i + 1) * E], top8[:, i, :], sel[:, i * E:(i + 1) * E], -3e38)
                ch.step(ins)
                ch.step(v.tensor_scalar(mask[:], tmp[:], -2e38, None, ALU.is_lt))
                ch.step(v.tensor_copy(mask16[:], grid(mask)))
                for i in range(TILES):
                    ins = v.tensor_tensor(seen16[:, i + 1, :], seen16[:, i, :], mask16[:, i, :], ALU.add)
                    if i < TILES - 1:
                        ch.step(ins)
                ins.then_inc(masked, 1)
                ch.step(v.tensor_tensor(score[:], score[:], mask[:], ALU.mult))
                ch.step(v.tensor_reduce(total[:], grid(score), AX, ALU.add))
                ch.step(v.reciprocal(total[:], total[:]))
                ch.step(v.tensor_scalar(total[:], total[:], 2.5, None, ALU.mult))
                ch.step(v.tensor_tensor(grid(score), grid(score), total[:].unsqueeze(2).broadcast_to([P, TILES, E]), ALU.mult))
                dve.wait_ge(ranked, 1)
                ch.step(v.tensor_scalar(whole[:, 0:E], ps_count[:, 0:E], 1.0 / P, 127.0 / 256, ALU.mult, ALU.add))
                ch.step(v.tensor_copy(nblk[:], whole[:, 0:E]))
                ch.step(v.tensor_tensor_scan(end[:], ones64[:], nblk[:], 0.0, ALU.mult, ALU.add))
                ch.step(v.tensor_tensor(start[:], end[:], nblk[:], ALU.subtract))
                ch.step(v.tensor_scalar(holds[:], nblk[:], 0.0, None, ALU.is_gt))
                ch.step(v.tensor_tensor_scan(held[:], ones64[:], holds[:], 0.0, ALU.mult, ALU.add))
                ch.step(v.tensor_scalar(ones64[:], end[:], k.c("row"), 0.0, ALU.is_le, ALU.add, accum_out=col[:, 0:1]))
                ch.step(v.tensor_scalar(ones64[:], held[:], k.c("row"), 0.0, ALU.is_le, ALU.add, accum_out=col[:, 1:2]))
                v.tensor_scalar(col[:], col[:], E - 1.0, None, ALU.min).then_inc(col_done, 1)
                ch.step(v.tensor_copy(routes.count[:, 0:1], end[0:1, E - 1:E]))
                ch.step(v.tensor_copy(routes.count[:, 1:2], held[0:1, E - 1:E]))
                ch.step(v.tensor_scalar(whole[:], ps_rank[:], 1.0 / P, -127.0 / 256, ALU.mult, ALU.add))
                ch.step(v.tensor_copy(tmp[:], whole[:]))
                ch.step(v.tensor_scalar(tmp[:], tmp[:], -(127.0 * P + P - 1), 1.0, ALU.mult, ALU.add))
                ch.step(v.scalar_tensor_tensor(tmp2[:], ps_rank[:], float(P), tmp[:], ALU.mult, ALU.add))
                ch.step(v.tensor_tensor(grid(tmp2), grid(tmp2), start[:].unsqueeze(1).broadcast_to([P, TILES, E]), ALU.add))
                ch.step(v.tensor_tensor(tmp2[:], tmp2[:], mask[:], ALU.mult))
                for i in range(TILES):
                    ins = v.max(top8[:, i, :], tmp2[:, i * E:(i + 1) * E])
                ch.step(ins)
                for i in range(TILES):
                    keys = tmp2[:, i * E:(i + 1) * E].unsqueeze(1).broadcast_to([P, TK, E])
                    mine = top8[:, i, :].unsqueeze(2).broadcast_to([P, TK, E])
                    gates = score[:, i * E:(i + 1) * E].unsqueeze(1).broadcast_to([P, TK, E])
                    ch.step(v.tensor_tensor(eq[:], keys, mine, ALU.is_equal))
                    ch.step(v.tensor_tensor(eq[:], eq[:], gates, ALU.mult))
                    ch.step(v.tensor_reduce(weight8[:, i * TK:(i + 1) * TK], eq[:], AX, ALU.add))
                flat8 = top8[:].rearrange("p i j -> p (i j)")
                ch.step(v.tensor_scalar(rank[:], flat8, -1.0, None, ALU.add))
                ch.step(v.tensor_scalar(whole[:, 0:64], rank[:], 1.0 / P, -127.0 / 256, ALU.mult, ALU.add))
                ch.step(v.tensor_copy(slot_p[:], whole[:, 0:64]))
                ch.step(v.scalar_tensor_tensor(slot_b[:], slot_p[:], -float(P), rank[:], ALU.mult, ALU.add))
                dve.wait_ge(lined, 1)
                r = lambda n: line[:, n, :]
                ch.step(v.tensor_copy(line[:, 0:2, :], ps_line[0:1, 0:2 * P].rearrange("p (a b) -> p a b", a=2)))
                ch.step(v.tensor_copy(routes.expert[:], r(1)))
                ch.step(v.memset(r(1), 1.0))
                ch.step(v.tensor_tensor(line[:, 1, 1:BLOCKS], line[:, 0, 1:BLOCKS], line[:, 0, 0:BLOCKS - 1], ALU.not_equal))
                ch.step(v.memset(r(2), 1.0))
                ch.step(v.tensor_tensor_scan(r(3), r(2), r(1), 0.0, ALU.mult, ALU.add))
                ch.step(v.tensor_copy(routes.number[:, 0:BLOCKS], r(3)))
                ch.step(v.tensor_scalar(r(6), k.c("iota")[0:1, :], end[0:1, E - 1:E], None, ALU.is_lt))
                ch.step(v.tensor_scalar(r(7), r(3), held[0:1, E - 1:E], None, ALU.is_lt))
                ch.step(v.tensor_tensor(r(6), r(6), r(7), ALU.mult))
                ch.step(v.tensor_tensor(r(6), r(6), r(1), ALU.mult))
                ch.step(v.tensor_tensor(routes.following[:, 0:BLOCKS], r(6), r(3), ALU.mult))
                ch.step(v.memset(routes.following[:, BLOCKS:LOOKED], 0))
                across = k.c("iota").unsqueeze(1).broadcast_to([P, TK, P])
                for i in range(TILES):
                    u = i % 2
                    if i >= 2:
                        dve.wait_ge(tabled, i - 1)
                    lo, hi = i * TK, (i + 1) * TK
                    v.tensor_tensor(hot_p[:, u], across, slot_p[:, lo:hi].unsqueeze(2).broadcast_to([P, TK, P]), ALU.is_equal)
                    ch.step(v.tensor_tensor(blocks[:], across, slot_b[:, lo:hi].unsqueeze(2).broadcast_to([P, TK, P]),
                                            ALU.is_equal))
                    v.tensor_scalar(hot_b[:, u, :, 0, :], blocks[:], k.c("token1")[:, i:i + 1], None, ALU.mult)
                    ins = v.tensor_tensor(hot_b[:, u, :, 1, :], blocks[:],
                                          weight8[:, lo:hi].unsqueeze(2).broadcast_to([P, TK, P]), ALU.mult)
                    ins.then_inc(hot, 1)
                    dve.wait_ge(hot, i + 1)
                dve.wait_ge(tabled, TILES)
                ch.step(v.tensor_scalar(pad[:], ps_table[:, 0:P], 0.0, k.c("padrow"), ALU.is_equal, ALU.mult))
                ch.step(v.scalar_tensor_tensor(pad[:], ps_table[:, 0:P], -1.0, pad[:], ALU.add, ALU.add))
                ch.step(v.tensor_copy(routes.token[:, 0:BLOCKS], pad[:]))
                ch.step(v.tensor_copy(routes.weight[:, 0:BLOCKS], ps_table[:, P:2 * P]))


def experts(k, layer, routes, name):
    nc, ap = k.nc, k.ap
    acc = k.moe_acc[layer]
    W = KS * F
    STAGES = 3
    with ExitStack() as ctx:
        stage = k.sb(name + "_stage", [P, STAGES, 3, W], ctx=ctx)
        gu_hi, gu_lo = (k.sb(f"{name}_{n}", [P, 2, KS, 2, F], F32R, ctx=ctx) for n in ("gu_hi", "gu_lo"))
        dn_hi, dn_lo = (k.sb(f"{name}_{n}", [P, 2, 2, D], F32R, ctx=ctx) for n in ("dn_hi", "dn_lo"))
        rows = [k.sb(f"{name}_rows{i}", [P, D], ctx=ctx) for i in range(2)]
        rows_hi, rows_lo = (k.sb(f"{name}_{n}", [P, KS, P], F32R, ctx=ctx) for n in ("rows_hi", "rows_lo"))
        gather_at = [k.sb(f"{name}_gather_at{i}", [P, 1], U32, ctx=ctx) for i in range(2)]
        add_at = k.sb(name + "_add_at", [P, 1], U32, ctx=ctx)
        silu = k.sb(name + "_silu", [P, F], ctx=ctx)
        hidden = k.sb(name + "_hidden", [P, F], ctx=ctx)
        hid_hi = [k.sb(f"{name}_hid_hi{i}", [P, 2, P], F32R, ctx=ctx) for i in range(2)]
        hid_lo = [k.sb(f"{name}_hid_lo{i}", [P, 2, P], F32R, ctx=ctx) for i in range(2)]
        y = [k.sb(f"{name}_y{i}", [P, D], ctx=ctx) for i in range(2)]
        ps_x = [k.ps(f"{name}_ps_x{i}", [P, 512], ctx=ctx) for i in range(2)]
        ps_gu = k.ps(name + "_ps_gu", [P, 512], ctx=ctx)
        ps_t = k.ps(name + "_ps_t", [P, 512], ctx=ctx)
        ps_y = [k.ps(f"{name}_ps_y{i}", [P, 512], ctx=ctx) for i in range(2)]
        w_in = [[k.sem(f"{name}_w_in{h}{j}") for j in range(3)] for h in range(2)]
        gu_landed, dn_landed = k.sem(name + "_gu_landed"), k.sem(name + "_dn_landed")
        rows_in = [k.sem(f"{name}_rows_in{i}") for i in range(2)]
        gu_rounded, dn_rounded, gu_split, dn_split = (k.sem(f"{name}_{n}") for n in
                                                      ("gu_rounded", "dn_rounded", "gu_split", "dn_split"))
        rows_turned, rows_rounded, rows_split = (k.sem(f"{name}_{n}") for n in ("rows_turned", "rows_rounded", "rows_split"))
        gu_done, silu_done, hid_done = (k.sem(f"{name}_{n}") for n in ("gu_done", "silu_done", "hid_done"))
        hid_turned, hid_rounded, hid_split = (k.sem(f"{name}_{n}") for n in ("hid_turned", "hid_rounded", "hid_split"))
        y_done, y_act, y_dve = (k.sem(f"{name}_{n}") for n in ("y_done", "y_act", "y_dve"))
        added, gather_set, add_set, pool_steps = (k.sem(f"{name}_{n}") for n in ("added", "gather_set", "add_set", "pool_steps"))

        def zero(b):
            return isinstance(b, int) and b == 0

        def when(eng, b, n, sure):
            return nullcontext() if sure else eng.If(b < n)

        def look(eng, table, at, low, high):
            return eng.value_load(table[0:1, bass.ds(at, 1)], min_val=low, max_val=high)

        def schedule(eng, step):
            n = look(eng, routes.count, 0, SURE, BLOCKS - 1)
            step(0, 0, n, True)
            step(1, 1, n, True)
            with eng.Fori(1, SURE // 2 - 1) as i:
                for half in range(2):
                    step(2 * i + half, half, n, True)
            with eng.Fori(SURE // 2 - 1, BLOCKS // 2) as i:
                with eng.If(2 * i < n + 1):
                    for half in range(2):
                        step(2 * i + half, half, n, False)
                    look(eng, routes.count, 0, SURE, BLOCKS - 1)
            return n

        def staged(place, j):
            piece = stage[:, bass.ds(place, 1), j, :].squeeze(1)
            return piece.rearrange("p (s f) -> p s f", f=F if j < 2 else D)

        def placed(t_gu, t_dn, half, j):
            return t_gu[:, bass.ds(half, 1), :, j, :].squeeze(1) if j < 2 else t_dn[:, bass.ds(half, 1)].squeeze(1)

        with nc.Block() as block:

            @block.sync
            def _(sp):
                sources = [ap[n][layer].rearrange("e (p s) f -> e p (s f)", p=P)
                           for n in ("exp_w_gate", "exp_w_up", "exp_w_down")]

                def load(o, place, parity, pieces):
                    e = look(sp, routes.expert, o, 0, E - 1)
                    for j in pieces:
                        if not isinstance(o, int) or o >= STAGES:
                            if j < 2:
                                sp.wait_ge(gu_split, 2 * (o - STAGES) + 1 + j)
                            else:
                                sp.wait_ge(dn_split, o - STAGES + 1)
                        sp.dma_start(stage[:, place, j, :], sources[j][bass.ds(e, 1)].squeeze(0)
                                     ).then_inc(w_in[parity][j], 16)

                def pass_on(o, parity, pieces):
                    for j in pieces:
                        sp.wait_ge(w_in[parity][j], 8 * (o - parity) + 16)
                        sp.sem_inc(gu_landed if j < 2 else dn_landed, 1)

                n = look(sp, routes.count, 1, TK, E)
                for o in range(4):
                    load(o, o % STAGES, o % 2, (0, 1))
                    if o >= 1:
                        load(o - 1, (o - 1) % STAGES, (o - 1) % 2, (2,))
                        pass_on(o - 1, (o - 1) % 2, (0, 1))
                    if o >= 2:
                        pass_on(o - 2, (o - 2) % 2, (2,))
                with sp.Fori(0, (E + 2 - 4 + 5) // 6) as i:
                    for u in range(6):
                        o = 6 * i + (4 + u)
                        with sp.If(o < n):
                            load(o, (4 + u) % STAGES, u % 2, (0, 1))
                        with sp.If(o < n + 1):
                            load(o - 1, (3 + u) % STAGES, (u + 1) % 2, (2,))
                            pass_on(o - 1, (u + 1) % 2, (0, 1))
                        with sp.If(o < n + 2):
                            pass_on(o - 2, u % 2, (2,))

            @block.gpsimd
            def _(pool):
                def gather(b, half, first=False):
                    if not first:
                        pool.wait_ge(rows_turned, 2 * (b - 1))
                    pool.tensor_copy(gather_at[half][:], routes.token[:, bass.ds(b, 1)]).then_inc(gather_set, 1)
                    pool.wait_ge(gather_set, b + 1)
                    pool.sem_inc(pool_steps, 1)
                    pool.indirect_dma_start(out=rows[half][:], out_offset=None, in_=k.h_rows,
                                            in_offset=bass.IndirectOffsetOnAxis(ap=gather_at[half][:], axis=0)
                                            ).then_inc(rows_in[half], 16)

                def add(b, half):
                    if not zero(b):
                        pool.wait_ge(added, 16 * b)
                    pool.tensor_copy(add_at[:], routes.token[:, bass.ds(b, 1)]).then_inc(add_set, 1)
                    pool.wait_ge(add_set, b + 1)
                    pool.wait_ge(y_act, b + 1)
                    pool.wait_ge(y_dve, b + 1)
                    pool.sem_inc(pool_steps, 1)
                    pool.indirect_dma_start(out=acc, out_offset=bass.IndirectOffsetOnAxis(ap=add_at[:], axis=0),
                                            in_=y[half][:], in_offset=None, compute_op=ALU.add).then_inc(added, 16)

                def rest_of_down(half, place, number):
                    pool.wait_ge(dn_rounded, number)
                    pool.tensor_tensor(placed(None, dn_lo, half, 2), staged(place, 2), placed(None, dn_hi, half, 2).bitcast(F32),
                                       ALU.subtract).then_inc(dn_split, 1)

                def step(b, half, n, sure):
                    with when(pool, b + 2, n, sure):
                        gather(b + 2, half)
                    if not zero(b):
                        after = look(pool, routes.following, b - 1, 0, E - 1)
                        with pool.If(after > 0):
                            rest_of_down(after % 2, after % STAGES, after + 1)
                        with when(pool, b - 1, n, sure):
                            add(b - 1, 1 - half)

                gather(0, 0, first=True)
                gather(1, 1, first=True)
                rest_of_down(0, 0, 1)
                n = schedule(pool, step)
                pool.wait_ge(added, 16 * n)

            @block.tensor
            def _(pe):
                def turn_rows(b, half):
                    pe.wait_ge(rows_in[half], 16 * (b // 2 + 1) if isinstance(b, int) else 8 * (b - half) + 16)
                    if not zero(b):
                        pe.wait_ge(rows_split, 2 * b)
                    for bank in range(2):
                        for s in range(4):
                            mm = pe.transpose(ps_x[bank][:, s * P:(s + 1) * P],
                                              rows[half][:, (4 * bank + s) * P:(4 * bank + s + 1) * P], k.c("ident"))
                        mm.then_inc(rows_turned, 1)

                def gate_up(b):
                    number = look(pe, routes.number, b, 1, E)
                    at = (number + 1) % 2
                    pe.wait_ge(gu_split, 2 * number)
                    pe.wait_ge(rows_split, 2 * (b + 1))
                    passes = ((rows_hi, gu_hi), (rows_hi, gu_lo), (rows_lo, gu_hi))
                    for n, (x, w) in enumerate(passes):
                        for s in range(KS):
                            mm = pe.matmul(ps_gu[:], x[:, s, :],
                                           w[:, bass.ds(at, 1), s].squeeze(1).rearrange("p a f -> p (a f)"),
                                           start=(n == 0 and s == 0), stop=(n == 2 and s == KS - 1))
                    mm.then_inc(gu_done, 1)

                def down(b, half, j, number, at):
                    if j == 0:
                        pe.wait_ge(dn_split, number)
                        pe.wait_ge(hid_split, b + 1)
                    if not zero(b):
                        pe.wait_ge(y_dve if j else y_act, b)
                    passes = ((hid_hi, dn_hi), (hid_hi, dn_lo), (hid_lo, dn_hi))
                    for n, (x, w) in enumerate(passes):
                        for c in range(2):
                            mm = pe.matmul(ps_y[j][:], x[half][:, c, :],
                                           w[:, bass.ds(at, 1), c, j * 512:(j + 1) * 512].squeeze(1),
                                           start=(n == 0 and c == 0), stop=(n == 2 and c == 1))
                    mm.then_inc(y_done, 1)

                def turn_hidden(b):
                    pe.wait_ge(hid_done, b + 1)
                    for c in range(2):
                        mm = pe.transpose(ps_t[:, c * P:(c + 1) * P], hidden[:, c * P:(c + 1) * P], k.c("ident"))
                    mm.then_inc(hid_turned, 1)

                def step(b, half, n, sure):
                    with when(pe, b, n, sure):
                        gate_up(b)
                    if not zero(b):
                        number = look(pe, routes.number, b - 1, 1, E)
                        at = (number + 1) % 2
                    with when(pe, b + 1, n, sure):
                        turn_rows(b + 1, 1 - half)
                    if not zero(b):
                        with when(pe, b - 1, n, sure):
                            down(b - 1, 1 - half, 0, number, at)
                    with when(pe, b, n, sure):
                        turn_hidden(b)
                    if not zero(b):
                        with when(pe, b - 1, n, sure):
                            down(b - 1, 1 - half, 1, number, at)

                turn_rows(0, 0)
                schedule(pe, step)

            @block.scalar
            def _(act):
                def round_rows(b):
                    act.wait_ge(rows_turned, 2 * (b + 1))
                    if not zero(b):
                        act.wait_ge(gu_done, b)
                    for bank in range(2):
                        act.copy(rows_hi[:, 4 * bank:4 * bank + 4, :],
                                 ps_x[bank][:].rearrange("p (s t) -> p s t", s=4)).then_inc(rows_rounded, 1)

                def silu_of(b):
                    act.wait_ge(gu_done, b + 1)
                    if not zero(b):
                        act.wait_ge(hid_done, b)
                    act.activation(silu[:], ps_gu[:, 0:F], ACT.Silu).then_inc(silu_done, 1)

                def y_back(b, half):
                    act.wait_ge(y_done, 2 * b + 1)
                    if not isinstance(b, int) or b >= 2:
                        act.wait_ge(added, 16 * (b - 1))
                    act.activation(y[half][:, 0:512], ps_y[0][:], ACT.Copy,
                                   scale=routes.weight[:, bass.ds(b, 1)]).then_inc(y_act, 1)

                def round_weights(half, place, o, j, sem):
                    act.wait_ge(gu_landed, 2 * o + j + 1) if j < 2 else act.wait_ge(dn_landed, o + 1)
                    act.copy(placed(gu_hi, dn_hi, half, j), staged(place, j)).then_inc(sem, 1)

                def round_gate_up(b, after):
                    with act.If(after > 0):
                        if not zero(b):
                            act.wait_ge(gu_done, b)
                        for j in range(2):
                            round_weights(after % 2, after % STAGES, after, j, gu_rounded)

                def step(b, half, n, sure):
                    after = look(act, routes.following, b, 0, E - 1)
                    after_next = look(act, routes.following, b + 1, 0, E - 1)
                    with when(act, b, n, sure):
                        silu_of(b)
                    with when(act, b + 1, n, sure):
                        round_rows(b + 1)
                    if not zero(b):
                        with when(act, b - 1, n, sure):
                            y_back(b - 1, 1 - half)
                    round_gate_up(b + 1, after_next)
                    with act.If(after > 0):
                        if not zero(b):
                            act.wait_ge(y_done, 2 * b)
                        round_weights(after % 2, after % STAGES, after, 2, dn_rounded)

                round_rows(0)
                for j in range(2):
                    round_weights(0, 0, 0, j, gu_rounded)
                round_gate_up(0, look(act, routes.following, 0, 0, E - 1))
                round_weights(0, 0, 0, 2, dn_rounded)
                schedule(act, step)

            @block.vector
            def _(dve):
                def rest_of_rows(b):
                    for bank in range(2):
                        dve.wait_ge(rows_rounded, 2 * b + bank + 1)
                        part = slice(4 * bank, 4 * bank + 4)
                        dve.tensor_tensor(rows_lo[:, part, :], ps_x[bank][:].rearrange("p (s t) -> p s t", s=4),
                                          rows_hi[:, part, :].bitcast(F32), ALU.subtract).then_inc(rows_split, 1)

                def hidden_of(b):
                    dve.wait_ge(silu_done, b + 1)
                    if not zero(b):
                        dve.wait_ge(hid_turned, b)
                    dve.tensor_tensor(hidden[:].rearrange("t (c p) -> t p c", c=2),
                                      silu[:].rearrange("t (p c) -> t p c", c=2),
                                      ps_gu[:, F:2 * F].rearrange("t (p c) -> t p c", c=2), ALU.mult).then_inc(hid_done, 1)

                def split_hidden(b, half):
                    dve.wait_ge(hid_turned, b + 1)
                    src = ps_t[:, 0:2 * P].rearrange("p (c t) -> p c t", c=2)
                    dve.tensor_copy(hid_hi[half][:], src).then_inc(hid_rounded, 1)
                    dve.wait_ge(hid_rounded, b + 1)
                    dve.tensor_tensor(hid_lo[half][:], src, hid_hi[half][:].bitcast(F32), ALU.subtract).then_inc(hid_split, 1)

                def y_back(b, half):
                    dve.wait_ge(y_done, 2 * b + 2)
                    if not isinstance(b, int) or b >= 2:
                        dve.wait_ge(added, 16 * (b - 1))
                    dve.tensor_scalar(y[half][:, 512:1024], ps_y[1][:], routes.weight[:, bass.ds(b, 1)], None,
                                      ALU.mult).then_inc(y_dve, 1)

                def rest_of_weights(half, place, number):
                    for j in range(2):
                        dve.wait_ge(gu_rounded, 2 * number - 1 + j)
                        dve.tensor_tensor(placed(gu_lo, None, half, j), staged(place, j),
                                          placed(gu_hi, None, half, j).bitcast(F32), ALU.subtract).then_inc(gu_split, 1)

                def rests_after(b):
                    after = look(dve, routes.following, b, 0, E - 1)
                    with dve.If(after > 0):
                        rest_of_weights(after % 2, after % STAGES, after + 1)

                def step(b, half, n, sure):
                    with when(dve, b, n, sure):
                        hidden_of(b)
                    with when(dve, b + 1, n, sure):
                        rest_of_rows(b + 1)
                    with when(dve, b, n, sure):
                        split_hidden(b, half)
                    if not zero(b):
                        with when(dve, b - 1, n, sure):
                            y_back(b - 1, 1 - half)
                    rests_after(b + 1)

                rest_of_rows(0)
                rest_of_weights(0, 0, 1)
                rests_after(0)
                schedule(dve, step)


def moe_residual(k, layer, m, name, out=None):
    nc = k.nc
    acc = k.moe_acc[layer]
    NB = 4
    with ExitStack() as ctx:
        gate = k.sb(name + "_gate", [P, D], ctx=ctx)
        part = k.sb(name + "_part", [P, NB, D], ctx=ctx)
        gate_in, gated_done, x_done = (k.sem(f"{name}_{n}") for n in ("gate_in", "gated", "x_done"))
        part_in = [k.sem(f"{name}_part_in{i}") for i in range(NB)]
        out_done = k.sem(name + "_out")
        scratch, squared = k.sb(name + "_scratch", [P, D], ctx=ctx), k.sem(name + "_squared")
        with nc.Block() as block:

            @block.sync
            def _(sp):
                sp.dma_start(gate[:], spread(k.mod[m, 2])).then_inc(gate_in, 16)
                for i in range(TILES):
                    if i >= NB:
                        sp.wait_ge(x_done, i - NB + 1)
                    sp.dma_start(k.x[:, i, :], k.x_rows[i * P:(i + 1) * P, :]).then_inc(part_in[i % NB], 16)
                    sp.dma_start(part[:, i % NB, :], acc[i * P:(i + 1) * P, :]).then_inc(part_in[i % NB], 16)

            @block.vector
            def _(dve):
                dve.wait_ge(gate_in, 16)
                for i in range(TILES):
                    dve.wait_ge(part_in[i % NB], 32 * (i // NB + 1))
                    nc.vector.tensor_tensor(part[:, i % NB, :], part[:, i % NB, :], gate[:], ALU.mult).then_inc(gated_done, 1)
                    dve.wait_ge(gated_done, i + 1)
                    nc.vector.tensor_tensor(k.x[:, i, :], k.x[:, i, :], part[:, i % NB, :], ALU.add).then_inc(x_done, 1)

            @block.scalar
            def _(act):
                if out is None:
                    k.sum_squares(act, scratch[:], x_done, squared)
                    return
                for i in range(TILES):
                    act.wait_ge(x_done, i + 1)
                    act.dma_start(out[i * P:(i + 1) * P, :], k.x[:, i, :]).then_inc(out_done, 16)
                act.wait_ge(out_done, 16 * TILES)


def moe_front(k, layer, m, name, routes):
    with ExitStack() as inner:
        hT = k.sb(name + "_hT", [P, KS, SEQ], ctx=inner)
        spilled = k.sem(name + "_spilled")

        def spill(sp):
            sp.dma_start(k.x_rows.rearrange("(i p) d -> p i d", p=P), k.x[:]).then_inc(spilled, 16)

        normalise(k, m, None, name + "_n", True, hT=hT, rows_out=True, extra=spill)
        route_and_share(k, layer, hT, routes, name + "_r", spilled)


def sine_tables(k, cos_sin, rotor, lam, dt, mag):
    nc, ap = k.nc, k.ap
    N = TILES * ROPE + GROUPS
    with ExitStack() as ctx:
        pos = k.sb("st_pos", [P, TILES], I32, ctx=ctx)
        pos_f = k.sb("st_pos_f", [P, TILES], ctx=ctx)
        lam_in = k.sb("st_lam_in", [GROUPS, 2, 2, NS], ctx=ctx)
        ang = k.sb("st_ang", [P, N], ctx=ctx)
        turns = k.sb("st_turns", [P, N], I32, ctx=ctx)
        turns_f = k.sb("st_turns_f", [P, N], ctx=ctx)
        co = k.sb("st_co", [P, N], ctx=ctx)
        both = k.sb("st_both", [P, 2, N], ctx=ctx)
        decay = k.sb("st_decay", [P, GROUPS], ctx=ctx)
        ps = k.ps("st_ps", [P, 512], ctx=ctx)
        loaded, turned, dt_done, ready, waves, chain = (k.sem(f"st_{n}") for n in
                                                        ("loaded", "turned", "dt", "ready", "waves", "chain"))
        with nc.Block() as block:

            @block.sync
            def _(sp):
                sp.dma_start(dt[:], spread(ap["s5_log_dt"][0])).then_inc(loaded, 16)
                for half in range(2):
                    sp.dma_start(lam_in[:, 0, half, :], ap["s5_lambda_re"][0]).then_inc(loaded, 16)
                    sp.dma_start(lam_in[:, 1, half, :], ap["s5_lambda_im"][0]).then_inc(loaded, 16)
                with nc.allow_non_contiguous_dma(reason="1024 positions"):
                    sp.dma_start(pos[:], ap["positions"][0].rearrange("(i p) -> p i", p=P)).then_inc(loaded, 16)

            @block.tensor
            def _(pe):
                pe.wait_ge(loaded, 96)
                for i in range(2):
                    mm = pe.transpose(ps[:, i * GROUPS:(i + 1) * GROUPS], lam_in[:, i].rearrange("g a p -> g (a p)"),
                                      k.c("ident")[0:GROUPS, 0:GROUPS])
                mm.then_inc(turned, 1)

            @block.scalar
            def _(act):
                act.wait_ge(loaded, 96)
                act.activation(dt[:], dt[:], ACT.Exp).then_inc(dt_done, 1)
                act.wait_ge(ready, 1)
                act.activation(mag[:, 0, :], decay[:], ACT.Exp)
                act.activation(mag[:, 1, :], decay[:], ACT.Exp, scale=float(CH)).then_inc(waves, 1)
                act.wait_ge(ready, 2)
                act.activation(both[:, 0, :], co[:], ACT.Sin)
                act.activation(both[:, 1, :], ang[:], ACT.Sin).then_inc(waves, 1)

            @block.vector
            def _(dve):
                ch = Chain(dve, chain)
                dve.wait_ge(turned, 1)
                ch.step(dve.tensor_copy(lam[:], ps[:, 0:2 * GROUPS].rearrange("p (a g) -> p a g", a=2)))
                dve.wait_ge(dt_done, 1)
                ch.step(dve.tensor_copy(pos_f[:], pos[:]))
                ch.step(dve.tensor_tensor(ang[:, 0:64].rearrange("p (i r) -> p i r", r=ROPE),
                                          pos_f[:].unsqueeze(2).broadcast_to([P, TILES, ROPE]),
                                          k.c("freq").unsqueeze(1).broadcast_to([P, TILES, ROPE]), ALU.mult))
                ch.step(dve.tensor_tensor(ang[:, 64:N], lam[:, 1, :], dt[:], ALU.mult))
                dve.tensor_tensor(decay[:], lam[:, 0, :], dt[:], ALU.mult).then_inc(ready, 1)
                ch.step(dve.tensor_scalar(turns[:], ang[:], float(1.0 / TWO_PI), None, ALU.mult))
                ch.step(dve.tensor_copy(turns_f[:], turns[:]))
                for part in (PI_A, PI_B, PI_C):
                    ch.step(dve.scalar_tensor_tensor(ang[:], turns_f[:], -part, ang[:], ALU.mult, ALU.add))
                ch.step(dve.tensor_scalar(ang[:], ang[:], 3.1415925, -3.1415925, ALU.min, ALU.max))
                ch.step(dve.scalar_tensor_tensor(co[:], ang[:], -1.0, ang[:], ALU.mult, ALU.max))
                dve.tensor_scalar(co[:], co[:], -1.0, float(np.pi / 2), ALU.mult, ALU.add).then_inc(ready, 1)
                dve.wait_ge(waves, 2)
                ch.step(dve.tensor_copy(cos_sin[:], both[:, :, 0:64].rearrange("p a (i r) -> p a i r", r=ROPE)))
                ch.step(dve.tensor_copy(rotor[:], both[:, :, 64:N]))


def s5(k, hT, w_u, w_u_in, uT, rows, mixT, rotor, lam, mag):
    nc, ap = k.nc, k.ap
    G = HALF_G
    NQ = GROUPS // 4
    with ExitStack() as ctx:
        sbt = lambda n, shape: k.sb("s5_" + n, shape, ctx=ctx)
        cc = sbt("c", [P, 2, GROUPS, GH])
        bb = sbt("b", [P, 2, GROUPS, GH])
        coef = sbt("coef", [P, 6, GROUPS])
        pw = sbt("pw", [P, 2, CH + 1, GROUPS])
        sg = sbt("sg", [P, 4, CH + 1, GROUPS])
        wbuf = sbt("wbuf", [P, G, 16, GH])
        vrev = sbt("vrev", [P, G, CH, GH])
        tmp_w = sbt("tmp_w", [P, (CH + 1) * G * GH])
        rot = sbt("rot", [P, 2, 7, GROUPS])
        tr = sbt("tr", [P, 2, G, CHUNKS])
        tmp_t = sbt("tmp_t", [P, G, CHUNKS // 2])
        bpad = sbt("bpad", [P, 4, 15, GH])
        m3 = sbt("m3", [P, 2, 4, P])
        m1 = sbt("m1", [P, 4, P])
        z = sbt("z", [P, 4, CHUNKS])
        zt = sbt("zt", [P, 4, CHUNKS])
        st = sbt("st", [P, 4, CHUNKS + 1])
        dcol = sbt("dcol", [P, GROUPS])
        bcol = sbt("bcol", [P, GROUPS])
        b_in = tmp_w[:, 0:1024].rearrange("p (a g h) -> p a g h", a=2, h=GH)
        tmp_b = tmp_w[:, 1024:1536].rearrange("p (g h) -> p g h", h=GH)
        c_in = tmp_t[:].rearrange("p g c -> p (g c)").rearrange("p (a t u n) -> p a t u n", a=2, t=4, u=2)
        glu = rows.rearrange("p g j h -> p g (j h)")
        out_rows = rows.rearrange("p g j h -> p (g j h)").rearrange("c (j n) -> c j n", j=CH)
        gate = sbt("gate", [P, 2, 4, CHUNKS])
        bank = [k.ps(f"s5_ps{i}", [P, 512], ctx=ctx) for i in range(8)]
        loaded, glu_clear, glu_in, c_turned, chain = (k.sem(f"s5_{n}") for n in
                                                      ("loaded", "glu_clear", "glu_in", "c_turned", "chain"))
        ready, m3_turned, m3_back, m1_done, m1_back = (k.sem(f"s5_{n}") for n in
                                                       ("ready", "m3_turned", "m3_back", "m1_done", "m1_back"))
        w_done, z_done, swapped, s_done, y_done, y_read = (k.sem(f"s5_{n}") for n in
                                                           ("w_done", "z_done", "swapped", "s_done", "y_done", "y_read"))
        gelu_done, glu_done, biased, sig_done, gated_done = (k.sem(f"s5_{n}") for n in
                                                             ("gelu", "glu_done", "biased", "sig", "gated"))
        u_done, u_copied, u_turned, u_back = (k.sem(f"s5_{n}") for n in ("u_done", "u_copied", "u_turned", "u_back"))
        y_turned, y_rows, mix_turned, mix_a, mix_v = (k.sem(f"s5_{n}") for n in
                                                      ("y_turned", "y_rows", "mix_turned", "mix_a", "mix_v"))

        with nc.Block() as block:

            @block.sync
            def _(sp):
                with nc.allow_non_contiguous_dma(reason="small tables of the S5 heads"):
                    for half in range(2):
                        for i, n in enumerate(("s5_b_re", "s5_b_im")):
                            sp.dma_start(b_in[half * NS:(half + 1) * NS, i], ap[n][0].rearrange("g p h -> p g h")
                                         ).then_inc(loaded, 16)
                        for i, n in enumerate(("s5_c_re", "s5_c_im")):
                            sp.dma_start(c_in[:, i, :, half, :], ap[n][0].rearrange("(t g) h p -> (g h) t p", t=4)
                                         ).then_inc(loaded, 16)
                    for j in range(CH):
                        sp.dma_start(dcol[j * GH:(j + 1) * GH, :], ap["s5_d"][0].rearrange("g h -> h g")).then_inc(loaded, 16)
                        sp.dma_start(bcol[j * GH:(j + 1) * GH, :], ap["s5_glu_b"][0].rearrange("g h -> h g")
                                     ).then_inc(loaded, 16)
                    sp.wait_ge(glu_clear, 1)
                    for j in range(CH):
                        sp.dma_start(glu[j * GH:(j + 1) * GH, :, j * GH:(j + 1) * GH],
                                     ap["s5_glu_w"][0].rearrange("g h e -> h g e")).then_inc(glu_in, 16)

            @block.gpsimd
            def _(pool):
                pool.wait_ge(u_turned, NQ)
                pool.memset(glu, 0.0).then_inc(glu_clear, 1)

            @block.tensor
            def _(pe):
                ident = k.c("ident")
                pe.wait_ge(loaded, 24 * 16)
                for i in range(2):
                    for t in range(4):
                        mm = pe.transpose(bank[i][:, t * P:(t + 1) * P], c_in[:, i, t].rearrange("q a p -> q (a p)"), ident)
                mm.then_inc(c_turned, 1)
                pe.wait_ge(w_u_in, 16)
                for j in range(CH):
                    if j >= 2:
                        pe.wait_ge(u_copied, j - 1)
                    for s in range(KS):
                        mm = pe.matmul(bank[6 + j % 2][:], hT[:, s, j:SEQ:CH], w_u[:, s, :], start=(s == 0),
                                       stop=(s == KS - 1))
                    mm.then_inc(u_done, 1)
                pe.wait_ge(u_copied, CH)
                for q in range(NQ):
                    if q >= 2:
                        pe.wait_ge(u_back, q - 1)
                    for g in range(4):
                        mm = pe.transpose(bank[4 + q % 2][:, g * P:(g + 1) * P],
                                          rows[:, 4 * q + g].rearrange("c j h -> c (j h)"), ident)
                    mm.then_inc(u_turned, 1)
                pe.wait_ge(u_back, NQ)

                def tables(q):
                    gs = [4 * (q % 4) + g for g in range(4)]
                    pe.wait_ge(ready, q + 1)
                    if q:
                        pe.wait_ge(m3_back, q)
                        pe.wait_ge(m1_back, q)
                    for g in range(4):
                        mm = pe.transpose(bank[0][:, g * P:(g + 1) * P], vrev[:, gs[g]].rearrange("p j h -> p (j h)"), ident)
                    mm.then_inc(m3_turned, 1)
                    for g in range(4):
                        bp = bpad[:, g].rearrange("p j h -> p (j h)")
                        wb = wbuf[:, gs[g]].rearrange("p j h -> p (j h)")
                        for j in range(CH):
                            mm = pe.matmul(bank[1][:, g * P:(g + 1) * P], bp[:, (7 - j) * GH:(7 - j) * GH + P],
                                           wb[:, (7 - j) * GH:(7 - j) * GH + P], start=(j == 0), stop=(j == CH - 1))
                    mm.then_inc(m1_done, 1)

                tables(0)
                for q in range(NQ):
                    gs = [4 * (q % 4) + g for g in range(4)]
                    pe.wait_ge(m3_back, q + 1)
                    if q:
                        pe.wait_ge(z_done, q)
                    for v in range(2):
                        for g in range(4):
                            mm = pe.matmul(bank[2 + v][:, g * P:(g + 1) * P], m3[:, v, g, :], uT[:, 4 * q + g, :],
                                           start=True, stop=True)
                    mm.then_inc(w_done, 1)
                    if (q + 1) % 4:
                        tables(q + 1)
                    pe.wait_ge(z_done, q + 1)
                    if q:
                        pe.wait_ge(s_done, q)
                    pe.matmul(bank[4][:], k.c("swap"), z[:].rearrange("p g c -> p (g c)"), start=True,
                              stop=True).then_inc(swapped, 1)
                    pe.wait_ge(s_done, q + 1)
                    pe.wait_ge(m1_back, q + 1)
                    if q:
                        pe.wait_ge(y_read, q)
                    for g in range(4):
                        out = bank[5][:, g * P:(g + 1) * P]
                        pe.matmul(out, m1[:, g, :], uT[:, 4 * q + g, :], start=True, stop=False)
                        mm = pe.matmul(out, wbuf[:, gs[g], 8:16].rearrange("p j h -> p (j h)"), st[:, g, 0:CHUNKS],
                                       start=False, stop=True)
                    mm.then_inc(y_done, 1)
                    if (q + 1) % 4 == 0 and q + 1 < NQ:
                        tables(q + 1)
                pe.wait_ge(gelu_done, NQ)
                pe.wait_ge(glu_in, 16 * CH)
                for q in range(NQ):
                    if q >= 2:
                        pe.wait_ge(biased, q - 1)
                    for g in range(4):
                        mm = pe.matmul(bank[6 + q % 2][:, g * P:(g + 1) * P], glu[:, 4 * q + g, :], uT[:, 4 * q + g, :],
                                       start=True, stop=True)
                    mm.then_inc(glu_done, 1)
                for q in range(NQ):
                    pe.wait_ge(gated_done, q + 1)
                    if q >= 2:
                        pe.wait_ge(y_rows, q - 1)
                    for g in range(4):
                        mm = pe.transpose(bank[q % 2][:, g * P:(g + 1) * P], uT[:, 4 * q + g, :], ident)
                    mm.then_inc(y_turned, 1)
                pe.wait_ge(y_rows, NQ)
                for t in range(4):
                    if t:
                        pe.wait_ge(mix_a, t)
                        pe.wait_ge(mix_v, t)
                    for j in range(CH):
                        mm = pe.transpose(bank[2 + j // 4][:, (j % 4) * P:(j % 4 + 1) * P], out_rows[:, j, t * P:(t + 1) * P], ident)
                    mm.then_inc(mix_turned, 1)

            @block.scalar
            def _(act):
                for j in range(CH):
                    act.wait_ge(u_done, j + 1)
                    act.copy(rows[:, :, j, :], bank[6 + j % 2][:].rearrange("c (g h) -> c g h", h=GH)).then_inc(u_copied, 1)
                for q in range(NQ):
                    act.wait_ge(u_turned, q + 1)
                    act.copy(uT[:, 4 * q:4 * q + 4, :], bank[4 + q % 2][:].rearrange("p (g c) -> p g c", g=4)
                             ).then_inc(u_back, 1)
                for q in range(NQ):
                    act.wait_ge(m1_done, q + 1)
                    if q:
                        act.wait_ge(y_done, q)
                    act.copy(m1[:].rearrange("p g n -> p (g n)"), bank[1][:]).then_inc(m1_back, 1)
                    act.wait_ge(y_read, q + 1)
                    part = uT[:, 4 * q:4 * q + 4, :]
                    act.activation(part, part, ACT.Gelu_apprx_tanh).then_inc(gelu_done, 1)
                for q in range(NQ):
                    act.wait_ge(biased, q + 1)
                    act.activation(gate[:, q % 2], gate[:, q % 2], ACT.Sigmoid).then_inc(sig_done, 1)
                for q in range(NQ):
                    act.wait_ge(y_turned, q + 1)
                    act.copy(out_rows[:, :, 4 * q * GH:4 * (q + 1) * GH].rearrange("c j (g h) -> c g j h", g=4),
                             bank[q % 2][:].rearrange("c (g j h) -> c g j h", g=4, j=CH)).then_inc(y_rows, 1)
                for t in range(4):
                    act.wait_ge(mix_turned, t + 1)
                    act.copy(mixT[:, t, :].rearrange("p (c j) -> p j c", j=CH)[:, 0:4, :],
                             bank[2][:].rearrange("p (j c) -> p j c", j=4)).then_inc(mix_a, 1)

            @block.vector
            def _(dve):
                ch = Chain(dve, chain)
                tt, ts = dve.tensor_tensor, dve.tensor_scalar
                T, B = slice(0, NS), slice(NS, P)

                def cmul(out_r, out_i, a_r, a_i, b_r, b_i, t):
                    ch.step(tt(out_r, a_r, b_r, ALU.mult))
                    ch.step(tt(t, a_i, b_i, ALU.mult))
                    ch.step(tt(out_r, out_r, t, ALU.subtract))
                    ch.step(tt(out_i, a_r, b_i, ALU.mult))
                    ch.step(tt(t, a_i, b_r, ALU.mult))
                    ch.step(tt(out_i, out_i, t, ALU.add))

                c6 = lambda i: coef[:, i, :]
                ch.step(dve.memset(pw[:, 0, 0, :], 1.0))
                ch.step(dve.memset(pw[:, 1, 0, :], 0.0))
                ch.step(tt(pw[:, 0, 1, :], mag[:, 0, :], rotor[:, 0, :], ALU.mult))
                ch.step(tt(pw[:, 1, 1, :], mag[:, 0, :], rotor[:, 1, :], ALU.mult))
                for j in range(2, CH + 1):
                    cmul(pw[:, 0, j, :], pw[:, 1, j, :], pw[:, 0, j - 1, :], pw[:, 1, j - 1, :], pw[:, 0, 1, :],
                         pw[:, 1, 1, :], c6(0))
                nr, ni, lr, li = c6(1), pw[:, 1, 1, :], lam[:, 0, :], lam[:, 1, :]
                ch.step(ts(nr, pw[:, 0, 1, :], -1.0, None, ALU.add))
                ch.step(tt(c6(0), lr, lr, ALU.mult))
                ch.step(tt(c6(2), li, li, ALU.mult))
                ch.step(tt(c6(0), c6(0), c6(2), ALU.add))
                ch.step(dve.reciprocal(c6(5), c6(0)))
                ch.step(tt(c6(2), nr, lr, ALU.mult))
                ch.step(tt(c6(0), ni, li, ALU.mult))
                ch.step(tt(c6(2), c6(2), c6(0), ALU.add))
                ch.step(tt(c6(2), c6(2), c6(5), ALU.mult))
                ch.step(tt(c6(3), ni, lr, ALU.mult))
                ch.step(tt(c6(0), nr, li, ALU.mult))
                ch.step(tt(c6(3), c6(3), c6(0), ALU.subtract))
                ch.step(tt(c6(3), c6(3), c6(5), ALU.mult))
                dve.wait_ge(loaded, 24 * 16)
                wide = lambda a: a.unsqueeze(2).broadcast_to([P, GROUPS, GH])
                cmul(bb[:, 0], bb[:, 1], b_in[:, 0], b_in[:, 1], wide(c6(2)), wide(c6(3)), tmp_b)
                dve.wait_ge(c_turned, 1)
                for i in range(2):
                    ch.step(dve.tensor_copy(cc[:, i].rearrange("p g h -> p (g h)"), bank[i][:]))
                for half in (T, B):
                    a_r, a_i = pw[half, 0], pw[half, 1]
                    top = half is T
                    ch.step(dve.tensor_copy(sg[half, 0], a_r if top else a_i))
                    ch.step(ts(sg[half, 1], a_i if top else a_r, -1.0 if top else 1.0, None, ALU.mult))
                    ch.step(ts(sg[half, 2], a_r if top else a_i, 1.0 if top else -1.0, None, ALU.mult))
                    ch.step(ts(sg[half, 3], a_i if top else a_r, -1.0, None, ALU.mult))
                dst = (c6(0), c6(1))
                cmul(dst[0], dst[1], rotor[:, 0, :], rotor[:, 1, :], rotor[:, 0, :], rotor[:, 1, :], c6(4))
                cmul(c6(2), c6(3), c6(0), c6(1), c6(0), c6(1), c6(4))
                cmul(rot[:, 0, 0, :], rot[:, 1, 0, :], c6(2), c6(3), c6(2), c6(3), c6(4))
                for l in range(1, 7):
                    cmul(rot[:, 0, l, :], rot[:, 1, l, :], rot[:, 0, l - 1, :], rot[:, 1, l - 1, :],
                         rot[:, 0, l - 1, :], rot[:, 1, l - 1, :], c6(4))
                ch.step(dve.memset(wbuf[:, :, 0:7, :], 0.0))
                ch.step(dve.memset(bpad[:], 0.0))
                ch.step(dve.memset(st[:, :, 0:1], 0.0))

                def half_tables(hf):
                    gsl = slice(hf * G, (hf + 1) * G)
                    t9 = tmp_w[:].rearrange("p (j g h) -> p j g h", j=CH + 1, g=G)
                    for j in range(CH + 1):
                        one = lambda t, i: t[:, i, gsl, :]
                        pj = lambda i: sg[:, i, j, gsl].unsqueeze(2).broadcast_to([P, G, GH])
                        dve.tensor_tensor(wbuf[:, :, 7 + j, :], one(cc, 0), pj(2), ALU.mult)
                        ins = dve.tensor_tensor(t9[:, j], one(cc, 1), pj(3), ALU.mult)
                    ch.step(ins)
                    for j in range(CH + 1):
                        ins = dve.tensor_tensor(wbuf[:, :, 7 + j, :], wbuf[:, :, 7 + j, :], t9[:, j], ALU.add)
                    ch.step(ins)
                    for j in range(CH):
                        one = lambda t, i: t[:, i, gsl, :]
                        pj = lambda i: sg[:, i, j, gsl].unsqueeze(2).broadcast_to([P, G, GH])
                        dve.tensor_tensor(vrev[:, :, 7 - j, :], one(bb, 0), pj(0), ALU.mult)
                        ins = dve.tensor_tensor(t9[:, j], one(bb, 1), pj(1), ALU.mult)
                    ch.step(ins)
                    for j in range(CH):
                        ins = dve.tensor_tensor(vrev[:, :, 7 - j, :], vrev[:, :, 7 - j, :], t9[:, j], ALU.add)
                    ch.step(ins)
                    ch.step(dve.memset(tr[:, 0, :, 0:1], 1.0))
                    ch.step(dve.memset(tr[:, 1, :, 0:1], 0.0))
                    for l in range(7):
                        n = 1 << l
                        r = lambda i: rot[:, i, l, gsl].unsqueeze(2).broadcast_to([P, G, n])
                        cmul(tr[:, 0, :, n:2 * n], tr[:, 1, :, n:2 * n], tr[:, 0, :, 0:n], tr[:, 1, :, 0:n], r(0), r(1),
                             tmp_t[:, :, 0:n])
                    ch.step(ts(tr[B, 1], tr[B, 1], -1.0, None, ALU.mult))

                def pad(q):
                    gl = slice(4 * (q % 4), 4 * (q % 4) + 4)
                    if q:
                        dve.wait_ge(m1_done, q)
                    dve.tensor_copy(bpad[:, :, 7, :], vrev[:, gl, 7, :]).then_inc(ready, 1)

                for q in range(NQ):
                    if q % 4 == 0:
                        if q:
                            dve.wait_ge(y_done, q)
                        half_tables(q // 4)
                        pad(q)
                    gl = slice(4 * (q % 4), 4 * (q % 4) + 4)
                    gg = slice(4 * q, 4 * q + 4)
                    dve.wait_ge(m3_turned, q + 1)
                    if q:
                        dve.wait_ge(w_done, q)
                    src = bank[0][:].rearrange("p (g n) -> p g n", g=4)
                    dve.tensor_copy(m3[:, 0], src)
                    dve.tensor_copy(m3[:, 1, :, 0:NS], src[:, :, NS:P])
                    dve.tensor_copy(m3[:, 1, :, NS:P], src[:, :, 0:NS]).then_inc(m3_back, 1)
                    if (q + 1) % 4:
                        pad(q + 1)
                    dve.wait_ge(w_done, q + 1)
                    four = lambda b: bank[b][:].rearrange("p (g c) -> p g c", g=4)
                    if q:
                        dve.wait_ge(swapped, q)
                    ch.step(tt(z[:], four(2), tr[:, 0, gl], ALU.mult))
                    ch.step(tt(zt[:], four(3), tr[:, 1, gl], ALU.mult))
                    ch.step(tt(zt[:], z[:], zt[:], ALU.add))
                    for g in range(4):
                        ins = dve.tensor_tensor_scan(z[:, g, :], mag[:, 1, 4 * q + g:4 * q + g + 1].broadcast_to([P, CHUNKS]),
                                                     zt[:, g, :], 0.0, ALU.mult, ALU.add)
                    ins.then_inc(z_done, 1)
                    dve.wait_ge(swapped, q + 1)
                    ch.step(tt(zt[:], four(4), tr[:, 1, gl], ALU.mult))
                    if q:
                        dve.wait_ge(y_done, q)
                    ch.step(tt(st[:, :, 1:CHUNKS + 1], z[:], tr[:, 0, gl], ALU.mult))
                    tt(st[:, :, 1:CHUNKS + 1], st[:, :, 1:CHUNKS + 1], zt[:], ALU.subtract).then_inc(s_done, 1)
                    dve.wait_ge(y_done, q + 1)
                    ch.step(tt(uT[:, gg, :], uT[:, gg, :], dcol[:, gg].unsqueeze(2).broadcast_to([P, 4, CHUNKS]), ALU.mult))
                    tt(uT[:, gg, :], uT[:, gg, :], four(5), ALU.add).then_inc(y_read, 1)
                for q in range(NQ + 1):
                    if q < NQ:
                        dve.wait_ge(glu_done, q + 1)
                        if q >= 2:
                            dve.wait_ge(gated_done, q - 1)
                        tt(gate[:, q % 2], bank[6 + q % 2][:].rearrange("p (g c) -> p g c", g=4),
                           bcol[:, 4 * q:4 * q + 4].unsqueeze(2).broadcast_to([P, 4, CHUNKS]), ALU.add).then_inc(biased, 1)
                    if q:
                        dve.wait_ge(sig_done, q)
                        part = uT[:, 4 * q - 4:4 * q, :]
                        tt(part, part, gate[:, (q - 1) % 2], ALU.mult).then_inc(gated_done, 1)
                for t in range(4):
                    dve.wait_ge(mix_turned, t + 1)
                    dve.tensor_copy(mixT[:, t, :].rearrange("p (c j) -> p j c", j=CH)[:, 4:8, :],
                                    bank[3][:].rearrange("p (j c) -> p j c", j=4)).then_inc(mix_v, 1)


NORMED = HEADS * HD + HD
AT_V, AT_QI, AT_KI, AT_WI = NORMED, NORMED + HD, NORMED + HD + HEADS * HD, NORMED + 2 * HD + HEADS * HD


def project_rest(k, hT, qT, kT, v_rows, w_rows):
    nc, ap = k.nc, k.ap
    widths = (512, 512, QKV - 1024)
    with ExitStack() as ctx:
        w = k.sb("p_w", [P, KS, QKV], ctx=ctx)
        gains = k.sb("p_gains", [P, NORMED], ctx=ctx)
        line = [k.sb(f"p_line{i}", [P, REST], ctx=ctx) for i in range(2)]
        square = k.sb("p_square", [P, NORMED], ctx=ctx)
        stat = k.sb("p_stat", [P, 3, HEADS + 1], ctx=ctx)
        turn = k.sb("p_turn", [P, 4, 2, HEADS + 1, ROPE], ctx=ctx)
        ps = [k.ps(f"p_ps{i}", [P, 512], ctx=ctx) for i in range(3)]
        ps_t = [k.ps(f"p_ps_t{i}", [P, 512], ctx=ctx) for i in range(3)]
        w_in = [k.sem(f"p_w_in{i}") for i in range(4)]
        gains_in, done, line_a, line_v = (k.sem(f"p_{n}") for n in ("gains_in", "done", "line_a", "line_v"))
        squared, mean_done, root_done, line_done = (k.sem(f"p_{n}") for n in ("squared", "mean", "root", "line_done"))
        turned, back_a, back_v, chain = (k.sem(f"p_{n}") for n in ("turned", "back_a", "back_v", "chain"))
        with nc.Block() as block:

            @block.sync
            def _(sp):
                columns = ap["hyb_w_in"][0][:, 512:512 + QKV].rearrange("(p s) n -> p s n", s=KS)
                for q in range(4):
                    sp.dma_start(w[:, 2 * q:2 * q + 2], columns[:, 2 * q:2 * q + 2]).then_inc(w_in[q], 16)
                for h in range(HEADS):
                    sp.dma_start(gains[:, h * HD:(h + 1) * HD], spread(ap["attn_q_norm_g"][0])).then_inc(gains_in, 16)
                sp.dma_start(gains[:, HEADS * HD:], spread(ap["attn_k_norm_g"][0])).then_inc(gains_in, 16)

            @block.tensor
            def _(pe):
                def turn_line(i):
                    pe.wait_ge(line_done, i + 1)
                    if i:
                        pe.wait_ge(back_a, i)
                        pe.wait_ge(back_v, i)
                    src = line[i % 2]
                    for b in range(2):
                        for j in range(4):
                            pe.transpose(ps_t[b][:, j * P:(j + 1) * P], src[:, b * 640 + j * P:b * 640 + (j + 1) * P],
                                         k.c("ident"))
                        mm = pe.transpose(ps_t[2][:, b * P:(b + 1) * P], src[:, b * 640 + 512:b * 640 + 640], k.c("ident"))
                    mm.then_inc(turned, 1)

                for i in range(TILES):
                    if i:
                        pe.wait_ge(line_a, i)
                        pe.wait_ge(line_v, i)
                    for s in range(KS):
                        if i == 0 and s % 2 == 0:
                            pe.wait_ge(w_in[s // 2], 16)
                        for n, width in enumerate(widths):
                            mm = pe.matmul(ps[n][:, 0:width], hT[:, s, i * P:(i + 1) * P],
                                           w[:, s, 512 * n:512 * n + width], start=(s == 0), stop=(s == KS - 1))
                    mm.then_inc(done, 1)
                    if i:
                        turn_line(i - 1)
                turn_line(TILES - 1)

            @block.scalar
            def _(act):
                def back(i):
                    act.wait_ge(turned, i + 1)
                    act.copy(qT[:, 0, :, i * P:(i + 1) * P], ps_t[0][:].rearrange("p (j t) -> p j t", j=4))
                    act.copy(kT[:, :, i * P:(i + 1) * P], ps_t[2][:, 0:2 * P].rearrange("p (j t) -> p j t", j=2)
                             ).then_inc(back_a, 1)

                for i in range(TILES):
                    act.wait_ge(done, i + 1)
                    if i >= 2:
                        act.wait_ge(turned, i - 1)
                    act.copy(line[i % 2][:, 0:512], ps[0][:])
                    act.copy(line[i % 2][:, 512:1024], ps[1][:]).then_inc(line_a, 1)
                    act.wait_ge(line_a, i + 1)
                    if i:
                        act.wait_ge(mean_done, i)
                    act.activation(square[:], line[i % 2][:, 0:NORMED], ACT.Square).then_inc(squared, 1)
                    act.wait_ge(mean_done, i + 1)
                    act.activation(stat[:, 2, :], stat[:, 1, :], ACT.Sqrt).then_inc(root_done, 1)
                    if i:
                        back(i - 1)
                back(TILES - 1)

            @block.vector
            def _(dve):
                ch = Chain(dve, chain)
                tt = dve.tensor_tensor

                def back(i):
                    dve.wait_ge(turned, i + 1)
                    dve.tensor_copy(qT[:, 1, :, i * P:(i + 1) * P], ps_t[1][:].rearrange("p (j t) -> p j t", j=4)
                                    ).then_inc(back_v, 1)

                dve.wait_ge(gains_in, 16 * (HEADS + 1))
                for i in range(TILES):
                    src = line[i % 2]
                    dve.wait_ge(done, i + 1)
                    if i >= 2:
                        dve.wait_ge(turned, i - 1)
                    dve.tensor_copy(src[:, 1024:QKV], ps[2][:, 0:QKV - 1024]).then_inc(line_v, 1)
                    dve.wait_ge(line_v, i + 1)
                    dve.wait_ge(line_a, i + 1)
                    ch.step(dve.tensor_copy(v_rows[:, i, :], src[:, AT_V:AT_V + HD]))
                    ch.step(dve.tensor_scalar(w_rows[:, i, :], src[:, AT_WI:AT_WI + HEADS], float(HEADS) ** -0.5, None,
                                              ALU.mult))
                    dve.wait_ge(squared, i + 1)
                    if i:
                        dve.wait_ge(root_done, i)
                    ch.step(dve.tensor_reduce(stat[:, 0, :], square[:].rearrange("p (h n) -> p h n", n=HD), AX, ALU.add))
                    dve.tensor_scalar(stat[:, 1, :], stat[:, 0, :], 1.0 / HD, EPS, ALU.mult, ALU.add).then_inc(mean_done, 1)
                    dve.wait_ge(root_done, i + 1)
                    ch.step(dve.reciprocal(stat[:, 0, :], stat[:, 2, :]))
                    heads = src[:, 0:NORMED].rearrange("p (h n) -> p h n", n=HD)
                    ch.step(tt(heads, heads, stat[:, 0, :].unsqueeze(2).broadcast_to([P, HEADS + 1, HD]), ALU.mult))
                    ch.step(tt(src[:, 0:NORMED], src[:, 0:NORMED], gains[:], ALU.mult))
                    rot = src[:].rearrange("p (b h n) -> p b h n", b=2, n=HD)[:, :, 0:HEADS + 1, :]
                    wave = lambda a: k.cos_sin[:, a, i, :].unsqueeze(1).unsqueeze(1).broadcast_to([P, 2, HEADS + 1, ROPE])
                    x1, x2 = rot[:, :, :, 0:ROPE], rot[:, :, :, ROPE:2 * ROPE]
                    tt(turn[:, 0], x1, wave(0), ALU.mult)
                    tt(turn[:, 1], x2, wave(1), ALU.mult)
                    tt(turn[:, 2], x1, wave(1), ALU.mult)
                    ch.step(tt(turn[:, 3], x2, wave(0), ALU.mult))
                    tt(x1, turn[:, 0], turn[:, 1], ALU.subtract)
                    ch.step(tt(x2, turn[:, 2], turn[:, 3], ALU.add))
                    dve.tensor_copy(src[:, AT_V:AT_V + HD], src[:, AT_V - HD:AT_V])
                    dve.tensor_copy(src[:, AT_WI:AT_WI + HD], src[:, AT_KI:AT_KI + HD]).then_inc(line_done, 1)
                    if i:
                        back(i - 1)
                back(TILES - 1)


def attention(k, qT, kT, v_rows, w_rows, mixT, w_ring):
    nc = k.nc
    FREE_TILES = TOPK // P
    jobs = []
    for i in range(TILES):
        for h in range(HEADS):
            jobs.append((i, h, False))
            if FREE_TILES <= i + 2 < TILES:
                jobs.append((i + 2, h, True))
    index_of = {j: n for n, j in enumerate([j for j in jobs if j[2]])}
    att_of = {j: n for n, j in enumerate([j for j in jobs if not j[2]])}
    with ExitStack() as ctx:
        relu = [k.sb(f"a_relu{i}", [P, SEQ], ctx=ctx) for i in range(2)]
        total = [k.sb(f"a_total{i}", [P, SEQ], ctx=ctx) for i in range(2)]
        work = k.sb("a_work", [P, SEQ], ctx=ctx)
        top8 = k.sb("a_top8", [P, 8], ctx=ctx)
        bias = k.sb("a_bias", [P, SEQ], ctx=ctx)
        score = [k.sb(f"a_score{i}", [P, SEQ], ctx=ctx) for i in range(2)]
        prob = [k.sb(f"a_prob{i}", [P, SEQ], ctx=ctx) for i in range(2)]
        probT = [k.sb(f"a_probT{i}", [P, SEQ], ctx=ctx) for i in range(2)]
        stat = k.sb("a_stat", [P, 3, 2], ctx=ctx)
        out = k.sb("a_out", [P, HEADS * HD], ctx=ctx)
        ps_s = [k.ps(f"a_ps_s{i}", [P, 1024], ctx=ctx) for i in range(2)]
        ps_t = k.ps("a_ps_t", [P, 1024], ctx=ctx)
        ps_o = [k.ps(f"a_ps_o{i}", [P, 512], ctx=ctx) for i in range(2)]
        ps_m = ps_o[1]
        index_done, att_done, relu_done, added = (k.sem(f"a_{n}") for n in ("index_done", "att_done", "relu_done", "added"))
        scored, exp_done, turned, back = (k.sem(f"a_{n}") for n in ("scored", "exp", "turned", "back"))
        inv_done, pv_done, out_done, out_turned, mixed = (k.sem(f"a_{n}") for n in
                                                         ("inv", "pv", "out", "out_turned", "mixed"))
        chain = k.sem("a_chain")
        mod_acc = k.sb("a_mod_acc", [P, 3, 3 * D], ctx=ctx)
        fold_after = [(4, 3, False), (5, 3, False), (6, 3, False)]
        w_in, w_used = [k.sem(f"a_w_in{i}") for i in range(2)], k.sem("a_w_used")
        w_scaled, folded, raw_copied, raw_out = (k.sem(f"a_{n}") for n in ("w_scaled", "folded", "raw_copied", "raw_out"))
        with nc.Block() as block:

            @block.sync
            def _(sp):
                for n in range(3 * KS):
                    if n >= 2:
                        sp.wait_ge(w_used, n - 1)
                    sp.dma_start(w_ring[:, n % 2, :], mod_weights(k.ap, 1 + n // KS)[n % KS]).then_inc(w_in[n % 2], 16)
                for m in range(3):
                    sp.wait_ge(raw_copied, 6 * (m + 1))
                    sp.dma_start(k.mod_raw[m].unsqueeze(0), mod_acc[0:1, m, :]).then_inc(raw_out, 16)
                sp.wait_ge(raw_out, 3 * 16)

            @block.gpsimd
            def _(pool):
                for n in range(3 * KS):
                    acc, w = mod_acc[:, n // KS, :], w_ring[:, n % 2, :]
                    s = n % KS
                    pool.wait_ge(w_in[n % 2], 16 * (n // 2 + 1))
                    pool.tensor_scalar(w if s else acc, w, k.c_silu[:, s:s + 1], None, ALU.mult).then_inc(w_scaled, 1)
                    pool.wait_ge(w_scaled, n + 1)
                    if s:
                        pool.tensor_tensor(acc, acc, w, ALU.add).then_inc(w_used, 1)
                    else:
                        pool.sem_inc(w_used, 1)
                    pool.wait_ge(w_used, n + 1)

            @block.tensor
            def _(pe):
                def scores(n):
                    i, h, indexer = jobs[n]
                    nk = P * (i + 1)
                    if n >= 2:
                        last = jobs[n - 2]
                        if last[2]:
                            pe.wait_ge(relu_done, index_of[last] + 1)
                        else:
                            pe.wait_ge(scored, att_of[last] + 1)
                    half = slice((h % 2) * HD, (h % 2) * HD + HD)
                    which = 1 if indexer else 0
                    for lo in range(0, nk, 512):
                        hi = min(nk, lo + 512)
                        mm = pe.matmul(ps_s[n % 2][:, lo:hi], qT[half, which, h // 2, i * P:(i + 1) * P],
                                       kT[half, which, lo:hi], start=True, stop=True)
                    mm.then_inc(index_done if indexer else att_done, 1)

                def values(n):
                    a = att_of[jobs[n]]
                    i, h, _ = jobs[n]
                    pe.wait_ge(exp_done, a + 1)
                    if a:
                        pe.wait_ge(back, a)
                    for j in range(i + 1):
                        mm = pe.transpose(ps_t[:, j * P:(j + 1) * P], prob[a % 2][:, j * P:(j + 1) * P], k.c("ident"))
                    mm.then_inc(turned, 1)
                    pe.wait_ge(back, a + 1)
                    if a >= 2:
                        pe.wait_ge(out_done, a - 1)
                    if h == 1 and i:
                        pe.wait_ge(mixed, i)
                    for j in range(i + 1):
                        mm = pe.matmul(ps_o[a % 2][:, 0:HD], probT[a % 2][:, j * P:(j + 1) * P],
                                       v_rows[:, j, :], start=(j == 0), stop=(j == i))
                    mm.then_inc(pv_done, 1)
                    if h == HEADS - 1:
                        pe.wait_ge(out_done, a + 1)
                        for j in range(4):
                            mm = pe.transpose(ps_m[:, j * P:(j + 1) * P], out[:, j * P:(j + 1) * P], k.c("ident"))
                        mm.then_inc(out_turned, 1)

                def fold(m):
                    pe.wait_ge(w_used, (m + 1) * KS)
                    pe.wait_ge(back, att_of[fold_after[m]] + 1)
                    for n in range(6):
                        if n >= 2:
                            pe.wait_ge(raw_copied, 6 * m + n - 1)
                        pe.matmul(ps_t[0:1, n % 2 * 512:n % 2 * 512 + 512], k.ones[:],
                                  mod_acc[:, m, n * 512:n * 512 + 512], start=True, stop=True).then_inc(folded, 1)

                scores(0)
                for n in range(len(jobs)):
                    if n + 1 < len(jobs):
                        scores(n + 1)
                    if not jobs[n][2]:
                        values(n)
                    if jobs[n] in fold_after:
                        fold(fold_after.index(jobs[n]))

            @block.scalar
            def _(act):
                for n, job in enumerate(jobs):
                    i, h, indexer = job
                    nk = P * (i + 1)
                    if indexer:
                        a = index_of[job]
                        act.wait_ge(index_done, a + 1)
                        if a >= 2:
                            act.wait_ge(added, a - 1)
                        act.activation(relu[a % 2][:, 0:nk], ps_s[n % 2][:, 0:nk], ACT.Relu, scale=float(HD) ** -0.5
                                       ).then_inc(relu_done, 1)
                        continue
                    a = att_of[job]
                    act.wait_ge(scored, a + 1)
                    if a >= 2:
                        act.wait_ge(turned, a - 1)
                    act.activation(prob[a % 2][:, 0:nk], score[a % 2][:, 0:nk], ACT.Exp, bias=stat[:, 0, a % 2:a % 2 + 1],
                                   scale=-1.0, accum_out=stat[:, 1, a % 2:a % 2 + 1]).then_inc(exp_done, 1)
                    act.wait_ge(turned, a + 1)
                    if a >= 2:
                        act.wait_ge(pv_done, a - 1)
                    act.copy(probT[a % 2][:, 0:nk], ps_t[:, 0:nk]).then_inc(back, 1)
                    if job in fold_after:
                        m = fold_after.index(job)
                        for piece in range(6):
                            act.wait_ge(folded, 6 * m + piece + 1)
                            act.copy(mod_acc[0:1, m, piece * 512:piece * 512 + 512],
                                     ps_t[0:1, piece % 2 * 512:piece % 2 * 512 + 512]).then_inc(raw_copied, 1)

            @block.vector
            def _(dve):
                ch = Chain(dve, chain)

                def finish(a):
                    i, h = a // HEADS, a % HEADS
                    dve.wait_ge(exp_done, a + 1)
                    dve.reciprocal(stat[:, 2, a % 2:a % 2 + 1], stat[:, 1, a % 2:a % 2 + 1]).then_inc(inv_done, 1)
                    dve.wait_ge(inv_done, a + 1)
                    dve.wait_ge(pv_done, a + 1)
                    if h == 0 and i:
                        dve.wait_ge(out_turned, i)
                    dve.tensor_scalar(out[:, h * HD:(h + 1) * HD], ps_o[a % 2][:, 0:HD],
                                      stat[:, 2, a % 2:a % 2 + 1], None, ALU.mult).then_inc(out_done, 1)
                    if h == HEADS - 1:
                        dve.wait_ge(out_turned, i + 1)
                        dve.tensor_copy(mixT[:, :, i * P:(i + 1) * P], ps_m[:].rearrange("p (j t) -> p j t", j=4)
                                        ).then_inc(mixed, 1)

                def weigh(i, h):
                    nk = P * (i + 1)
                    a = index_of[(i, h, True)]
                    dve.wait_ge(relu_done, a + 1)
                    w, t = w_rows[:, i, h:h + 1], total[i % 2][:, 0:nk]
                    if h == 0:
                        ins = dve.tensor_scalar(t, relu[a % 2][:, 0:nk], w, None, ALU.mult)
                    else:
                        ins = dve.scalar_tensor_tensor(t, relu[a % 2][:, 0:nk], w, t, ALU.mult, ALU.add)
                    ins.then_inc(added, 1)
                    dve.wait_ge(added, a + 1)

                def search(i, r):
                    nk = P * (i + 1)
                    t = total[i % 2]
                    if r == 0:
                        ch.step(dve.tensor_tensor(t[:, i * P:nk], t[:, i * P:nk], k.c("causal"), ALU.add))
                    src = work if r else t
                    ch.step(dve.max(top8[:], src[:, 0:nk]))
                    ch.step(dve.match_replace(work[:, 0:nk], top8[:], src[:, 0:nk], -3e38))

                def set_bias(i):
                    nk = P * (i + 1)
                    if i < FREE_TILES:
                        if i:
                            ch.step(dve.memset(bias[:, 0:i * P], 0.0))
                        ch.step(dve.tensor_scalar(bias[:, i * P:nk], k.c("causal"), 8.0, None, ALU.mult))
                    else:
                        ch.step(dve.tensor_scalar(bias[:, 0:nk], work[:, 0:nk], -2e38, 8.0 * NEG, ALU.is_gt, ALU.mult))

                ROUNDS = TOPK // 8 // HEADS
                set_bias(0)
                for i in range(TILES):
                    nk = P * (i + 1)
                    for h in range(HEADS):
                        a = att_of[(i, h, False)]
                        n = jobs.index((i, h, False))
                        dve.wait_ge(att_done, a + 1)
                        if a >= 2:
                            dve.wait_ge(exp_done, a - 1)
                        dve.tensor_tensor_reduce(score[a % 2][:, 0:nk], ps_s[n % 2][:, 0:nk], bias[:, 0:nk],
                                                 -float(HD) ** -0.5, 3e38, ALU.add, ALU.min, stat[:, 0, a % 2:a % 2 + 1]
                                                 ).then_inc(scored, 1)
                        if h:
                            finish(a - 1)
                        if FREE_TILES <= i + 1 < TILES:
                            for r in range(ROUNDS * h, ROUNDS * (h + 1)):
                                search(i + 1, r)
                        if FREE_TILES <= i + 2 < TILES:
                            weigh(i + 2, h)
                    if i + 1 < TILES:
                        set_bias(i + 1)
                    finish(a)


def hybrid_out(k, mix_ssm, mix_att):
    nc, ap = k.nc, k.ap
    with ExitStack() as ctx:
        w = k.sb("o_w", [P, KS, D], ctx=ctx)
        gate = k.sb("o_gate", [P, D], ctx=ctx)
        part = k.sb("o_part", [P, 2, D], ctx=ctx)
        scratch, squared = k.sb("o_scratch", [P, D], ctx=ctx), k.sem("o_squared")
        raw = k.sb("o_raw", [P, 3, 3, 8], ctx=ctx)
        bias = k.sb("o_bias", [P, 3, 3, 8], ctx=ctx)
        gain = k.sb("o_gain", [P, 3, 8], ctx=ctx)
        ps = [k.ps(f"o_ps{i}", [P, 1024], ctx=ctx) for i in range(2)]
        w_in = [k.sem(f"o_w_in{i}") for i in range(4)]
        gate_in, done, gated_done, x_done = (k.sem(f"o_{n}") for n in ("gate_in", "done", "gated", "x_done"))
        small_in, x_in, rows_done, rows_out, chain = (k.sem(f"o_{n}") for n in
                                                      ("small_in", "x_in", "rows_done", "rows_out", "chain"))
        with nc.Block() as block:

            @block.sync
            def _(sp):
                rows = ap["hyb_w_out"][0].rearrange("(s p) n -> p s n", p=P)
                for q in range(4):
                    sp.dma_start(w[:, 2 * q:2 * q + 2], rows[:, 2 * q:2 * q + 2]).then_inc(w_in[q], 16)
                with nc.allow_non_contiguous_dma(reason="modulation rows, eight columns a partition"):
                    for m in range(3):
                        which, layer = MOD_SOURCES[m + 1]
                        sp.dma_start(raw[:, m], k.mod_raw[m].rearrange("(j p c) -> p j c", j=3, c=8)).then_inc(small_in, 16)
                        sp.dma_start(bias[:, m], ap[which + "_mod_b"][layer].rearrange("(j p c) -> p j c", j=3, c=8)
                                     ).then_inc(small_in, 16)
                        sp.dma_start(gain[:, m], ap[which + "_norm_g"][layer].rearrange("(p c) -> p c", c=8)
                                     ).then_inc(small_in, 16)
                sp.dma_start(gate[:], spread(k.mod[0, 2])).then_inc(gate_in, 16)
                sp.dma_start(k.x[:], ap["x"][0].rearrange("(i p) d -> p i d", p=P)).then_inc(x_in, 16)
                sp.wait_ge(rows_done, 1)
                with nc.allow_non_contiguous_dma(reason="modulation rows, eight columns a partition"):
                    for src, dst in ((1, 0), (0, 1), (2, 2)):
                        for m in range(3):
                            sp.dma_start(k.mod[m + 1, dst].rearrange("(p c) -> p c", c=8), raw[:, m, src, :]
                                         ).then_inc(rows_out, 16)
                sp.wait_ge(rows_out, 9 * 16)

            @block.tensor
            def _(pe):
                for i in range(TILES):
                    if i >= 2:
                        pe.wait_ge(gated_done, i - 1)
                    for s in range(KS):
                        if i == 0 and s % 2 == 0:
                            pe.wait_ge(w_in[s // 2], 16)
                        for n in range(2):
                            mix = mix_ssm if s < 4 else mix_att
                            mm = pe.matmul(ps[i % 2][:, n * 512:(n + 1) * 512], mix[:, s % 4, i * P:(i + 1) * P],
                                           w[:, s, n * 512:(n + 1) * 512], start=(s == 0), stop=(s == KS - 1))
                    mm.then_inc(done, 1)

            @block.scalar
            def _(act):
                k.sum_squares(act, scratch[:], x_done, squared)

            @block.vector
            def _(dve):
                ch = Chain(dve, chain)
                dve.wait_ge(small_in, 9 * 16)
                ch.step(dve.tensor_tensor(raw[:], raw[:], bias[:], ALU.add))
                dve.scalar_tensor_tensor(raw[:, :, 1, :], raw[:, :, 1, :], 1.0, gain[:], ALU.add, ALU.mult
                                         ).then_inc(rows_done, 1)
                dve.wait_ge(gate_in, 16)
                dve.wait_ge(x_in, 16)
                for i in range(TILES):
                    dve.wait_ge(done, i + 1)
                    dve.tensor_tensor(part[:, i % 2], ps[i % 2][:], gate[:], ALU.mult).then_inc(gated_done, 1)
                    dve.wait_ge(gated_done, i + 1)
                    dve.tensor_tensor(k.x[:, i, :], k.x[:, i, :], part[:, i % 2], ALU.add).then_inc(x_done, 1)


class PoolWeights:

    def __init__(self, k, ctx):
        NW = len(WINDOWS)
        self.k = k
        self.band = k.sb("l_band", [P, NW, 3, P], ctx=ctx)
        self.w = k.sb("l_w", [P, NW, 2, PG], ctx=ctx)
        self.gate = k.sb("l_gate", [P, D], ctx=ctx)
        self.scale = k.sb("l_scale", [P, D], ctx=ctx)
        self.loaded = k.sem("l_loaded")

    def load(self, sp):
        ap = self.k.ap
        sp.dma_start(self.band[:].rearrange("p a b c -> p (a b c)"), ap["band"]).then_inc(self.loaded, 16)
        sp.dma_start(self.w[:].rearrange("p g c n -> p (g c) n"),
                     ap["pool_w"][0].rearrange("g (c p) n -> p (g c) n", p=P)).then_inc(self.loaded, 16)
        sp.dma_start(self.gate[:], spread(self.k.mod[2, 2])).then_inc(self.loaded, 16)
        sp.dma_start(self.scale[:], spread(ap["pool_scale"][0])).then_inc(self.loaded, 16)


def pool_mixer(k, h, weights):
    nc = k.nc
    NW = len(WINDOWS)
    band, w, gate, scale, loaded = weights.band, weights.w, weights.gate, weights.scale, weights.loaded
    with ExitStack() as ctx:
        pooled = [k.sb(f"l_pooled{i}", [P, KS, P], ctx=ctx) for i in range(2)]
        part = k.sb("l_part", [P, 2, D], ctx=ctx)
        scratch, squared = k.sb("l_scratch", [P, D], ctx=ctx), k.sem("l_squared")
        ps_p = [k.ps(f"l_ps_p{i}", [P, 512], ctx=ctx) for i in range(2)]
        ps_y = [k.ps(f"l_ps_y{i}", [P, 1024], ctx=ctx) for i in range(2)]
        scaled, pool_done, pool_a, pool_v = (k.sem(f"l_{n}") for n in ("scaled", "pool_done", "pool_a", "pool_v"))
        done, gated_done, x_done = (k.sem(f"l_{n}") for n in ("done", "gated", "x_done"))
        with nc.Block() as block:

            @block.tensor
            def _(pe):
                pe.wait_ge(loaded, 64)

                def pool(i):
                    if i:
                        pe.wait_ge(pool_a, i)
                        pe.wait_ge(pool_v, i)
                    for s in range(KS):
                        out = ps_p[s // 4][:, (s % 4) * P:(s % 4 + 1) * P]
                        cols = slice(s * P, (s + 1) * P)
                        mm = pe.matmul(out, h[:, i, cols], band[:, s // 2, 1 if i else 0, :], start=True, stop=(i == 0))
                        if i:
                            mm = pe.matmul(out, h[:, i - 1, cols], band[:, s // 2, 2, :], start=False, stop=True)
                    mm.then_inc(pool_done, 1)

                pool(0)
                for i in range(TILES):
                    pe.wait_ge(pool_a, i + 1)
                    pe.wait_ge(pool_v, i + 1)
                    if i + 1 < TILES:
                        pool(i + 1)
                    if i >= 2:
                        pe.wait_ge(gated_done, i - 1)
                    for g in range(NW):
                        for c in range(2):
                            mm = pe.matmul(ps_y[i % 2][:, g * PG:(g + 1) * PG], pooled[i % 2][:, 2 * g + c, :], w[:, g, c, :],
                                           start=(c == 0), stop=(c == 1))
                    mm.then_inc(done, 1)

            @block.scalar
            def _(act):
                def squares_of(i):
                    act.wait_ge(x_done, i + 1)
                    if i:
                        act.wait_ge(squared, i)
                    act.activation(scratch[:], k.x[:, i, :], ACT.Square, accum_out=k.squares[:, i:i + 1]
                                   ).then_inc(squared, 1)

                for i in range(TILES):
                    act.wait_ge(pool_done, i + 1)
                    if i >= 2:
                        act.wait_ge(done, i - 1)
                    act.copy(pooled[i % 2][:, 0:4, :], ps_p[0][:].rearrange("p (s t) -> p s t", s=4)).then_inc(pool_a, 1)
                    if i:
                        squares_of(i - 1)
                squares_of(TILES - 1)

            @block.vector
            def _(dve):
                dve.wait_ge(loaded, 64)
                dve.tensor_tensor(gate[:], gate[:], scale[:], ALU.mult).then_inc(scaled, 1)
                dve.wait_ge(scaled, 1)

                def pool_back(i):
                    dve.wait_ge(pool_done, i + 1)
                    if i >= 2:
                        dve.wait_ge(done, i - 1)
                    dve.tensor_copy(pooled[i % 2][:, 4:8, :], ps_p[1][:].rearrange("p (s t) -> p s t", s=4)
                                    ).then_inc(pool_v, 1)

                pool_back(0)
                for i in range(TILES):
                    if i + 1 < TILES:
                        pool_back(i + 1)
                    dve.wait_ge(done, i + 1)
                    dve.tensor_tensor(part[:, i % 2], ps_y[i % 2][:], gate[:], ALU.mult).then_inc(gated_done, 1)
                    dve.wait_ge(gated_done, i + 1)
                    dve.tensor_tensor(k.x[:, i, :], k.x[:, i, :], part[:, i % 2], ALU.add).then_inc(x_done, 1)


def hybrid_layer(k, ctx):
    uT = k.sb("uT", [P, GROUPS, CHUNKS], ctx=ctx)
    mix_ssm = k.sb("mix_ssm", [P, 4, SEQ], ctx=ctx)
    mix_att = uT[:].rearrange("p g c -> p (g c)").rearrange("p (s t) -> p s t", s=4)
    with ExitStack() as inner:
        hT = k.sb("hT", [P, KS, SEQ], ctx=inner)
        u_ctx = inner.enter_context(ExitStack())
        u_w = k.sb("u_w", [P, KS, GROUPS * GH], ctx=u_ctx)
        u_w_in = k.sem("u_w_in")

        def load_u(sp):
            sp.dma_start(u_w[:], k.ap["hyb_w_in"][0][:, 0:GROUPS * GH].rearrange("(p s) n -> p s n", s=KS)
                         ).then_inc(u_w_in, 16)

        with ExitStack() as first:
            k.hold_x(first, "x_first")
            load_and_modulate(k)
            normalise(k, 0, None, "n0", True, hT=hT, extra=load_u)
        with ExitStack() as heads:
            rotor, lam, mag = (k.sb(n, [P, 2, GROUPS], ctx=heads) for n in ("rotor", "lam", "mag"))
            dt = k.sb("dt", [P, GROUPS], ctx=heads)
            sine_tables(k, k.cos_sin, rotor, lam, dt, mag)
            u_rows = k.sb("u_rows", [P, GROUPS, CH, GH], ctx=heads)
            s5(k, hT, u_w, u_w_in, uT, u_rows[:], mix_ssm, rotor, lam, mag)
        u_ctx.close()
        v_rows = k.sb("v_rows", [P, TILES, HD], ctx=inner)
        w_rows = k.sb("w_rows", [P, TILES, HEADS], ctx=inner)
        qT = k.sb("qT", [P, 2, 4, SEQ], ctx=inner)
        kT = k.sb("kT", [P, 2, SEQ], ctx=inner)
        project_rest(k, hT, qT, kT, v_rows, w_rows)
        w_ring = hT[:].rearrange("p s t -> p (s t)")[:, 0:6 * D].rearrange("p (r n) -> p r n", r=2)
        attention(k, qT, kT, v_rows, w_rows, mix_att, w_ring)
    k.hold_x(ctx, "x0")
    hybrid_out(k, mix_ssm, mix_att)


def program(nc, ap, out):
    with ExitStack() as ctx:
        k = Core(nc, ctx, ap)
        with ExitStack() as part:
            routes = Routes(k, part, "m0")
            with ExitStack() as inner:
                hybrid_layer(k, inner)
                k.recycle()
                moe_front(k, 0, 1, "m0", routes)
            experts(k, 0, routes, "m0_e")
        k.recycle()
        with ExitStack() as part:
            routes = Routes(k, part, "m1")
            with ExitStack() as inner:
                k.hold_x(inner, "x1")
                moe_residual(k, 0, 1, "m0_x")
                with ExitStack() as mixer:
                    h = k.sb("h1", [P, TILES, D], ctx=mixer)
                    weights = PoolWeights(k, mixer)
                    normalise(k, 2, h, "n1", False, extra=weights.load)
                    pool_mixer(k, h, weights)
                moe_front(k, 1, 3, "m1", routes)
            k.recycle()
            experts(k, 1, routes, "m1_e")
        with ExitStack() as part:
            k.hold_x(part, "x2")
            moe_residual(k, 1, 3, "m1_x", out=out[0])


_INS = ["x", "c", "positions", "mix_norm_g", "mix_mod_w", "mix_mod_b", "ffn_norm_g", "ffn_mod_w", "ffn_mod_b",
        "hyb_w_in", "hyb_w_out", "s5_lambda_re", "s5_lambda_im", "s5_log_dt", "s5_b_re", "s5_b_im", "s5_c_re",
        "s5_c_im", "s5_d", "s5_glu_w", "s5_glu_b", "attn_q_norm_g", "attn_k_norm_g", "pool_w", "pool_scale",
        "router_w", "router_bias", "exp_w_gate", "exp_w_up", "exp_w_down", "sh_w_gate", "sh_w_up", "sh_w_down"]


def kernel(**inputs):
    import concourse.bacc as bacc
    from concourse.bass_utils import run_bass_kernel_spmd

    nc = bacc.Bacc("TRN2", target_bir_lowering=False, num_devices=1)
    arrays, ap = {}, {}
    given = {n: np.ascontiguousarray(inputs[n]) for n in _INS}
    for name, a in {**given, "const": CONST, "band": BAND}.items():
        arrays[f"in_{name}"] = a
        ap[name] = nc.dram_tensor(f"in_{name}", a.shape, mybir.dt.from_np(a.dtype), kind="ExternalInput").ap()
    out = nc.dram_tensor("out_x", (1, SEQ, D), F32, kind="ExternalOutput").ap()
    program(nc, ap, out)
    r = run_bass_kernel_spmd(nc, [arrays], core_ids=[0])
    return r.results[0]["out_x"]
```
